# Optimizing a Trainium2 kernel written in Bass

```python
import math
import numpy as np
import jax, jax.numpy as jnp
from jax import lax

D_MODEL = 1024
BATCH = 1
SEQ = 1024
DEPTH = 1
DEC_BATCH = 8
DEC_SEQ = 8
PAST_LEN = 2048
PAGE_SIZE = 128

D_MIX = D_MODEL
N_HEADS_ATT = 8
HEAD_DIM_ATT = (D_MIX // 2) // N_HEADS_ATT
ATT_W = N_HEADS_ATT * HEAD_DIM_ATT
N_IDX_HEADS = 4
IDX_DIM = 64
TOP_K_MAX = 256
Q_BLOCK = 128
N_HEADS_GDN = 4
HEAD_DIM_K = 128
HEAD_DIM_V = (D_MIX - ATT_W) // N_HEADS_GDN
GDN_K = N_HEADS_GDN * HEAD_DIM_K
GDN_V = N_HEADS_GDN * HEAD_DIM_V
CONV_W = 4
CONV_CH = 2 * GDN_K + GDN_V
CHUNK = 64
D_FF = 4 * D_MODEL
EPS = 1e-6
SPLIT_SIZES = (ATT_W, ATT_W, ATT_W, N_IDX_HEADS * IDX_DIM, IDX_DIM, N_IDX_HEADS,
               CONV_CH, N_HEADS_GDN, N_HEADS_GDN, GDN_V)
N_IN = 3 * ATT_W + N_IDX_HEADS * IDX_DIM + IDX_DIM + N_IDX_HEADS + CONV_CH + 2 * N_HEADS_GDN + GDN_V

kernel_name = 'hybrid_dsa_gated_deltanet_step'

def rmsnorm(x, g):
    x32 = x.astype(jnp.float32)
    y = x32 * lax.rsqrt(jnp.mean(x32 * x32, axis=-1, keepdims=True) + EPS)
    return (y * g.astype(jnp.float32)).astype(x.dtype)

def l2norm(x):
    return x * lax.rsqrt(jnp.sum(x * x, axis=-1, keepdims=True) + EPS)

def dsa_block(q, qi, wi, q_pos, k_all, v_all, ki_all, key_pos, n_sel):
    f32 = jnp.float32
    logits = jnp.einsum('bqhd,bsd->bqhs', qi, ki_all, preferred_element_type=f32) * (IDX_DIM ** -0.5)
    score = jnp.einsum('bqhs,bqh->bqs', jax.nn.relu(logits), wi.astype(f32))
    causal = key_pos[None, :] <= q_pos[:, None]
    score = jnp.where(causal[None], score, -jnp.inf)
    _, sel = lax.top_k(score, n_sel)
    valid = jnp.take(key_pos, sel) <= q_pos[None, :, None]
    gather = jax.vmap(lambda a, i: a[i])
    kg = gather(k_all, sel)
    vg = gather(v_all, sel)
    s = jnp.einsum('bqhd,bqkhd->bhqk', q, kg, preferred_element_type=f32) * (HEAD_DIM_ATT ** -0.5)
    s = jnp.where(valid[:, None], s, -jnp.inf)
    p = jax.nn.softmax(s, axis=-1)
    o = jnp.einsum('bhqk,bqkhd->bqhd', p.astype(vg.dtype), vg, preferred_element_type=f32)
    return o.astype(q.dtype)

def gated_delta_rule(q, k, v, g, beta, s0, chunk):
    B, T, H, DK = q.shape
    DV = v.shape[-1]
    n = T // chunk

    def chunks(a):
        a = a.reshape(B, n, chunk, H, *a.shape[3:])
        return jnp.moveaxis(a, 3, 1)

    q, k, v, g, beta = (chunks(a) for a in (q, k, v, g, beta))
    gc = jnp.cumsum(g, axis=-1)
    idx = jnp.arange(chunk)
    incl = idx[:, None] >= idx[None, :]
    strict = idx[:, None] > idx[None, :]
    decay = jnp.exp(jnp.where(incl, gc[..., :, None] - gc[..., None, :], -jnp.inf))
    kb = k * beta[..., None]
    vb = v * beta[..., None]
    lower = jnp.where(strict, jnp.einsum('bhncd,bhnsd->bhncs', kb, k) * decay, 0.0)
    a_mat = lower + jnp.eye(chunk, dtype=lower.dtype)
    rhs = jnp.concatenate([vb, kb * jnp.exp(gc)[..., None]], axis=-1)
    sol = lax.linalg.triangular_solve(a_mat, rhs, left_side=True, lower=True, unit_diagonal=True)
    u, w = sol[..., :DV], sol[..., DV:]
    aqk = jnp.where(incl, jnp.einsum('bhncd,bhnsd->bhncs', q, k) * decay, 0.0)

    def step(S, xs):
        qc, kc, uc, wc, gcc, ac = xs
        v_new = uc - jnp.einsum('bhck,bhkv->bhcv', wc, S)
        o = (jnp.einsum('bhck,bhkv->bhcv', qc * jnp.exp(gcc)[..., None], S)
             + jnp.einsum('bhcs,bhsv->bhcv', ac, v_new))
        g_last = gcc[..., -1]
        S = (S * jnp.exp(g_last)[..., None, None]
             + jnp.einsum('bhck,bhcv->bhkv', kc * jnp.exp(g_last[..., None] - gcc)[..., None], v_new))
        return S, o

    xs = tuple(jnp.moveaxis(a, 2, 0) for a in (q, k, u, w, gc, aqk))
    s_final, o = lax.scan(step, s0, xs)
    o = jnp.transpose(o, (1, 0, 3, 2, 4)).reshape(B, T, H, DV)
    return o, s_final

def hybrid_layer(x, k_past, v_past, ki_past, ssm0, conv0,
                 norm_mix, w_in, conv_w, a_log, dt_bias, norm_gdn_out, w_out, norm_mlp, w_up, w_down):
    B, T, _ = x.shape
    P = k_past.shape[1]
    f32 = jnp.float32
    h = rmsnorm(x, norm_mix)
    proj = h @ w_in
    offs = [int(o) for o in np.cumsum(SPLIT_SIZES)[:-1]]
    qa, ka, va, qi, ki, wi, qkv, a_in, b_in, z = jnp.split(proj, offs, axis=-1)

    qa = qa.reshape(B, T, N_HEADS_ATT, HEAD_DIM_ATT)
    ka = ka.reshape(B, T, N_HEADS_ATT, HEAD_DIM_ATT)
    va = va.reshape(B, T, N_HEADS_ATT, HEAD_DIM_ATT)
    qi = qi.reshape(B, T, N_IDX_HEADS, IDX_DIM)
    wi = wi * (N_IDX_HEADS ** -0.5)
    k_all = jnp.concatenate([k_past, ka], axis=1)
    v_all = jnp.concatenate([v_past, va], axis=1)
    ki_all = jnp.concatenate([ki_past, ki], axis=1)
    L = P + T
    n_sel = min(TOP_K_MAX, L // 4)
    key_pos = jnp.arange(L, dtype=jnp.int32)
    q_pos = P + jnp.arange(T, dtype=jnp.int32)
    attend = lambda xs: dsa_block(xs[0], xs[1], xs[2], xs[3], k_all, v_all, ki_all, key_pos, n_sel)
    qb = Q_BLOCK if T % Q_BLOCK == 0 else T
    nb = T // qb
    if nb == 1:
        o_a = attend((qa, qi, wi, q_pos))
    else:
        blk = lambda a: jnp.moveaxis(a.reshape(B, nb, qb, *a.shape[2:]), 1, 0)
        o_a = lax.map(attend, (blk(qa), blk(qi), blk(wi), q_pos.reshape(nb, qb)))
        o_a = jnp.moveaxis(o_a, 0, 1).reshape(B, T, N_HEADS_ATT, HEAD_DIM_ATT)

    xc = jnp.concatenate([conv0, qkv], axis=1)
    conv = xc[:, 0:T] * conv_w[0]
    for j in range(1, CONV_W):
        conv = conv + xc[:, j:j + T] * conv_w[j]
    conv = jax.nn.silu(conv)
    conv_new = xc[:, T:]
    qg, kg, vg = jnp.split(conv.astype(f32), [GDN_K, 2 * GDN_K], axis=-1)
    qg = l2norm(qg.reshape(B, T, N_HEADS_GDN, HEAD_DIM_K)) * (HEAD_DIM_K ** -0.5)
    kg = l2norm(kg.reshape(B, T, N_HEADS_GDN, HEAD_DIM_K))
    vg = vg.reshape(B, T, N_HEADS_GDN, HEAD_DIM_V)
    g = -jnp.exp(a_log.astype(f32)) * jax.nn.softplus(a_in.astype(f32) + dt_bias.astype(f32))
    beta = jax.nn.sigmoid(b_in.astype(f32))
    chunk = CHUNK if T % CHUNK == 0 else T
    o_b, ssm_new = gated_delta_rule(qg, kg, vg, g, beta, ssm0.astype(f32), chunk)
    zz = z.reshape(B, T, N_HEADS_GDN, HEAD_DIM_V).astype(f32)
    o_b = rmsnorm(o_b, norm_gdn_out) * jax.nn.silu(zz)

    mix = jnp.concatenate([o_a.reshape(B, T, ATT_W), o_b.reshape(B, T, GDN_V).astype(x.dtype)], axis=-1)
    x = x + mix @ w_out
    hm = rmsnorm(x, norm_mlp)
    x = x + jnp.square(jax.nn.relu(hm @ w_up)) @ w_down
    return x, ka, va, ki, ssm_new.astype(ssm0.dtype), conv_new

def setup_inputs(seed: int = 0) -> dict:
    key = jax.random.key(seed)
    ks = jax.random.split(key, 24)
    f32 = jnp.float32
    nrm = lambda k, shape, s: jax.random.normal(k, shape, f32) * s
    n_pages = PAST_LEN // PAGE_SIZE
    n_used = DEC_BATCH * n_pages
    n_phys = n_used + n_used // 4
    perm = jax.random.permutation(ks[0], n_phys).astype(jnp.int32)
    page_table = perm[:n_used].reshape(DEC_BATCH, n_pages)
    dt = jnp.exp(jax.random.uniform(ks[1], (DEPTH, N_HEADS_GDN), f32, math.log(1e-3), math.log(1e-1)))
    dt_bias = dt + jnp.log(-jnp.expm1(-dt))
    a_log = jnp.log(jax.random.uniform(ks[2], (DEPTH, N_HEADS_GDN), f32, 1.0, 16.0))
    return {
        'x_prompt': nrm(ks[3], (BATCH, SEQ, D_MODEL), 1.0),
        'x_sample': nrm(ks[4], (DEC_BATCH, DEC_SEQ, D_MODEL), 1.0),
        'cache_k': nrm(ks[5], (DEPTH, n_phys, PAGE_SIZE, N_HEADS_ATT, HEAD_DIM_ATT), 1.0),
        'cache_v': nrm(ks[6], (DEPTH, n_phys, PAGE_SIZE, N_HEADS_ATT, HEAD_DIM_ATT), 1.0),
        'cache_kidx': nrm(ks[7], (DEPTH, n_phys, PAGE_SIZE, IDX_DIM), 1.0),
        'state_ssm': nrm(ks[8], (DEPTH, DEC_BATCH, N_HEADS_GDN, HEAD_DIM_K, HEAD_DIM_V), HEAD_DIM_K ** -0.5),
        'state_conv': nrm(ks[9], (DEPTH, DEC_BATCH, CONV_W - 1, CONV_CH), 1.0),
        'page_table': page_table,
        'norm_mix': 1.0 + nrm(ks[10], (DEPTH, D_MODEL), 0.02),
        'w_in': nrm(ks[11], (DEPTH, D_MODEL, N_IN), D_MODEL ** -0.5),
        'conv_w': nrm(ks[12], (DEPTH, CONV_W, CONV_CH), CONV_W ** -0.5),
        'a_log': a_log,
        'dt_bias': dt_bias,
        'norm_gdn_out': 1.0 + nrm(ks[13], (DEPTH, HEAD_DIM_V), 0.02),
        'w_out': nrm(ks[14], (DEPTH, D_MIX, D_MODEL), D_MIX ** -0.5),
        'norm_mlp': 1.0 + nrm(ks[15], (DEPTH, D_MODEL), 0.02),
        'w_up': nrm(ks[16], (DEPTH, D_MODEL, D_FF), D_MODEL ** -0.5),
        'w_down': nrm(ks[17], (DEPTH, D_FF, D_MODEL), D_FF ** -0.5),
        'norm_final': 1.0 + nrm(ks[18], (D_MODEL,), 0.02),
    }

def reference(x_prompt, x_sample, cache_k, cache_v, cache_kidx, state_ssm, state_conv, page_table,
              norm_mix, w_in, conv_w, a_log, dt_bias, norm_gdn_out, w_out, norm_mlp, w_up, w_down, norm_final):
    bp = x_prompt.shape[0]
    bs = x_sample.shape[0]
    past = page_table.shape[1] * cache_k.shape[2]
    dt = x_prompt.dtype
    yp, ys = x_prompt, x_sample
    kp_l, vp_l, kip_l, sp_l, cp_l = [], [], [], [], []
    ks_l, vs_l, kis_l, ss_l, cs_l = [], [], [], [], []
    for l in range(DEPTH):
        w = (norm_mix[l], w_in[l], conv_w[l], a_log[l], dt_bias[l], norm_gdn_out[l],
             w_out[l], norm_mlp[l], w_up[l], w_down[l])
        yp, kp, vp, kip, sp, cp = hybrid_layer(
            yp,
            jnp.zeros((bp, 0, N_HEADS_ATT, HEAD_DIM_ATT), dt),
            jnp.zeros((bp, 0, N_HEADS_ATT, HEAD_DIM_ATT), dt),
            jnp.zeros((bp, 0, IDX_DIM), dt),
            jnp.zeros((bp, N_HEADS_GDN, HEAD_DIM_K, HEAD_DIM_V), state_ssm.dtype),
            jnp.zeros((bp, CONV_W - 1, CONV_CH), dt),
            *w)
        k_past = cache_k[l][page_table].reshape(bs, past, N_HEADS_ATT, HEAD_DIM_ATT)
        v_past = cache_v[l][page_table].reshape(bs, past, N_HEADS_ATT, HEAD_DIM_ATT)
        ki_past = cache_kidx[l][page_table].reshape(bs, past, IDX_DIM)
        ys, ks_, vs_, kis, ss, cs = hybrid_layer(ys, k_past, v_past, ki_past, state_ssm[l], state_conv[l], *w)
        kp_l.append(kp); vp_l.append(vp); kip_l.append(kip); sp_l.append(sp); cp_l.append(cp)
        ks_l.append(ks_); vs_l.append(vs_); kis_l.append(kis); ss_l.append(ss); cs_l.append(cs)
    y_prompt = rmsnorm(yp, norm_final)
    y_sample = rmsnorm(ys, norm_final)
    return (y_prompt, y_sample,
            jnp.stack(kp_l), jnp.stack(vp_l), jnp.stack(kip_l), jnp.stack(sp_l), jnp.stack(cp_l),
            jnp.stack(ks_l), jnp.stack(vs_l), jnp.stack(kis_l), jnp.stack(ss_l), jnp.stack(cs_l))


_drawn_inputs = setup_inputs


def setup_inputs(seed=0):
    import zlib

    import numpy as np

    out = dict(_drawn_inputs(seed))
    spreads = {}
    factors = {'norm_gdn_out': 6.383, 'norm_mlp': 3.308, 'norm_final': 2.903}
    for name, (base, spread) in spreads.items():
        noise = np.random.default_rng([zlib.crc32(name.encode()), seed]).standard_normal(out[name].shape)
        drawn = base * np.exp(spread * noise) if base else spread * noise
        out[name] = __import__('jax').numpy.asarray(drawn.astype(out[name].dtype))
    for name, factor in factors.items():
        out[name] = (out[name] * factor).astype(out[name].dtype)
    return out
```

```python
from contextlib import ExitStack

import numpy as np

import concourse.bass as bass
from concourse import mybir

F32 = mybir.dt.float32
BF16 = mybir.dt.bfloat16
I32 = mybir.dt.int32
ALU = mybir.AluOpType
ACT = mybir.ActivationFunctionType
AX_X = mybir.AxisListType.X

P = 128
D = 1024
KD = D // P
SEQ = 1024
NT = SEQ // P
DB, DS = 8, 8
NS = DB * DS
TOK = SEQ + NS
PAST, PAGE = 2048, 128
NPG = PAST // PAGE
LS = PAST + NS
H, HD = 8, 64
AW = H * HD
NI, DI = 4, 64
TOPK = 256
G, DK = 4, 128
GW = G * DK
CW = 4
CC = 3 * GW
CF = CC // P
FF = 4 * D
EPS = 1e-6
OFF_Q, OFF_K, OFF_V = 0, AW, 2 * AW
OFF_QI = 3 * AW
OFF_KI = OFF_QI + NI * DI
OFF_WI = OFF_KI + DI
OFF_CONV = OFF_WI + NI
OFF_A = OFF_CONV + CC
OFF_Z = OFF_A + 2 * G
N_IN = OFF_Z + GW
FIRST_SEL = TOPK // P
NEG_SCORE = -3.0e38
TAKEN = -3.3e38
MASKED = -1.0e30
LEVELS = 7
S_LEVELS = 3

IX_QI, IX_KI, IX_KI2, IX_WI, IX_A, IX_B = 0, 256, 320, 384, 388, 392
IX_W = 396


def constants():
    r = np.arange(P)
    row, col = r[:, None], r[None, :]
    s_ok = (row < NS) & (col < NS) & (row // DS == col // DS)
    parts = {}
    parts["ident"] = np.eye(P)
    parts["ones"] = np.ones((P, P))
    parts["tri"] = (row <= col)
    parts["tri_s"] = (row <= col) & s_ok
    parts["block_s"] = s_ok
    lev = []
    for l in range(LEVELS):
        s = 1 << l
        lev.append(-1.0 * ((row // (2 * s) == col // (2 * s)) & (row // s % 2 == 0) & (col // s % 2 == 1)))
    parts["level"] = np.concatenate(lev, 1)
    parts["score_causal"] = NEG_SCORE * (col > row)
    parts["score_new"] = NEG_SCORE * ~(s_ok & (col <= row))[:, :NS]
    parts["attn_causal"] = MASKED * (col > row)
    parts["low_big"] = -MASKED * (col >= row)
    parts["low_big_s"] = -MASKED * ~((col < row) & s_ok)
    parts["up_big"] = MASKED * (col < row)
    parts["up_big_s"] = MASKED * ~((row <= col) & s_ok)
    sel, sum_h = [], []
    for g in range(2):
        m = np.zeros((P, P))
        for bb in range(4):
            for h in range(NI):
                for q in range(DS):
                    m[(4 * g + bb) * DS + q, bb * 32 + h * DS + q] = 1
        sel.append(m)
        sum_h.append(m.T[:, :NS])
    parts["sel_ix"] = np.concatenate(sel, 1)
    parts["sum_ix"] = np.concatenate(sum_h, 1)
    parts["head_ix"] = ((r // DS) % NI)[:, None] == np.arange(NI)[None]
    sel = []
    for i in range(DB // 2):
        m = np.zeros((P, P))
        for b2 in range(2):
            for h in range(H):
                for q in range(DS):
                    m[(2 * i + b2) * DS + q, b2 * 64 + h * DS + q] = 1
        sel.append(m)
    parts["sel_at"] = np.concatenate(sel, 1)
    parts["in_batch"] = (r[:, None] < NS) & (r[:, None] // DS == np.arange(DB)[None])
    parts["columns"] = np.broadcast_to((np.arange(NS) // DS == np.arange(DB)[:, None]).reshape(1, -1), (P, DB * NS))
    at, where = 0, {}
    for n, a in parts.items():
        where[n] = (at, a.shape[1])
        at += a.shape[1]
    return np.ascontiguousarray(np.concatenate([np.asarray(a, np.float32) for a in parts.values()], 1)), where


CONST, CONST_AT = constants()
NC_COLS = CONST.shape[1]
BF_CONST = ("ident", "level", "columns", "attn_causal", "low_big", "low_big_s", "up_big", "up_big_s", "sel_at")
F_CONST = tuple(n for n in CONST_AT if n not in BF_CONST[1:])


class Map:

    def __init__(self, start=0):
        self.at = start

    def take(self, n):
        self.at += n
        return self.at - n


STORES = ("kidx", "mix0", "mix1", "mix2", "mix3", "conv", "ssm", "y")


class Kernel:

    def __init__(self, nc, ctx, a):
        self.nc, self.ctx, self.a = nc, ctx, a
        self.in_use = []
        self.stored = {n: nc.alloc_semaphore(name=n + "_stored") for n in STORES}
        self.words = 53200
        self.arena = ctx.enter_context(nc.sbuf_tensor("arena", [P, self.words], F32))
        self.banks = ctx.enter_context(nc.psum_tensor("banks", [P, 8 * 512], F32))
        self.psum = [self.banks[:, i * 512:(i + 1) * 512] for i in range(8)]
        m = Map()
        self.c = {}
        for n in F_CONST:
            w = CONST_AT[n][1]
            self.c[n] = self.view(m.take(w), w)
        self.b = {}
        for n in BF_CONST:
            w = CONST_AT[n][1]
            self.b[n] = self.view(m.take(w // 2), w // 2).bitcast(BF16)
        self.g_mix = self.view(m.take(KD), KD)
        self.g_mlp = self.view(m.take(KD), KD)
        self.conv_w = self.view(m.take(CF * CW), CF, CW)
        self.gdn_row = self.view(m.take(GW), G, DK)
        self.a_row = self.view(m.take(2 * G), 2 * G)
        self.table = self.view(m.take(DB * NPG), DB * NPG).bitcast(I32)
        self.eps = self.view(m.take(1), 1)
        self.hT_at = m.take(KD * TOK)
        self.x2_at = m.at
        self.psI = self.view(m.take(IX_W), IX_W)
        self.psA = self.view(m.take(3 * AW), 3 * AW)
        self.psC = self.view(m.take(CC), CC)
        self.psZ = self.view(m.take(GW), GW)
        self.maskP = []
        for t in range(NT):
            n = (t + 1) * P
            self.maskP.append(self.view(m.take(n // 2), n // 2).bitcast(BF16) if t >= FIRST_SEL else None)
        self.maskS = self.view(m.take(LS // 2), LS // 2).bitcast(BF16)
        self.kiwi = self.view(m.take(NT * 76), NT, 76)
        self.xc_at = m.take(CF * (SEQ + CW - 1))
        self.z_at = m.take(NT * GW)
        self.free_at = m.at
        self.sc_at = m.take(sum((t + 1) * P for t in range(FIRST_SEL, NT)) + LS)
        self.ring_at = m.take(2 * KD * 512)
        self.stage_at = m.take(4 * 512)
        self.best_at = m.take(64)
        assert m.at <= self.words, m.at

    def view(self, at, *dims):
        n = int(np.prod(dims))
        ap = self.arena[:, at:at + n]
        if len(dims) == 2:
            ap = ap.rearrange("p (a b) -> p a b", a=dims[0])
        if len(dims) == 3:
            ap = ap.rearrange("p (a b c) -> p a b c", a=dims[0], b=dims[1])
        return ap

    def sem(self, name):
        self.in_use.append(self.nc.alloc_semaphore(name=name))
        return self.in_use[-1]

    def stage_done(self):
        self.nc.all_engine_barrier()
        self.nc.clear_and_free_semaphores(self.in_use)
        self.nc.all_engine_barrier()
        self.in_use = []

    def sems(self, name, n):
        return [self.sem(f"{name}{i}") for i in range(n)]


def rows_of(t):
    return P if t < NT else NS


def stage_constants(k):
    nc, a = k.nc, k.a
    landed, to_bf = k.sem("const_landed"), k.sem("const_bf16")
    stage = k.view(k.xc_at, NC_COLS)
    small = 6
    with nc.Block() as block:
        @block.sync
        def _(sp):
            sp.dma_start(stage, a["const"]).then_inc(landed, 16)
            with nc.allow_non_contiguous_dma(reason="small parameters laid over partitions"):
                sp.dma_start(k.g_mix, a["norm_mix"].rearrange("a (k p) -> p (a k)", p=P)).then_inc(landed, 16)
                sp.dma_start(k.g_mlp, a["norm_mlp"].rearrange("a (k p) -> p (a k)", p=P)).then_inc(landed, 16)
                for j in range(CW):
                    sp.dma_start(k.conv_w[:, :, j], a["conv_w"][0, j, :].rearrange("(f p) -> p f", p=P)).then_inc(landed, 16)
            for h in range(G):
                sp.dma_start(k.gdn_row[:, h, :], a["norm_gdn_out"].partition_broadcast(P).rearrange("p a n -> p (a n)")).then_inc(landed, 16)
            sp.dma_start(k.a_row[:, 0:G], a["a_log"].partition_broadcast(P).rearrange("p a n -> p (a n)")).then_inc(landed, 16)
            sp.dma_start(k.a_row[:, G:2 * G], a["dt_bias"].partition_broadcast(P).rearrange("p a n -> p (a n)")).then_inc(landed, 16)
            sp.dma_start(k.table[0:1, :], a["page_table"].rearrange("b n -> (b n)").rearrange("(a n) -> a n", a=1)).then_inc(landed, 16)
            sp.wait_ge(landed, 16 * (6 + CW + G))

        @block.vector
        def _(dve):
            dve.memset(k.eps, EPS)
            dve.wait_ge(landed, 16 * (6 + CW + G))
            for n in F_CONST:
                at, w = CONST_AT[n]
                dve.tensor_copy(k.c[n], stage[:, at:at + w])
            for n in BF_CONST:
                at, w = CONST_AT[n]
                dve.tensor_copy(k.b[n], stage[:, at:at + w])


def stage_norm(k, name, tiles, out_at, gain, load):
    nc = k.nc
    out = k.view(out_at, KD, TOK)
    free = Map(k.ring_at)
    xn = [k.view(free.take(D), D) for _ in range(2)]
    junk = k.view(free.take(D), D)
    stat = k.view(free.take(3 * (NT + 1)), 3, NT + 1)
    loaded = k.sems(name + "_loaded", 3)
    squared, rooted, scaled = k.sem(name + "_squared"), k.sem(name + "_rooted"), k.sem(name + "_rstd")
    normed, turned, kept = k.sem(name + "_normed"), k.sem(name + "_turned"), k.sem(name + "_kept")
    n = NT + 1
    with nc.Block() as block:
        if load is not None:
            @block.sync
            def _(sp):
                for t in range(n):
                    if t >= 3:
                        sp.wait_ge(normed, t - 2)
                    sp.dma_start(tiles[t][0:rows_of(t), :], load(t)).then_inc(loaded[t % 3], 16)

        @block.scalar
        def _(act):
            for t in range(n):
                r = rows_of(t)
                if load is not None:
                    act.wait_ge(loaded[t % 3], 16 * (t // 3 + 1))
                if t:
                    act.wait_ge(squared, t)
                act.activation(junk[0:r, :], tiles[t][0:r, :], ACT.Square, accum_out=stat[0:r, 0, t:t + 1]).then_inc(squared, 1)
                act.wait_ge(squared, t + 1)
                act.activation(stat[0:r, 1, t:t + 1], stat[0:r, 0, t:t + 1], ACT.Sqrt, scale=1.0 / D, bias=k.eps[0:r, :]).then_inc(rooted, 1)

        @block.vector
        def _(dve):
            def norm(t):
                r = rows_of(t)
                dve.wait_ge(rooted, t + 1)
                dve.reciprocal(stat[0:r, 2, t:t + 1], stat[0:r, 1, t:t + 1]).then_inc(scaled, 1)
                if t >= 2:
                    dve.wait_ge(turned, t - 1)
                dve.wait_ge(scaled, t + 1)
                dve.tensor_scalar(xn[t % 2][0:r, :], tiles[t][0:r, :], stat[0:r, 2, t:t + 1], None, ALU.mult).then_inc(normed, 1)

            def keep(t):
                r = rows_of(t)
                dve.wait_ge(turned, t + 1)
                for half in range(2):
                    src = k.psum[2 * (t % 2) + half][:, :].rearrange("p (f n) -> p f n", f=4)[:, :, 0:r]
                    g = gain[:, 4 * half:4 * half + 4].unsqueeze(2).to_broadcast([P, 4, r])
                    dve.tensor_tensor(out[:, 4 * half:4 * half + 4, t * P:t * P + r], src, g, ALU.mult).then_inc(kept, 1)

            norm(0)
            for t in range(n):
                if t + 1 < n:
                    norm(t + 1)
                keep(t)

        @block.tensor
        def _(pe):
            for t in range(n):
                r = rows_of(t)
                pe.wait_ge(normed, t + 1)
                if t >= 2:
                    pe.wait_ge(kept, 2 * (t - 1))
                for f in range(KD):
                    last = pe.transpose(k.psum[2 * (t % 2) + f // 4][:, (f % 4) * P:(f % 4) * P + r],
                                        xn[t % 2][0:r, f * P:(f + 1) * P], k.c["ident"][0:r, 0:r])
                last.then_inc(turned, 1)


def projection_of_indexer():
    jobs = [(0, "F", f * P, P, j) for f in range(2) for j in range(2)]
    jobs += [(0, "F", IX_KI, P, j) for j in range(2)]
    jobs += [(0, "T", IX_KI2, IX_W - IX_KI2, t) for t in range(NT)]
    jobs += [(0, "S", 0, IX_W, 0)]
    return jobs


def load_indexer_weights(k, q, dst, sem):
    w = k.a["w_in"][0].rearrange("(k p) n -> p k n", p=P)
    for at, off, n in ((IX_QI, OFF_QI, NI * DI), (IX_KI, OFF_KI, DI), (IX_KI2, OFF_KI, DI + NI), (IX_A, OFF_A, 2 * G)):
        q.dma_start(dst[:, :, at:at + n], w[:, :, off:off + n]).then_inc(sem, 16)
    return 4


def project_products(k, pe, jobs, banks, sems):
    hT = k.view(k.hT_at, KD, TOK)
    landed, made, kept = sems
    seen = -1
    for n, (c, kind, col, w, at) in enumerate(jobs):
        if c != seen:
            pe.wait_ge(landed[c % 2], k.landed_at[c])
            seen = c
        if n >= banks:
            pe.wait_ge(kept, n - banks + 1)
        bank = k.psum[n % banks]
        ring = k.view(k.ring_at + (c % 2) * KD * 512, KD, 512)
        if kind == "K":
            pe.wait_ge(kept, k.turn_of[n] + 1)
            src = k.view(k.stage_at + k.slot_of[k.turn_of[n]] * 512, 512)
            for i in range(4):
                last = pe.transpose(bank[:, i * P:(i + 1) * P], src[:, i * P:(i + 1) * P], k.c["ident"])
        for f in range(KD if kind != "K" else 0):
            if kind == "F":
                last = pe.matmul(bank[0:w, :], ring[:, f, col:col + w], hT[:, f, at * 512:(at + 1) * 512],
                                 start=(f == 0), stop=(f == KD - 1))
            elif kind == "T":
                last = pe.matmul(bank[:, 0:w], hT[:, f, at * P:(at + 1) * P], ring[:, f, col:col + w],
                                 start=(f == 0), stop=(f == KD - 1))
            else:
                last = pe.matmul(bank[0:NS, 0:w], hT[:, f, SEQ:TOK], ring[:, f, col:col + w],
                                 start=(f == 0), stop=(f == KD - 1))
        last.then_inc(made, 1)


def stage_indexer_projection(k):
    nc = k.nc
    jobs = projection_of_indexer()
    landed, made, kept = k.sems("ixw_landed", 2), k.sem("ix_made"), k.sem("ix_kept")
    k.qiT = k.view(k.xc_at, 2, SEQ)
    k.kiT = k.view(k.xc_at + 2 * SEQ, SEQ)
    with nc.Block() as block:
        @block.sync
        def _(sp):
            n = load_indexer_weights(k, sp, k.view(k.ring_at, KD, 512), landed[0])
            k.landed_at = {0: 16 * n}

        @block.tensor
        def _(pe):
            project_products(k, pe, jobs, 8, (landed, made, kept))

        @block.scalar
        def _(act):
            for n, (c, kind, col, w, at) in enumerate(jobs):
                act.wait_ge(made, n + 1)
                bank = k.psum[n % 8]
                if kind == "F" and col == IX_KI:
                    act.copy(k.kiT[:, at * 512:(at + 1) * 512], bank[:, :]).then_inc(kept, 1)
                elif kind == "F":
                    act.copy(k.qiT[:, col // P, at * 512:(at + 1) * 512], bank[:, :]).then_inc(kept, 1)
                elif kind == "T":
                    act.copy(k.kiwi[:, at, :], bank[:, 0:w]).then_inc(kept, 1)
                else:
                    act.copy(k.psI[0:NS, :], bank[0:NS, 0:w]).then_inc(kept, 1)


def stage_prompt_scores(k):
    nc = k.nc
    k.scP, at = [None] * NT, k.sc_at
    for t in range(FIRST_SEL, NT):
        k.scP[t] = k.view(at, (t + 1) * P)
        at += (t + 1) * P
    k.scS = k.view(at, LS)
    relu_buf = [k.view(k.ring_at + i * 512, 512) for i in range(4)]
    w_half = k.view(k.ring_at + 2048, NT, NI)
    made, relued, summed, halved = k.sem("scp_made"), k.sem("scp_relued"), k.sem("scp_summed"), k.sem("scp_halved")
    out_sem = k.stored["kidx"]
    items = [(t, c, min(512, (t + 1) * P - c), h)
             for t in range(FIRST_SEL, NT) for c in range(0, (t + 1) * P, 512) for h in range(NI)]
    with nc.Block() as block:
        @block.sync
        def _(sp):
            sp.dma_start(k.a["new_kidx_prompt"][0, 0].rearrange("(t p) d -> p t d", p=P), k.kiwi[:, :, 0:DI]).then_inc(out_sem, 16)
            sp.dma_start(k.a["new_kidx_sample"][0].rearrange("b t d -> (b t) d"), k.psI[0:NS, IX_KI:IX_KI + DI]).then_inc(out_sem, 16)
            sp.wait_ge(out_sem, 32)

        @block.tensor
        def _(pe):
            for n, (t, c, w, h) in enumerate(items):
                if n >= 4:
                    pe.wait_ge(relued, n - 3)
                lo = (h % 2) * DI
                pe.matmul(k.psum[n % 4][:, 0:w], k.qiT[lo:lo + DI, h // 2, t * P:(t + 1) * P],
                          k.kiT[lo:lo + DI, c:c + w], start=True, stop=True).then_inc(made, 1)

        @block.scalar
        def _(act):
            for n, (t, c, w, h) in enumerate(items):
                act.wait_ge(made, n + 1)
                if n >= 4:
                    act.wait_ge(summed, n - 3)
                act.activation(relu_buf[n % 4][:, 0:w], k.psum[n % 4][:, 0:w], ACT.Relu).then_inc(relued, 1)

        @block.vector
        def _(dve):
            dve.tensor_scalar(w_half, k.kiwi[:, :, DI:DI + NI], DI ** -0.5 * NI ** -0.5, None, ALU.mult).then_inc(halved, 1)
            dve.wait_ge(halved, 1)
            done = 0
            for n, (t, c, w, h) in enumerate(items):
                dve.wait_ge(relued, n + 1)
                sc = k.scP[t][:, c:c + w]
                if h == 0:
                    dve.tensor_scalar(sc, relu_buf[n % 4][:, 0:w], w_half[:, t, h:h + 1], None, ALU.mult).then_inc(summed, 1)
                else:
                    dve.wait_ge(summed, n)
                    dve.scalar_tensor_tensor(out=sc, in0=relu_buf[n % 4][:, 0:w], scalar=w_half[:, t, h:h + 1],
                                             in1=sc, op0=ALU.mult, op1=ALU.add).then_inc(summed, 1)
            dve.wait_ge(summed, len(items))
            for t in range(FIRST_SEL, NT):
                own = k.scP[t][:, t * P:(t + 1) * P]
                dve.tensor_tensor(own, own, k.c["score_causal"], ALU.add)


def stage_sample_scores(k):
    nc = k.nc
    m = Map(k.xc_at)
    qi_dup = k.view(m.take(NI * 2 * DI), NI, 2 * DI)
    qiS = k.view(m.take(NI * NS), NI, NS)
    qiB = k.view(m.take(DB * NI * DS), DB, NI * DS)
    kiN = k.view(m.take(NS), NS)
    wi_s = k.view(m.take(NI), NI)
    w_pick = [k.view(m.take(NI), NI) for _ in range(2)]
    w_row = k.view(m.take(2), 2)
    pages = [k.view(m.take(NPG * DI), NPG, DI) for _ in range(2)]
    k.kT4 = [k.view(m.take(NPG // 2 * PAGE), NPG // 2, PAGE) for _ in range(4)]
    rel = [k.view(m.take(512), 512) for _ in range(3)]
    assert m.at <= k.z_at + NT * GW
    landed = k.sems("kidx_landed", 2)
    prep, prep_pe, turned, kept = k.sem("scs_prep"), k.sem("scs_prep_pe"), k.sem("scs_turned"), k.sem("scs_kept")
    made, relued, summed, drained = k.sem("scs_made"), k.sem("scs_relued"), k.sem("scs_summed"), k.sem("scs_drained")
    NH = NI * DS
    with nc.Block() as block:
        @block.sync
        def _(sp):
            for b in range(DB):
                if b >= 2:
                    sp.wait_ge(turned, b - 1)
                for p in range(NPG):
                    page = sp.value_load(k.table[0:1, b * NPG + p:b * NPG + p + 1], min_val=0, max_val=k.a["cache_kidx"].shape[1] - 1)
                    sp.dma_start(pages[b % 2][:, p, :], k.a["cache_kidx"][0, bass.ds(page, 1), :, :].rearrange("a p d -> p (a d)")).then_inc(landed[b % 2], 16)

        @block.tensor
        def _(pe):
            pe.wait_ge(prep, 1)
            for h in range(NI):
                last = pe.transpose(k.psum[4][:, h * NS:(h + 1) * NS], qi_dup[0:NS, h, :], k.c["ident"][0:NS, 0:NS])
            last = pe.transpose(k.psum[4][0:DI, NI * NS:NI * NS + NS], k.psI[0:NS, IX_KI:IX_KI + DI], k.c["ident"][0:NS, 0:NS])
            last.then_inc(prep_pe, 1)
            for g in range(2):
                last = pe.matmul(k.psum[5][:, g * NI:(g + 1) * NI], k.c["sel_ix"][0:NS, g * P:(g + 1) * P], wi_s[0:NS, :],
                                 start=True, stop=True)
            last.then_inc(prep_pe, 1)
            pe.wait_ge(prep, 7)

            def turn(b):
                pe.wait_ge(landed[b % 2], 16 * NPG * (b // 2 + 1))
                if b >= 1:
                    pe.wait_ge(kept, 2 * b)
                for j in range(NPG // 2):
                    last = pe.transpose(k.psum[4 + j // 4][:, (j % 4) * P:(j % 4 + 1) * P],
                                        pages[b % 2][:, 2 * j:2 * j + 2, :].rearrange("p a d -> p (a d)"), k.c["ident"])
                last.then_inc(turned, 1)

            n = 0
            for g in range(2):
                for bb in range(4):
                    turn(4 * g + bb)
                pe.wait_ge(kept, 8 * (g + 1))
                for par in range(2):
                    for half in range(2):
                        if n >= 2:
                            pe.wait_ge(relued, n - 1)
                        for bb in range(4):
                            last = pe.matmul(k.psum[6 + n % 2][bb * NH:(bb + 1) * NH, :],
                                             qiB[par * DI:(par + 1) * DI, 4 * g + bb, :],
                                             k.kT4[bb][par * DI:(par + 1) * DI, 4 * half:4 * half + 4, :],
                                             start=True, stop=True)
                        last.then_inc(made, 1)
                        pe.wait_ge(relued, n + 1)
                        pe.matmul(k.psum[n % 4][0:NS, :], k.c["sum_ix"][:, g * NS:(g + 1) * NS], rel[n % 3],
                                  start=(g == 0), stop=(g == 1)).then_inc(summed, 1)
                        n += 1
                pe.wait_ge(relued, n)
            pe.wait_ge(drained, 4)
            for g in range(2):
                for bb in range(4):
                    last = pe.matmul(k.psum[6 + g][bb * NH:(bb + 1) * NH, 0:NS], qiB[0:DI, 4 * g + bb, :], kiN[0:DI, :],
                                     start=True, stop=True)
                last.then_inc(made, 1)
            for g in range(2):
                pe.wait_ge(relued, 8 + g + 1)
                pe.matmul(k.psum[0][0:NS, 0:NS], k.c["sum_ix"][:, g * NS:(g + 1) * NS], rel[g][:, 0:NS],
                          start=(g == 0), stop=(g == 1)).then_inc(summed, 1)

        @block.scalar
        def _(act):
            for b in range(DB):
                act.wait_ge(turned, b + 1)
                if b >= 4:
                    act.wait_ge(made, 4)
                if b == 0:
                    act.wait_ge(prep, 7)
                for i in range(2):
                    act.copy(k.kT4[b % 4][:, 4 * i:4 * i + 4, :].rearrange("p a n -> p (a n)"), k.psum[4 + i][:, :]).then_inc(kept, 1)

        @block.vector
        def _(dve):
            for i in range(2):
                last = dve.tensor_copy(qi_dup[0:NS, :, i * DI:(i + 1) * DI], k.psI[0:NS, 0:NI * DI].rearrange("p (h d) -> p h d", h=NI))
            last = dve.tensor_scalar(wi_s[0:NS, :], k.psI[0:NS, IX_WI:IX_WI + NI], DI ** -0.5 * NI ** -0.5, None, ALU.mult)
            last.then_inc(prep, 1)
            dve.wait_ge(prep_pe, 1)
            dve.tensor_copy(qiB.rearrange("p b (h q) -> p b h q", h=NI),
                            k.psum[4][:, 0:NI * NS].rearrange("p (h b q) -> p b h q", h=NI, b=DB)).then_inc(prep, 1)
            dve.tensor_copy(kiN[0:DI, :], k.psum[4][0:DI, NI * NS:NI * NS + NS]).then_inc(prep, 1)
            dve.wait_ge(prep_pe, 2)
            for g in range(2):
                dve.tensor_tensor(w_pick[g], k.psum[5][:, g * NI:(g + 1) * NI], k.c["head_ix"], ALU.mult).then_inc(prep, 1)
            dve.wait_ge(prep, 5)
            for g in range(2):
                dve.reduce_sum(w_row[:, g:g + 1], w_pick[g], AX_X).then_inc(prep, 1)
            dve.wait_ge(prep, 7)
            for n in range(8):
                dve.wait_ge(made, n + 1)
                if n >= 3:
                    dve.wait_ge(summed, n - 2)
                dve.tensor_scalar(rel[n % 3], k.psum[6 + n % 2][:, :], 0.0, w_row[:, n // 4:n // 4 + 1], ALU.max, ALU.mult).then_inc(relued, 1)
            dve.wait_ge(summed, 8)
            for n in range(4):
                par, half = n // 2, n % 2
                dst = k.scS[0:NS, 0:PAST].rearrange("q (j r n) -> q r j n", r=2, n=PAGE)[:, par, 4 * half:4 * half + 4, :]
                dve.tensor_copy(dst, k.psum[n][0:NS, :].rearrange("q (j n) -> q j n", j=4)).then_inc(drained, 1)
            for g in range(2):
                dve.wait_ge(made, 8 + g + 1)
                dve.tensor_scalar(rel[g][:, 0:NS], k.psum[6 + g][:, 0:NS], 0.0, w_row[:, g:g + 1], ALU.max, ALU.mult).then_inc(relued, 1)
            dve.wait_ge(summed, 10)
            dve.tensor_tensor(k.scS[0:NS, PAST:LS], k.psum[0][0:NS, 0:NS], k.c["score_new"][0:NS, :], ALU.add)


CHUNKS = (OFF_Q, OFF_K, OFF_V, OFF_CONV, OFF_CONV + 512, OFF_CONV + 1024, OFF_Z)


def projection_of_mixers():
    jobs = [(0, "F", f * P, P, j) for f in range(4) for j in range(2)] + [(0, "S", 0, 512, 0)]
    keys = [(1, "F", f * P, P, j) for f in range(4) for j in range(2)]
    jobs += interleave_turns(keys) + [(1, "S", 0, 512, 0)]
    jobs += [(2, "T", 0, 512, t) for t in range(NT)] + [(2, "S", 0, 512, 0)]
    for c in range(3):
        jobs += [(3 + c, "F", f * P, P, j) for f in range(4) for j in range(2)] + [(3 + c, "S", 0, 512, 0)]
    jobs += [(6, "T", 0, 512, t) for t in range(NT)] + [(6, "S", 0, 512, 0)]
    return jobs


def interleave_turns(keys):
    out = []
    for n in range(len(keys) + 2):
        if n < len(keys):
            out.append(keys[n])
        if n >= 2:
            c, _, col, w, j = keys[n - 2]
            out.append((c, "K", col, w, j))
    return out


def stage_mixer_projection(k):
    nc = k.nc
    jobs = projection_of_mixers()
    w = k.a["w_in"][0].rearrange("(k p) n -> p k n", p=P)
    landed, made, kept = k.sems("mxw_landed", 2), k.sem("mx_made"), k.sem("mx_kept")
    stored = [k.stored[f"mix{i}"] for i in range(4)]
    out_sem = k.sem("mx_out")
    last_job = {c: max(n for n, j in enumerate(jobs) if j[0] == c) for c in range(len(CHUNKS))}
    k.landed_at = {c: 16 * (c // 2 + 1) for c in range(len(CHUNKS))}
    staged = [n for n, j in enumerate(jobs) if j[0] <= 2 and j[1] != "S"]
    k.slot_of = {n: i % 4 for i, n in enumerate(staged)}
    order = {n: i for i, n in enumerate(staged)}
    k.turn_of = {n: jobs.index((1, "F") + j[2:]) for n, j in enumerate(jobs) if j[1] == "K"}
    turned_by = {m: n for n, m in k.turn_of.items()}
    xc = k.view(k.xc_at, CF, SEQ + CW - 1)
    z = k.view(k.z_at, NT, GW)
    stage = [k.view(k.stage_at + i * 512, 512) for i in range(4)]
    topk_at = k.sem("topk_max"), k.sem("topk_taken")
    best = k.view(k.best_at, 8, 8)
    work = [(P, k.scP[t]) for t in range(FIRST_SEL, NT)] + [(NS, k.scS)]
    masks = [k.maskP[t] for t in range(FIRST_SEL, NT)] + [k.maskS]
    with nc.Block() as block:
        @block.sync
        def _(sp):
            for c, off in enumerate(CHUNKS):
                if c >= 2:
                    sp.wait_ge(made, last_job[c - 2] + 1)
                sp.dma_start(k.view(k.ring_at + (c % 2) * KD * 512, KD, 512), w[:, :, off:off + 512]).then_inc(landed[c % 2], 16)

        @block.tensor
        def _(pe):
            project_products(k, pe, jobs, 8, (landed, made, kept))

        @block.scalar
        def _(act):
            for n, (c, kind, col, wd, at) in enumerate(jobs):
                act.wait_ge(made, n + 1)
                bank = k.psum[n % 8]
                if kind == "S":
                    dst = (k.psA[0:NS, c * 512:(c + 1) * 512] if c <= 2 else
                           k.psC[0:NS, (c - 3) * 512:(c - 2) * 512] if c <= 5 else k.psZ[0:NS, :])
                    act.copy(dst, bank[0:NS, :]).then_inc(kept, 1)
                elif c <= 2:
                    i = order[n]
                    if i >= 4:
                        act.wait_ge(stored[i % 4], 16 * (i // 4))
                        if staged[i - 4] in turned_by:
                            act.wait_ge(made, turned_by[staged[i - 4]] + 1)
                    act.copy(stage[i % 4], bank[:, :]).then_inc(kept, 1)
                elif c <= 5:
                    act.copy(xc[:, (c - 3) * 4 + col // P, CW - 1 + at * 512:CW - 1 + (at + 1) * 512], bank[:, :]).then_inc(kept, 1)
                else:
                    act.copy(z[:, at, :], bank[:, :]).then_inc(kept, 1)

        @block.gpsimd
        def _(pool):
            pool.memset(xc[:, :, 0:CW - 1], 0.0)
            for i, n in enumerate(staged):
                c, kind, col, wd, at = jobs[n]
                pool.wait_ge(kept, n + 1)
                if c == 0:
                    dst, src = k.a["q_T"][col:col + P, at * 512:(at + 1) * 512], stage[i % 4]
                elif c == 1 and kind == "F":
                    dst, src = k.a["k_T"][col:col + P, at * 512:(at + 1) * 512], stage[i % 4]
                elif c == 1:
                    rows = k.a["new_k_prompt"][0, 0].rearrange("t h d -> t (h d)").rearrange("(j i p) n -> j p i n", i=4, p=P)
                    dst, src = rows[at, :, :, col:col + P], stage[i % 4].rearrange("p (i n) -> p i n", i=4)
                else:
                    dst, src = k.a["new_v_prompt"][0, 0].rearrange("t h d -> t (h d)")[at * P:(at + 1) * P, :], stage[i % 4]
                pool.dma_start(dst, src).then_inc(stored[i % 4], 16)
            for i in range(4):
                pool.wait_ge(stored[i], 16 * len(staged[i::4]))

        @block.vector
        def _(dve):
            maxed, taken = topk_at
            n = len(work)
            for r in range(TOPK // 8):
                for i, (rows, sc) in enumerate(work):
                    if r:
                        dve.wait_ge(taken, (r - 1) * n + i + 1)
                    dve.max(best[0:rows, i, :], sc[0:rows, :]).then_inc(maxed, 1)
                for i, (rows, sc) in enumerate(work):
                    dve.wait_ge(maxed, r * n + i + 1)
                    dve.match_replace(sc[0:rows, :], best[0:rows, i, :], sc[0:rows, :], TAKEN).then_inc(taken, 1)
            for i, (rows, sc) in enumerate(work):
                dve.wait_ge(taken, (TOPK // 8 - 1) * n + i + 1)
                dve.tensor_scalar(masks[i][0:rows, :], sc[0:rows, :], TAKEN, MASKED, ALU.not_equal, ALU.mult)


def stage_conv(k):
    nc, a = k.nc, k.a
    xc = k.view(k.xc_at, CF, SEQ + CW - 1)
    z = k.view(k.z_at, NT * GW)
    n_all = NT + 1
    m = Map(k.free_at)
    k.qkvS = k.view(m.take(CF * NS), CF, NS)
    k.gates = k.view(m.take(4 * n_all * G), 4, n_all * G)
    k.gdn_at = m.at
    acc = [k.view(m.take(SEQ), SEQ) for _ in range(2)]
    state = k.view(m.take(CC), CC)
    tail = k.view(m.take(CC), CC)
    xs = k.view(m.take(CF * DB * (DS + CW - 1)), CF * DB, DS + CW - 1)
    tap = [k.view(m.take(CF * NS), CF * DB, DS) for _ in range(2)]
    ab = k.view(m.take(n_all * 2 * G), n_all, 2 * G)
    w = [k.view(m.take(n_all * G), n_all, G) for _ in range(7)]
    alog = k.view(m.take(G), G)
    assert m.at <= k.words
    k.alog = alog
    landed, out_sem = k.sem("cv_landed"), k.stored["conv"]
    turned, tails, laid = k.sem("cv_turned"), k.sem("cv_tails"), k.sem("cv_laid")
    tapped, rounded, tapped_s = k.sem("cv_tapped"), k.sem("cv_silu"), k.sem("cv_tapped_sample")
    gate_v, gate_s = k.sem("cv_gate_vector"), k.sem("cv_gate_scalar")
    z_silu, z_done = k.sem("cv_z_silu"), k.sem("cv_z_done")
    zero = k.sem("cv_zero")
    with nc.Block() as block:
        @block.sync
        def _(sp):
            sp.dma_start(state[0:DB * (CW - 1), :], a["state_conv"][0].rearrange("b j c -> (b j) c")).then_inc(landed, 16)
            n = 0
            for b in range(DB):
                sp.dma_start(a["new_conv_sample"][0, b], k.psC[b * DS + DS - CW + 1:(b + 1) * DS, :]).then_inc(out_sem, 16)
            sp.dma_start(a["new_k_sample"][0].rearrange("b t h d -> (b t) (h d)"), k.psA[0:NS, AW:2 * AW]).then_inc(out_sem, 16)
            sp.dma_start(a["new_v_sample"][0].rearrange("b t h d -> (b t) (h d)"), k.psA[0:NS, 2 * AW:3 * AW]).then_inc(out_sem, 16)
            sp.wait_ge(tails, 3)
            sp.dma_start(a["new_conv_prompt"][0, 0], tail[0:CW - 1, :]).then_inc(out_sem, 16)
            sp.wait_ge(out_sem, 16 * (DB + 3))

        @block.tensor
        def _(pe):
            for f in range(CF):
                last = pe.transpose(k.psum[f // 4][0:CW - 1, (f % 4) * P:(f % 4 + 1) * P], xc[:, f, SEQ:SEQ + CW - 1], k.c["ident"])
            for f in range(CF):
                last = pe.transpose(k.psum[4 + f // 6][:, (f % 6) * NS:(f % 6 + 1) * NS], k.psC[0:NS, f * P:(f + 1) * P], k.c["ident"][0:NS, 0:NS])
            pe.wait_ge(landed, 16)
            n = DB * (CW - 1)
            for f in range(CF):
                last = pe.transpose(k.psum[3][:, f * n:(f + 1) * n], state[0:n, f * P:(f + 1) * P], k.c["ident"][0:n, 0:n])
            last.then_inc(turned, 1)

        @block.scalar
        def _(act):
            act.wait_ge(turned, 1)
            for i in range(3):
                act.copy(tail[0:CW - 1, i * 512:(i + 1) * 512], k.psum[i][0:CW - 1, :]).then_inc(tails, 1)
            act.wait_ge(gate_v, 4)
            act.activation(alog, k.a_row[:, 0:G], ACT.Exp).then_inc(gate_s, 1)
            act.activation(w[1], w[0], ACT.Abs).then_inc(gate_s, 1)
            act.wait_ge(gate_s, 2)
            act.activation(w[2], w[1], ACT.Exp, scale=-1.0).then_inc(gate_s, 1)
            act.activation(w[3], ab[:, :, G:2 * G], ACT.Exp, scale=-1.0).then_inc(gate_s, 1)
            act.wait_ge(gate_s, 4)
            act.activation(w[4], w[2], ACT.Ln, bias=1.0).then_inc(gate_s, 1)
            act.activation(w[5], w[3], ACT.Ln, bias=1.0).then_inc(gate_s, 1)
            for i in range(4):
                act.activation(z[:, i * 1024:(i + 1) * 1024], z[:, i * 1024:(i + 1) * 1024], ACT.Silu).then_inc(z_silu, 1)
            act.activation(k.psZ[0:NS, :], k.psZ[0:NS, :], ACT.Silu).then_inc(z_silu, 1)
            for f in range(CF):
                act.wait_ge(tapped, CW * (f + 1))
                act.activation(xc[:, f, 0:SEQ], acc[f % 2], ACT.Silu).then_inc(rounded, 1)
            act.wait_ge(tapped_s, 7)
            act.activation(k.qkvS.rearrange("p f n -> p (f n)"), tap[1].rearrange("p f n -> p (f n)"), ACT.Silu)

        @block.gpsimd
        def _(pool):
            for i in range(NT):
                pool.wait_ge(z_silu, i // 2 + 1)
                zi = z[:, i * GW:(i + 1) * GW]
                pool.tensor_tensor(zi, zi, k.gdn_row.rearrange("p h d -> p (h d)"), ALU.mult)
            pool.wait_ge(z_silu, 5)
            pool.tensor_tensor(k.psZ[0:NS, :], k.psZ[0:NS, :], k.gdn_row[0:NS].rearrange("p h d -> p (h d)"), ALU.mult)

        @block.vector
        def _(dve):
            dve.memset(ab, 0.0).then_inc(gate_v, 1)
            dve.wait_ge(gate_v, 1)
            dve.tensor_copy(ab[:, 0:NT, :], k.kiwi[:, :, DI + NI:DI + NI + 2 * G]).then_inc(gate_v, 1)
            dve.tensor_copy(ab[0:NS, NT, :], k.psI[0:NS, IX_A:IX_A + 2 * G]).then_inc(gate_v, 1)
            dve.wait_ge(gate_v, 3)
            dve.tensor_tensor(w[0], ab[:, :, 0:G], k.a_row[:, G:2 * G].unsqueeze(1).to_broadcast([P, n_all, G]), ALU.add).then_inc(gate_v, 1)
            dve.wait_ge(turned, 1)
            dve.tensor_copy(xs[:, :, 0:CW - 1], k.psum[3][:, 0:CF * DB * (CW - 1)].rearrange("p (f j) -> p f j", j=CW - 1)).then_inc(laid, 1)
            for i in range(2):
                dve.tensor_copy(xs[:, i * 6 * DB:(i + 1) * 6 * DB, CW - 1:], k.psum[4 + i][:, 0:6 * NS].rearrange("p (f j) -> p f j", j=DS)).then_inc(laid, 1)
            for f in range(CF):
                if f >= 2:
                    dve.wait_ge(rounded, f - 1)
                for j in range(CW):
                    wj = k.conv_w[:, f, j:j + 1]
                    if j == 0:
                        dve.tensor_scalar(acc[f % 2], xc[:, f, j:j + SEQ], wj, None, ALU.mult).then_inc(tapped, 1)
                    else:
                        dve.wait_ge(tapped, CW * f + j)
                        dve.scalar_tensor_tensor(out=acc[f % 2], in0=xc[:, f, j:j + SEQ], scalar=wj, in1=acc[f % 2],
                                                 op0=ALU.mult, op1=ALU.add).then_inc(tapped, 1)
            g, beta, lnb = (k.gates[:, i, :].rearrange("p (t h) -> p t h", h=G) for i in range(3))
            dve.wait_ge(gate_s, 6)
            dve.scalar_tensor_tensor(out=w[6], in0=w[0], scalar=0.0, in1=w[4], op0=ALU.max, op1=ALU.add).then_inc(gate_v, 1)
            dve.tensor_scalar(lnb, w[5], -1.0, None, ALU.mult)
            dve.tensor_scalar(w[3], w[3], 1.0, None, ALU.add).then_inc(gate_v, 1)
            dve.wait_ge(gate_v, 6)
            dve.scalar_tensor_tensor(out=g, in0=w[6], scalar=-1.0, in1=alog.unsqueeze(1).to_broadcast([P, n_all, G]),
                                     op0=ALU.mult, op1=ALU.mult)
            dve.reciprocal(beta, w[3])
            dve.wait_ge(laid, 3)
            n = 0
            xs4 = xs.rearrange("p (f b) j -> p f b j", b=DB)
            t4 = [t.rearrange("p (f b) j -> p f b j", b=DB) for t in tap]
            for j in range(CW):
                wj = k.conv_w[:, :, j:j + 1].unsqueeze(3).to_broadcast([P, CF, DB, DS])
                if j >= 2:
                    dve.wait_ge(tapped_s, n)
                dve.tensor_tensor(t4[0 if j else 1], xs4[:, :, :, j:j + DS], wj, ALU.mult).then_inc(tapped_s, 1)
                n += 1
                if j:
                    dve.wait_ge(tapped_s, n)
                    dve.tensor_tensor(tap[1], tap[1], tap[0], ALU.add).then_inc(tapped_s, 1)
                    n += 1


def gdn_view(k, t, part):
    if t == NT:
        return k.qkvS[:, part * G:(part + 1) * G, :]
    return k.view(k.xc_at, CF, SEQ + CW - 1)[:, part * G:(part + 1) * G, t * P:(t + 1) * P]


def stage_l2norm(k):
    nc = k.nc
    xc = k.view(k.xc_at, CF, SEQ + CW - 1)
    m = Map(k.gdn_at)
    sq = [k.view(m.take(512), 512) for _ in range(4)]
    root = [k.view(m.take(512), 512) for _ in range(4)]
    inv = [k.view(m.take(512), 512) for _ in range(2)]
    q_eps = k.view(m.take(1), 1)
    ready = k.sem("l2_eps")
    squared, summed, rooted, inverted, scaled = (k.sem("l2_" + n) for n in ("squared", "summed", "rooted", "inverted", "scaled"))
    items = [(xc[:, f, j * 512:(j + 1) * 512], [(0, 512, f < G)]) for f in range(2 * G) for j in range(2)]
    items.append((k.qkvS[:, 0:2 * G, :].rearrange("p f n -> p (f n)"), [(0, 256, True), (256, 256, False)]))
    with nc.Block() as block:
        @block.scalar
        def _(act):
            def square(n):
                if n >= 4:
                    act.wait_ge(summed, n - 3)
                act.activation(sq[n % 4], items[n][0], ACT.Square).then_inc(squared, 1)

            act.wait_ge(ready, 1)
            square(0)
            square(1)
            for n, (src, parts) in enumerate(items):
                if n + 2 < len(items):
                    square(n + 2)
                act.wait_ge(summed, n + 1)
                if n >= 4:
                    act.wait_ge(inverted, n - 3)
                for c, w, is_q in parts:
                    last = act.activation(root[n % 4][:, c:c + w], k.psum[n % 4][:, c:c + w], ACT.Sqrt,
                                          scale=float(DK) if is_q else 1.0, bias=q_eps if is_q else k.eps)
                last.then_inc(rooted, 1)

        @block.tensor
        def _(pe):
            for n in range(len(items)):
                pe.wait_ge(squared, n + 1)
                if n >= 4:
                    pe.wait_ge(rooted, n - 3)
                pe.matmul(k.psum[n % 4][:, :], k.c["ones"], sq[n % 4], start=True, stop=True).then_inc(summed, 1)

        @block.vector
        def _(dve):
            dve.memset(q_eps, EPS * DK).then_inc(ready, 1)
            for n, (src, parts) in enumerate(items):
                dve.wait_ge(rooted, n + 1)
                dve.reciprocal(inv[n % 2], root[n % 4]).then_inc(inverted, 1)
                dve.wait_ge(inverted, n + 1)
                dve.tensor_tensor(src, src, inv[n % 2], ALU.mult)


def stage_gates(k):
    nc = k.nc
    m = Map(k.gdn_at)
    k.AQ = [k.view(m.take(512), G, P) for _ in range(NT + 1)]
    k.KD = [k.view(m.take(512), G, P) for _ in range(NT + 1)]
    k.uS = k.view(m.take(512), G, P)
    n = (NT + 1) * G
    k.decay_sum, k.gcb, k.ngc, k.egc, k.ebc, k.ekd, k.egl, k.gl, k.t1 = (k.view(m.take(n), NT + 1, G) for _ in range(9))
    k.gb = k.view(m.take(DB * G), DB, G)
    k.eglS = k.view(m.take(DB * G), DB * G)
    k.temp_at = (m.take(8 * 512), k.hT_at)
    k.sc_spare = m.take(3 * 512 + 3 * n)
    assert m.at <= k.words, m.at
    g, beta, lnb = (k.gates[:, i, :].rearrange("p (t h) -> p t h", h=G) for i in range(3))
    summed, base, diff, done = k.sem("gt_summed"), k.sem("gt_base"), k.sem("gt_diff"), k.sem("gt_exp")
    np_ = NT * G
    flat = lambda x: x.rearrange("p t h -> p (t h)")
    with nc.Block() as block:
        @block.tensor
        def _(pe):
            gf = flat(g)
            pe.matmul(k.psum[0][:, 0:np_], k.c["tri"], gf[:, 0:np_], start=True, stop=True)
            pe.matmul(k.psum[0][:, np_:n], k.c["tri_s"], gf[:, np_:n], start=True, stop=True)
            pe.matmul(k.psum[1][:, 0:np_], k.c["ones"], gf[:, 0:np_], start=True, stop=True)
            pe.matmul(k.psum[1][:, np_:n], k.c["block_s"], gf[:, np_:n], start=True, stop=True)
            pe.wait_ge(base, 1)
            pe.matmul(k.psum[2][:, 0:DB * G], k.c["ones"][0:NS, :], k.gb[0:NS].rearrange("p b h -> p (b h)"), start=True, stop=True).then_inc(summed, 1)

        @block.vector
        def _(dve):
            dve.tensor_tensor(k.gb[0:NS], k.c["in_batch"][0:NS].unsqueeze(2).to_broadcast([NS, DB, G]),
                              g[0:NS, NT:NT + 1, :].to_broadcast([NS, DB, G]), ALU.mult).then_inc(base, 1)
            dve.wait_ge(summed, 1)
            dve.tensor_copy(flat(k.decay_sum), k.psum[0][:, 0:n]).then_inc(base, 1)
            dve.tensor_copy(flat(k.gl), k.psum[1][:, 0:n]).then_inc(base, 1)
            dve.wait_ge(base, 3)
            dve.tensor_tensor(flat(k.gcb), flat(k.decay_sum), flat(lnb), ALU.add).then_inc(diff, 1)
            dve.tensor_scalar(flat(k.ngc), flat(k.decay_sum), -1.0, None, ALU.mult).then_inc(diff, 1)
            dve.tensor_tensor(flat(k.t1), flat(k.gl), flat(k.decay_sum), ALU.subtract).then_inc(diff, 1)
            dve.wait_ge(done, 1)
            dve.tensor_tensor(flat(k.ebc), flat(k.egc), flat(beta), ALU.mult)

        @block.scalar
        def _(act):
            act.wait_ge(diff, 3)
            act.activation(flat(k.egc), flat(k.decay_sum), ACT.Exp).then_inc(done, 1)
            act.activation(flat(k.egl), flat(k.gl), ACT.Exp)
            act.activation(flat(k.ekd), flat(k.t1), ACT.Exp)
            act.activation(k.eglS, k.psum[2][:, 0:DB * G], ACT.Exp)


PAIRS = [(0, 1), (2, 3), (4, 5), (6, 7), (8,)]


def stage_chunks(k):
    nc = k.nc
    S = 2
    t_at = [Map(at) for at in k.temp_at]
    kbe, vb, Lm, X, TG = ([k.view(m.take(512), G, P) for m in t_at] for _ in range(5))
    ZM = [k.view(m.take(1024), 2 * G, P) for m in t_at]
    beta = k.gates[:, 1, :].rearrange("p (t h) -> p t h", h=G)
    g = k.gates[:, 0, :].rearrange("p (t h) -> p t h", h=G)
    names = ("spread", "turned", "decay", "kept", "gram", "built", "init", "x_made", "masked", "y_made", "grown", "solved", "left")
    (spread, turned, decay, kept, gram, built, init, x_made, masked, y_made, grown, solved, left) = (k.sems("ch_" + n, S) for n in names)
    decayed = k.sems("ch_decayed", S)
    levels = lambda t: LEVELS if t < NT else S_LEVELS
    steps = LEVELS

    def bank(s, i, r):
        return k.psum[4 * s + i].rearrange("p (h n) -> p h n", h=G)[0:r, :, 0:r]

    with nc.Block() as block:
        @block.tensor
        def _(pe):
            for i, pair in enumerate(PAIRS):
                for s, t in enumerate(pair):
                    r = rows_of(t)
                    if i:
                        pe.wait_ge(left[s], 2 * i)
                    for part, b in ((1, 0), (2, 1)):
                        for h in range(G):
                            last = pe.transpose(k.psum[4 * s + b][0:r, h * P:(h + 1) * P], gdn_view(k, t, part)[:, h, :], k.c["ident"])
                    last.then_inc(turned[s], 1)
                    pe.wait_ge(spread[s], i + 1)
                    for b, mask in ((2, "low_big"), (3, "up_big")):
                        mask = k.b[mask if t < NT else mask + "_s"][0:r, 0:r].unsqueeze(1).to_broadcast([r, G, r])
                        pe.matmul(bank(s, b, r), k.c["ones"][0:r, 0:r], TG[s][0:r, :, 0:r], start=True, stop=False)
                        last = pe.matmul(bank(s, b, r), k.b["ident"][0:r, 0:r], mask, start=False, stop=True)
                    last.then_inc(decay[s], 1)
                for s, t in enumerate(pair):
                    r = rows_of(t)
                    pe.wait_ge(kept[s], i + 1)
                    kT, qT = gdn_view(k, t, 1), gdn_view(k, t, 0)
                    for h in range(G):
                        pe.matmul(bank(s, 0, r)[:, h, :], kT[:, h, :], kT[:, h, :], start=True, stop=True)
                    for h in range(G):
                        last = pe.matmul(bank(s, 1, r)[:, h, :], kT[:, h, :], qT[:, h, :], start=True, stop=True)
                    last.then_inc(gram[s], 1)
                for l in range(steps):
                    for s, t in enumerate(pair):
                        if l >= levels(t):
                            continue
                        r = rows_of(t)
                        if l == 0:
                            pe.wait_ge(built[s], i + 1)
                            pe.wait_ge(init[s], i + 1)
                        else:
                            pe.wait_ge(grown[s], LEVELS * i + l)
                        for h in range(G):
                            last = pe.matmul(bank(s, 2, r)[:, h, :], Lm[s][0:r, h, 0:r], ZM[s][0:r, h, 0:r], start=True, stop=True)
                        last.then_inc(x_made[s], 1)
                    for s, t in enumerate(pair):
                        if l >= levels(t):
                            continue
                        r = rows_of(t)
                        pe.wait_ge(masked[s], LEVELS * i + l + 1)
                        for h in range(G):
                            last = pe.matmul(bank(s, 0, r)[:, h, :], ZM[s][0:r, G + h, 0:r], X[s][0:r, h, 0:r], start=True, stop=True)
                        if l < levels(t) - 1:
                            for h in range(G):
                                last = pe.matmul(bank(s, 1, r)[:, h, :], X[s][0:r, h, 0:r], ZM[s][0:r, G + h, 0:r], start=True, stop=True)
                        last.then_inc(y_made[s], 1)
                for s, t in enumerate(pair):
                    r = rows_of(t)
                    pe.wait_ge(grown[s], LEVELS * i + levels(t))
                    for h in range(G):
                        pe.matmul(k.psum[4 * s + 2][0:r, h * P:(h + 1) * P], ZM[s][0:r, h, 0:r], vb[s][0:r, h, :], start=True, stop=True)
                    for h in range(G):
                        last = pe.matmul(k.psum[4 * s + 3][:, h * P:h * P + r], kbe[s][0:r, h, :], ZM[s][0:r, h, 0:r], start=True, stop=True)
                    last.then_inc(solved[s], 1)

        @block.scalar
        def _(act):
            for i, pair in enumerate(PAIRS):
                for s, t in enumerate(pair):
                    r = rows_of(t)
                    act.wait_ge(decay[s], i + 1)
                    for h in range(G):
                        act.activation(Lm[s][0:r, h, 0:r], bank(s, 2, r)[:, h, :], ACT.Exp, scale=-1.0, bias=k.gcb[0:r, t, h:h + 1])
                        last = act.activation(k.AQ[t][0:r, h, 0:r], bank(s, 3, r)[:, h, :], ACT.Exp, bias=k.ngc[0:r, t, h:h + 1])
                    last.then_inc(decayed[s], 1)
                for s, t in enumerate(pair):
                    r = rows_of(t)
                    act.wait_ge(solved[s], i + 1)
                    u = k.uS[0:NS] if t == NT else gdn_view(k, t, 2)
                    act.copy(u, k.psum[4 * s + 2][0:r, :].rearrange("p (h n) -> p h n", h=G)).then_inc(left[s], 1)
                    act.copy(gdn_view(k, t, 1), k.psum[4 * s + 3][:, :].rearrange("p (h n) -> p h n", h=G)[:, :, 0:r]).then_inc(left[s], 1)

        @block.gpsimd
        def _(pool):
            for i, pair in enumerate(PAIRS):
                for s, t in enumerate(pair):
                    if i:
                        pool.wait_ge(solved[s], i)
                    pool.tensor_copy(ZM[s], k.c["ident"].unsqueeze(1).to_broadcast([P, 2 * G, P])).then_inc(init[s], 1)

        @block.vector
        def _(dve):
            for i, pair in enumerate(PAIRS):
                for s, t in enumerate(pair):
                    r = rows_of(t)
                    tri = k.c["tri" if t < NT else "tri_s"][0:r, 0:r].unsqueeze(1).to_broadcast([r, G, r])
                    if i:
                        dve.wait_ge(decay[s], i)
                    dve.tensor_tensor(TG[s][0:r, :, 0:r], tri, g[0:r, t, :].unsqueeze(2).to_broadcast([r, G, r]), ALU.mult).then_inc(spread[s], 1)
                for s, t in enumerate(pair):
                    r = rows_of(t)
                    wide = lambda x: x[0:r, t, :].unsqueeze(2).to_broadcast([r, G, P])
                    kk, vv = (k.psum[4 * s + b][0:r, :].rearrange("p (h n) -> p h n", h=G) for b in (0, 1))
                    dve.wait_ge(turned[s], i + 1)
                    if i:
                        dve.wait_ge(solved[s], i)
                    dve.tensor_tensor(kbe[s][0:r], kk, wide(k.ebc), ALU.mult)
                    dve.tensor_tensor(k.KD[t][0:r], kk, wide(k.ekd), ALU.mult)
                    dve.tensor_tensor(vb[s][0:r], vv, wide(beta), ALU.mult).then_inc(kept[s], 1)
                for s, t in enumerate(pair):
                    r = rows_of(t)
                    dve.wait_ge(gram[s], i + 1)
                    dve.wait_ge(decayed[s], i + 1)
                    L, A = Lm[s][0:r, :, 0:r], k.AQ[t][0:r, :, 0:r]
                    dve.tensor_tensor(L, bank(s, 0, r), L, ALU.mult)
                    dve.tensor_tensor(A, bank(s, 1, r), A, ALU.mult).then_inc(built[s], 1)
                for l in range(steps):
                    for s, t in enumerate(pair):
                        if l >= levels(t):
                            continue
                        r = rows_of(t)
                        dve.wait_ge(x_made[s], LEVELS * i + l + 1)
                        mask = k.b["level"][0:r, l * P:l * P + r].unsqueeze(1).to_broadcast([r, G, r])
                        dve.tensor_tensor(X[s][0:r, :, 0:r], bank(s, 2, r), mask, ALU.mult).then_inc(masked[s], 1)
                    for s, t in enumerate(pair):
                        if l >= levels(t):
                            continue
                        r = rows_of(t)
                        n = G if l == levels(t) - 1 else 2 * G
                        dve.wait_ge(y_made[s], LEVELS * i + l + 1)
                        if l == 0:
                            dve.wait_ge(init[s], i + 1)
                        zm = ZM[s][0:r, 0:n, 0:r]
                        y = k.banks[0:r, 4 * s * 512:4 * s * 512 + n * P].rearrange("p (h n) -> p h n", h=n)[:, :, 0:r]
                        dve.tensor_tensor(zm, zm, y, ALU.add).then_inc(grown[s], 1)


def stage_scan(k):
    nc, a = k.nc, k.a
    mix = k.view(k.hT_at, KD, TOK)
    z = k.view(k.z_at, NT, G, DK)
    zS = k.psZ[0:NS, :].rearrange("p (h d) -> p h d", h=G)
    m = Map(k.temp_at[0])
    S0 = k.view(m.take(DB * G * DK), DB * G, DK)
    m = Map(k.temp_at[1])
    S = [k.view(m.take(512), G, DK) for _ in range(2)]
    vnew = [k.view(m.take(512), G, DK) for _ in range(2)]
    o = [k.view(m.take(512), G, DK) for _ in range(2)]
    sq = k.view(m.take(512), G, DK)
    m = Map(k.temp_at[1])
    wTm = k.view(m.take(G * DB * NS), G, DB * NS)
    qTm = k.view(m.take(G * DB * NS), G, DB * NS)
    vnm = k.view(k.temp_at[1], G, DB * DK)
    m = Map(k.sc_spare)
    vS, oS, sqS = (k.view(m.take(512), G, DK) for _ in range(3))
    stat = k.view(m.take(3 * G * (NT + 1)), 3, (NT + 1) * G)
    fade, fadeS = k.sem("sc_fade"), k.sem("sc_fadeS")
    names = ("ws", "qs", "vnew", "av", "kv", "state", "scaled", "out", "sq", "sum", "root", "inv", "norm", "gated", "turned", "kept")
    (ws, qs, vn, av, kv, state, faded, outs, sqd, sm, root, inv, normed, gated, turned, kept) = (k.sem("sc_" + n) for n in names)
    landed, out_sem = k.sem("sc_landed"), k.stored["ssm"]
    mask_sem, vm_sem, kvS, addS = k.sem("sc_mask"), k.sem("sc_vmask"), k.sem("sc_kvS"), k.sem("sc_addS")
    heads = lambda b: b.rearrange("p (h n) -> p h n", h=G)
    n_all = NT + 1
    with nc.Block() as block:
        @block.sync
        def _(sp):
            sp.dma_start(S0, a["state_ssm"][0].rearrange("b h k v -> k (b h) v")).then_inc(landed, 16)
            sp.wait_ge(state, NT + 1)
            sp.dma_start(a["new_ssm_prompt"][0, 0].rearrange("h k v -> k h v"), S[NT % 2]).then_inc(out_sem, 16)
            sp.wait_ge(addS, 2 * G)
            sp.dma_start(a["new_ssm_sample"][0].rearrange("b h k v -> k (b h) v"), S0).then_inc(out_sem, 16)
            sp.wait_ge(out_sem, 32)

        @block.tensor
        def _(pe):
            def turn(t):
                r = rows_of(t)
                src = o[t % 2] if t < NT else oS
                pe.wait_ge(gated, t + 1)
                if t:
                    pe.wait_ge(kept, t)
                for h in range(G):
                    last = pe.transpose(k.psum[7][:, h * P:h * P + r], src[0:r, h, :], k.c["ident"][0:r, 0:r])
                last.then_inc(turned, 1)

            for t in range(NT):
                pe.wait_ge(state, t + 1)
                for h in range(G):
                    last = pe.matmul(heads(k.psum[0])[:, h, :], gdn_view(k, t, 1)[:, h, :], S[t % 2][:, h, :], start=True, stop=True)
                last.then_inc(ws, 1)
                if t:
                    pe.wait_ge(outs, t)
                for h in range(G):
                    last = pe.matmul(heads(k.psum[1])[:, h, :], gdn_view(k, t, 0)[:, h, :], S[t % 2][:, h, :], start=True, stop=True)
                last.then_inc(qs, 1)
                pe.wait_ge(vn, t + 1)
                for h in range(G):
                    last = pe.matmul(heads(k.psum[2])[:, h, :], k.KD[t][:, h, :], vnew[t % 2][:, h, :], start=True, stop=True)
                last.then_inc(kv, 1)
                for h in range(G):
                    last = pe.matmul(heads(k.psum[3])[:, h, :], k.AQ[t][:, h, :], vnew[t % 2][:, h, :], start=True, stop=True)
                last.then_inc(av, 1)
                if t:
                    turn(t - 1)
            turn(NT - 1)
            pe.wait_ge(landed, 16)
            pe.wait_ge(mask_sem, 1)
            for src, b0, sem in ((wTm, 4, ws), (qTm, 5, qs)):
                for h in range(G):
                    for b in range(DB):
                        last = pe.matmul(k.psum[b0][0:NS, h * DK:(h + 1) * DK], src[:, h, b * NS:(b + 1) * NS], S0[:, b * G + h, :],
                                         start=(b == 0), stop=(b == DB - 1))
                last.then_inc(sem, 1)
            pe.wait_ge(vn, NT + 1)
            for h in range(G):
                last = pe.matmul(k.psum[6][0:NS, h * DK:(h + 1) * DK], k.AQ[NT][0:NS, h, 0:NS], vS[0:NS, h, :], start=True, stop=True)
            last.then_inc(av, 1)
            pe.wait_ge(vm_sem, 1)
            for n in range(2 * G):
                h, half = n // 2, n % 2
                if n >= 4:
                    pe.wait_ge(addS, n - 3)
                pe.matmul(k.psum[n % 4][:, :], k.KD[NT][0:NS, h, :], vnm[0:NS, h, half * 512:(half + 1) * 512],
                          start=True, stop=True).then_inc(kvS, 1)
            turn(NT)

        @block.scalar
        def _(act):
            for t in range(n_all):
                r = rows_of(t)
                act.wait_ge(sm, t + 1)
                act.activation(stat[0:r, 1, t * G:(t + 1) * G], stat[0:r, 0, t * G:(t + 1) * G], ACT.Sqrt, scale=1.0 / DK, bias=k.eps[0:r, :]).then_inc(root, 1)
                act.wait_ge(turned, t + 1)
                act.copy(mix[:, KD // 2:KD, t * P:t * P + r], heads(k.psum[7])[:, :, 0:r]).then_inc(kept, 1)

        @block.vector
        def _(dve):
            def output(t, q_bank, a_bank, out, sqr, zz):
                r = rows_of(t)
                wide = lambda x: x.unsqueeze(2).to_broadcast([r, G, DK])
                dve.wait_ge(qs, t + 1)
                if 2 <= t < NT:
                    dve.wait_ge(turned, t - 1)
                dve.tensor_tensor(out, heads(k.psum[q_bank])[0:r], wide(k.egc[0:r, t, :]), ALU.mult).then_inc(faded, 1)
                dve.wait_ge(av, t + 1)
                dve.wait_ge(faded, t + 1)
                dve.tensor_tensor(out, out, heads(k.psum[a_bank])[0:r], ALU.add).then_inc(outs, 1)
                dve.wait_ge(outs, t + 1)
                if t:
                    dve.wait_ge(sm, t)
                dve.tensor_tensor(sqr, out, out, ALU.mult).then_inc(sqd, 1)
                dve.wait_ge(sqd, t + 1)
                dve.reduce_sum(stat[0:r, 0, t * G:(t + 1) * G], sqr, AX_X).then_inc(sm, 1)
                dve.tensor_tensor(out, out, zz, ALU.mult).then_inc(normed, 1)
                dve.wait_ge(root, t + 1)
                dve.reciprocal(stat[0:r, 2, t * G:(t + 1) * G], stat[0:r, 1, t * G:(t + 1) * G]).then_inc(inv, 1)
                dve.wait_ge(inv, t + 1)
                dve.wait_ge(normed, t + 1)
                dve.tensor_tensor(out, out, wide(stat[0:r, 2, t * G:(t + 1) * G]), ALU.mult).then_inc(gated, 1)

            dve.memset(S[0], 0.0).then_inc(state, 1)
            for t in range(NT):
                old, new = S[t % 2], S[(t + 1) % 2]
                dve.wait_ge(state, t + 1)
                dve.tensor_tensor(new, old, k.egl[:, t, :].unsqueeze(2).to_broadcast([P, G, DK]), ALU.mult).then_inc(fade, 1)
                dve.wait_ge(ws, t + 1)
                if t >= 2:
                    dve.wait_ge(av, t - 1)
                dve.tensor_tensor(vnew[t % 2], gdn_view(k, t, 2), heads(k.psum[0]), ALU.subtract).then_inc(vn, 1)
                dve.wait_ge(kv, t + 1)
                dve.wait_ge(fade, t + 1)
                dve.tensor_tensor(new, new, heads(k.psum[2]), ALU.add).then_inc(state, 1)
                output(t, 1, 3, o[t % 2], sq, z[:, t])
            dve.wait_ge(turned, NT)
            dve.wait_ge(out_sem, 16)
            cm = k.b["columns"].rearrange("p (b n) -> p b n", b=DB)
            for h in range(G):
                for dst, part in ((wTm, 1), (qTm, 0)):
                    last = dve.tensor_tensor(dst[:, h, :].rearrange("p (b n) -> p b n", b=DB), cm,
                                             gdn_view(k, NT, part)[:, h, :].unsqueeze(1).to_broadcast([P, DB, NS]), ALU.mult)
            last.then_inc(mask_sem, 1)
            dve.wait_ge(ws, NT + 1)
            dve.tensor_tensor(vS[0:NS], k.uS[0:NS], heads(k.psum[4])[0:NS], ALU.subtract).then_inc(vn, 1)
            dve.wait_ge(vn, NT + 1)
            dve.wait_ge(qs, NT + 1)
            for h in range(G):
                last = dve.tensor_tensor(vnm[0:NS, h, :].rearrange("p (b d) -> p b d", b=DB),
                                         vS[0:NS, h, :].unsqueeze(1).to_broadcast([NS, DB, DK]),
                                         k.c["in_batch"][0:NS].unsqueeze(2).to_broadcast([NS, DB, DK]), ALU.mult)
            last.then_inc(vm_sem, 1)
            output(NT, 5, 6, oS[0:NS], sqS[0:NS], zS)
            S0v = S0.rearrange("p (b h) v -> p b h v", h=G)
            eg = k.eglS.rearrange("p (b h) -> p b h", h=G)
            for n in range(2 * G):
                h, half = n // 2, n % 2
                part = S0v[:, 4 * half:4 * half + 4, h, :]
                dve.wait_ge(kvS, n + 1)
                dve.tensor_tensor(part, part, eg[:, 4 * half:4 * half + 4, h].unsqueeze(2).to_broadcast([P, 4, DK]), ALU.mult).then_inc(fadeS, 1)
                dve.wait_ge(fadeS, n + 1)
                dve.tensor_tensor(part, part, k.psum[n % 4].rearrange("p (b v) -> p b v", b=4), ALU.add).then_inc(addS, 1)


def stage_prompt_attention(k):
    nc, a = k.nc, k.a
    m = Map(k.xc_at)
    qT, kT = (k.view(m.take(4 * SEQ), 4, SEQ) for _ in range(2))
    V = k.view(m.take(NT * AW), NT, AW)
    m = Map(k.z_at)
    prob = [k.view(m.take(SEQ), SEQ) for _ in range(2)]
    probT = [k.view(m.take(SEQ), SEQ) for _ in range(2)]
    m = Map(k.free_at)
    stat = k.view(m.take(3 * NT * H), 3, NT * H)
    mix = k.view(k.hT_at, KD, TOK)
    items = [(t, h) for t in range(NT) for h in range(H)]
    q_in, k_in, v_in = k.sem("pa_q_landed"), k.sem("pa_k_landed"), k.sem("pa_v_landed")
    names = ("q_scaled", "scores", "max", "exp", "inv", "scaled", "turned", "kept", "made", "out")
    q_scaled, scores, maxed, exped, inverted, scaled, turned, kept, made, out = (k.sem("pa_" + n) for n in names)
    n_items = len(items)
    with nc.Block() as block:
        @block.sync
        def _(sp):
            sp.dma_start(qT, a["q_T"].rearrange("(f p) n -> p f n", p=P)).then_inc(q_in, 16)
            sp.dma_start(kT, a["k_T"].rearrange("(f p) n -> p f n", p=P)).then_inc(k_in, 16)
            sp.dma_start(V, a["new_v_prompt"][0, 0].rearrange("t h d -> t (h d)").rearrange("(t p) n -> p t n", p=P)).then_inc(v_in, 16)

        @block.gpsimd
        def _(pool):
            pool.wait_ge(q_in, 16)
            for f in range(4):
                pool.tensor_scalar(qT[:, f, :], qT[:, f, :], HD ** -0.5, None, ALU.mult).then_inc(q_scaled, 1)

        @block.tensor
        def _(pe):
            def score(n):
                t, h = items[n]
                lo = (h % 2) * HD
                if n >= 2:
                    pe.wait_ge(exped, n - 1)
                for c in range(0, (t + 1) * P, 512):
                    w = min(512, (t + 1) * P - c)
                    bank = k.psum[2 * (n % 2) + c // 512]
                    pe.matmul(bank[:, 0:w], qT[lo:lo + HD, h // 2, t * P:(t + 1) * P], kT[lo:lo + HD, h // 2, c:c + w], start=True, stop=False)
                    if t < FIRST_SEL:
                        last = pe.matmul(bank[:, t * P:(t + 1) * P], k.b["ident"], k.b["attn_causal"], start=False, stop=True)
                    else:
                        last = pe.matmul(bank[:, 0:w], k.b["ident"], k.maskP[t][:, c:c + w], start=False, stop=True)
                last.then_inc(scores, 1)

            def values(n):
                t, h = items[n]
                lo = (h % 2) * HD
                pe.wait_ge(scaled, n + 1)
                if n:
                    pe.wait_ge(kept, n)
                for j in range(t + 1):
                    last = pe.transpose(k.psum[4 + j // 4][:, (j % 4) * P:(j % 4 + 1) * P], prob[n % 2][:, j * P:(j + 1) * P], k.c["ident"])
                last.then_inc(turned, 1)
                pe.wait_ge(kept, n + 1)
                if n >= 2:
                    pe.wait_ge(out, n - 1)
                for j in range(t + 1):
                    last = pe.matmul(k.psum[6 + n % 2][lo:lo + HD, 0:P], V[:, j, h * HD:(h + 1) * HD], probT[n % 2][:, j * P:(j + 1) * P],
                                     start=(j == 0), stop=(j == t))
                last.then_inc(made, 1)

            pe.wait_ge(q_scaled, 4)
            pe.wait_ge(k_in, 16)
            score(0)
            pe.wait_ge(v_in, 16)
            for n in range(n_items):
                if n + 1 < n_items:
                    score(n + 1)
                values(n)

        @block.scalar
        def _(act):
            def exps(n):
                t, h = items[n]
                w = (t + 1) * P
                b0 = 2 * (n % 2) * 512
                act.wait_ge(maxed, n + 1)
                if n >= 2:
                    act.wait_ge(turned, n - 1)
                act.activation(prob[n % 2][:, 0:w], k.banks[:, b0:b0 + w], ACT.Exp, bias=stat[:, 0, n:n + 1],
                               accum_out=stat[:, 1, n:n + 1]).then_inc(exped, 1)

            exps(0)
            for n in range(n_items):
                if n + 1 < n_items:
                    exps(n + 1)
                w = (items[n][0] + 1) * P
                act.wait_ge(turned, n + 1)
                if n >= 2:
                    act.wait_ge(made, n - 1)
                act.copy(probT[n % 2][:, 0:w], k.banks[:, 4 * 512:4 * 512 + w]).then_inc(kept, 1)

        @block.vector
        def _(dve):
            def maxes(n):
                w = (items[n][0] + 1) * P
                b0 = 2 * (n % 2) * 512
                dve.wait_ge(scores, n + 1)
                dve.tensor_reduce(stat[:, 0, n:n + 1], k.banks[:, b0:b0 + w], AX_X, ALU.max, negate=True).then_inc(maxed, 1)

            def keep(n):
                t, h = items[n]
                lo = (h % 2) * HD
                dve.wait_ge(made, n + 1)
                dve.tensor_copy(mix[lo:lo + HD, h // 2, t * P:(t + 1) * P], k.psum[6 + n % 2][lo:lo + HD, 0:P]).then_inc(out, 1)

            maxes(0)
            for n in range(n_items):
                if n + 1 < n_items:
                    maxes(n + 1)
                w = (items[n][0] + 1) * P
                dve.wait_ge(exped, n + 1)
                dve.reciprocal(stat[:, 2, n:n + 1], stat[:, 1, n:n + 1]).then_inc(inverted, 1)
                dve.wait_ge(inverted, n + 1)
                dve.tensor_scalar(prob[n % 2][:, 0:w], prob[n % 2][:, 0:w], stat[:, 2, n:n + 1], None, ALU.mult).then_inc(scaled, 1)
                if n:
                    keep(n - 1)
            keep(n_items - 1)


def stage_sample_attention(k):
    nc, a = k.nc, k.a
    IT = DB // 2
    NCH = NPG // 4
    m = Map(k.xc_at)
    kp = [k.view(m.take(4 * AW), 4, AW) for _ in range(3)]
    vp = [k.view(m.take(4 * AW), 4, AW) for _ in range(3)]
    kts = [k.view(m.take(4 * 512), 4, 512) for _ in range(2)]
    S = [k.view(m.take(LS), LS) for _ in range(2)]
    PT = k.view(m.take((NPG + 1) * P), NPG + 1, P)
    qblk = k.view(m.take(DB * 4 * 64), DB * 4, 64)
    ktn = k.view(m.take(4 * NS), 4, NS)
    osb = k.view(m.take(512), 512)
    stat = k.view(m.take(3 * IT), 3, IT)
    assert m.at <= k.words
    mix = k.view(k.hT_at, KD, TOK)
    kl, vl = k.sems("sa_k_landed", 3), k.sems("sa_v_landed", 3)
    names = ("zero", "prep_pe", "prep", "k_turned", "kept_act", "kept_dve", "qk", "scores", "copied", "max", "exp", "inv",
             "scaled", "p_turned", "p_kept", "v_used", "out", "out_kept", "o_turned", "laid")
    (zero, prep_pe, prep, k_turned, kept_a, kept_v, qk, scores, copied, maxed, exped, inverted, scaled, p_turned,
     p_kept, v_used, out, out_kept, o_turned, laid) = (k.sem("sa_" + n) for n in names)
    loads = [(it, c, b2) for it in range(IT) for c in range(NCH) for b2 in range(2)]
    PG = NCH + 1

    def load(q, cache, ring, sem, used):
        for n, (it, c, b2) in enumerate(loads):
            if n >= 3:
                q.wait_ge(used, used_at(n - 3, used))
            for p in range(4):
                at = (2 * it + b2) * NPG + 4 * c + p
                page = q.value_load(k.table[0:1, at:at + 1], min_val=0, max_val=cache.shape[1] - 1)
                src = cache[0, bass.ds(page, 1), :, :, :].rearrange("a p h d -> p (a h d)")
                q.dma_start(ring[n % 3][:, p, :], src).then_inc(sem[n % 3], 16)

    def used_at(n, used):
        return 4 * (n + 1) if used is k_turned else n + 1

    with nc.Block() as block:
        @block.sync
        def _(sp):
            load(sp, a["cache_k"], kp, kl, k_turned)

        @block.gpsimd
        def _(pool):
            pool.memset(qblk, 0.0).then_inc(zero, 1)
            load(pool, a["cache_v"], vp, vl, v_used)

        @block.tensor
        def _(pe):
            for p in range(4):
                pe.transpose(k.psum[6][:, p * NS:(p + 1) * NS], k.psA[0:NS, p * P:(p + 1) * P], k.c["ident"][0:NS, 0:NS])
            for p in range(4):
                last = pe.transpose(k.psum[7][:, p * NS:(p + 1) * NS], k.psA[0:NS, AW + p * P:AW + (p + 1) * P], k.c["ident"][0:NS, 0:NS])
            last.then_inc(prep_pe, 1)
            pe.wait_ge(prep, 9)

            def turn(n):
                pe.wait_ge(kl[n % 3], 64 * (n // 3 + 1))
                for p in range(4):
                    if n:
                        pe.wait_ge((kept_a, kept_v)[p % 2], 2 * (n - 1) + p // 2 + 1)
                    if p == 3 and loads[n][0] >= 2 and loads[n][1:] == (0, 0):
                        pe.wait_ge(p_kept, PG * (loads[n][0] - 1))
                    for j in range(4):
                        last = pe.transpose(k.psum[p][:, j * PAGE:(j + 1) * PAGE], kp[n % 3][:, j, p * P:(p + 1) * P], k.c["ident"])
                    last.then_inc(k_turned, 1)

            def mask_rows(it, b2):
                at = it * P + b2 * 64
                return k.b["sel_at"][0:NS, at:at + 64]

            def product(n):
                it, c, b2 = loads[n]
                i = it * (NCH + 1) + c
                bank = k.psum[4 + i % 2]
                pe.wait_ge(kept_a, 2 * (n + 1))
                pe.wait_ge(kept_v, 2 * (n + 1))
                if b2 == 0 and i >= 2:
                    pe.wait_ge(copied, i - 1)
                rows = bank[b2 * 64:(b2 + 1) * 64, :]
                pe.matmul(rows, mask_rows(it, b2), k.maskS[0:NS, c * 512:(c + 1) * 512], start=True, stop=False)
                for p in range(4):
                    last = pe.matmul(rows, qblk[:, (2 * it + b2) * 4 + p, :], kts[n % 2][:, p, :], start=False, stop=(p == 3))
                last.then_inc(qk, 1)

            def new_keys(it):
                i = it * (NCH + 1) + NCH
                bank = k.psum[4 + i % 2]
                if i >= 2:
                    pe.wait_ge(copied, i - 1)
                for b2 in range(2):
                    rows = bank[b2 * 64:(b2 + 1) * 64, 0:NS]
                    pe.matmul(rows, mask_rows(it, b2), k.maskS[0:NS, PAST:LS], start=True, stop=False)
                    for p in range(4):
                        last = pe.matmul(rows, qblk[:, (2 * it + b2) * 4 + p, :], ktn[:, p, :], start=False, stop=(p == 3))
                last.then_inc(scores, 1)

            def keys(it):
                n0 = it * 2 * NCH
                turn(n0)
                for n in range(n0, n0 + 2 * NCH):
                    if n + 1 < n0 + 2 * NCH:
                        turn(n + 1)
                    product(n)
                new_keys(it)

            def values(it):
                pe.wait_ge(scaled, it + 1)
                for g in range(PG):
                    n = it * PG + g
                    bank = k.psum[7 if g % 2 == 0 else 3]
                    if n >= 2:
                        pe.wait_ge(p_kept, n - 1)
                    if g == 0 and it:
                        pe.wait_ge(laid, 8 * it)
                        pe.wait_ge(p_kept, n)
                    if g == 1:
                        pe.wait_ge(kept_v, 2 * min(2 * NCH * (it + 2), len(loads)))
                    for j in range(4 * g, min(4 * g + 4, NPG + 1)):
                        w = PAGE if j < NPG else NS
                        last = pe.transpose(bank[0:w, (j % 4) * P:(j % 4 + 1) * P], S[it % 2][:, j * P:j * P + w], k.c["ident"])
                    last.then_inc(p_turned, 1)
                pe.wait_ge(p_kept, PG * (it + 1))
                if it:
                    pe.wait_ge(out_kept, it)
                for c in range(NCH):
                    for b2 in range(2):
                        n = it * 2 * NCH + 2 * c + b2
                        pe.wait_ge(vl[n % 3], 64 * (n // 3 + 1))
                        for j in range(4):
                            last = pe.matmul(k.psum[6][b2 * 64:(b2 + 1) * 64, :], PT[:, 4 * c + j, b2 * 64:(b2 + 1) * 64], vp[n % 3][:, j, :],
                                             start=(c == 0 and j == 0), stop=False)
                        last.then_inc(v_used, 1)
                for b2 in range(2):
                    last = pe.matmul(k.psum[6][b2 * 64:(b2 + 1) * 64, :], PT[0:NS, NPG, b2 * 64:(b2 + 1) * 64], k.psA[0:NS, 2 * AW:3 * AW],
                                     start=False, stop=True)
                last.then_inc(out, 1)
                pe.wait_ge(out_kept, it + 1)
                for p in range(4):
                    last = pe.transpose(k.psum[7][:, p * P:(p + 1) * P], osb[:, p * P:(p + 1) * P], k.c["ident"])
                last.then_inc(o_turned, 1)

            keys(0)
            for it in range(IT):
                if it + 1 < IT:
                    keys(it + 1)
                values(it)

        def keep_keys(eng, copy, mine, sem, it, n):
            for p in mine:
                eng.wait_ge(k_turned, 4 * n + p + 1)
                if n >= 2:
                    eng.wait_ge(qk, n - 1)
                copy(kts[n % 2][:, p, :], k.psum[p][:, :]).then_inc(sem, 1)

        @block.scalar
        def _(act):
            def scores_out(it, c):
                i = it * (NCH + 1) + c
                if c < NCH:
                    act.wait_ge(qk, it * 2 * NCH + 2 * c + 2)
                else:
                    act.wait_ge(scores, it + 1)
                if it >= 2 and c == 0:
                    act.wait_ge(p_turned, PG * (it - 1))
                w = 512 if c < NCH else NS
                act.copy(S[it % 2][:, c * 512:c * 512 + w], k.psum[4 + i % 2][:, 0:w]).then_inc(copied, 1)

            def keys(it):
                n0 = it * 2 * NCH
                keep_keys(act, act.copy, (0, 2), kept_a, it, n0)
                for n in range(n0, n0 + 2 * NCH):
                    if n + 1 < n0 + 2 * NCH:
                        keep_keys(act, act.copy, (0, 2), kept_a, it, n + 1)
                    if n % 2:
                        scores_out(it, (n - n0) // 2)
                scores_out(it, NCH)

            keys(0)
            for it in range(IT):
                act.wait_ge(maxed, it + 1)
                act.activation(S[it % 2], S[it % 2], ACT.Exp, bias=stat[:, 0, it:it + 1], accum_out=stat[:, 1, it:it + 1]).then_inc(exped, 1)
                if it + 1 < IT:
                    keys(it + 1)
                act.wait_ge(out, it + 1)
                act.copy(osb, k.psum[6][:, :]).then_inc(out_kept, 1)

        @block.vector
        def _(dve):
            dve.wait_ge(prep_pe, 1)
            dve.wait_ge(zero, 1)
            for h in range(H):
                lo, p = (h % 2) * HD, h // 2
                dst = qblk.rearrange("d (b p) n -> d b p n", p=4)[lo:lo + HD, :, p, h * DS:(h + 1) * DS]
                dve.tensor_scalar(dst, k.psum[6][lo:lo + HD, p * NS:(p + 1) * NS].rearrange("d (b q) -> d b q", b=DB),
                                  HD ** -0.5, None, ALU.mult).then_inc(prep, 1)
            dve.tensor_copy(ktn.rearrange("p a n -> p (a n)"), k.psum[7][:, 0:4 * NS]).then_inc(prep, 1)

            def keys(it):
                for n in range(it * 2 * NCH, (it + 1) * 2 * NCH):
                    keep_keys(dve, dve.tensor_copy, (1, 3), kept_v, it, n)

            keys(0)
            for it in range(IT):
                dve.wait_ge(copied, (NCH + 1) * (it + 1))
                dve.tensor_reduce(stat[:, 0, it:it + 1], S[it % 2], AX_X, ALU.max, negate=True).then_inc(maxed, 1)
                dve.wait_ge(exped, it + 1)
                dve.reciprocal(stat[:, 2, it:it + 1], stat[:, 1, it:it + 1]).then_inc(inverted, 1)
                dve.wait_ge(inverted, it + 1)
                dve.tensor_scalar(S[it % 2], S[it % 2], stat[:, 2, it:it + 1], None, ALU.mult).then_inc(scaled, 1)
                if it + 1 < IT:
                    keys(it + 1)
                for g in range(PG):
                    n = it * PG + g
                    dve.wait_ge(p_turned, n + 1)
                    if g == 0 and it:
                        dve.wait_ge(out, it)
                    bank = k.psum[7 if g % 2 == 0 else 3]
                    if g < NCH:
                        dve.tensor_copy(PT[:, 4 * g:4 * g + 4, :].rearrange("p a n -> p (a n)"), bank[:, :]).then_inc(p_kept, 1)
                    else:
                        dve.tensor_copy(PT[0:NS, NPG, :], bank[0:NS, 0:P]).then_inc(p_kept, 1)
                dve.wait_ge(o_turned, it + 1)
                for h in range(H):
                    lo, p = (h % 2) * HD, h // 2
                    src = k.psum[7][lo:lo + HD, p * P:(p + 1) * P].rearrange("d (b n) -> d b n", b=2)[:, :, h * DS:(h + 1) * DS]
                    dst = mix[lo:lo + HD, p, SEQ + it * 2 * DS:SEQ + (it + 1) * 2 * DS].rearrange("d (b q) -> d b q", b=2)
                    dve.tensor_copy(dst, src).then_inc(laid, 1)


def stage_output_projection(k):
    nc, a = k.nc, k.a
    mix = k.view(k.hT_at, KD, TOK)
    m = Map(k.x2_at)
    x2 = k.view(m.take((NT + 1) * D), NT + 1, D)
    w = k.view(m.take(KD * D), KD, D)
    w_in = k.sems("op_w_landed", 2)
    made, added = k.sem("op_made"), k.sem("op_added")
    x_landed = k.sems("op_x_landed", 3)
    xp = a["x_prompt"][0].rearrange("(t p) d -> t p d", p=P)
    xs = a["x_sample"].rearrange("b t d -> (b t) d")
    x = [k.view(m.take(D), D) for _ in range(3)]
    wv = a["w_out"][0].rearrange("(k p) n -> p k n", p=P)
    with nc.Block() as block:
        @block.sync
        def _(sp):
            for i in range(2):
                sp.dma_start(w[:, :, i * 512:(i + 1) * 512], wv[:, :, i * 512:(i + 1) * 512]).then_inc(w_in[i], 16)
            for t in range(NT + 1):
                if t >= 3:
                    sp.wait_ge(added, 2 * (t - 2))
                sp.dma_start(x[t % 3][0:rows_of(t), :], xp[t] if t < NT else xs).then_inc(x_landed[t % 3], 16)

        @block.tensor
        def _(pe):
            for t in range(NT + 1):
                r = rows_of(t)
                for i in range(2):
                    n = 2 * t + i
                    if t == 0:
                        pe.wait_ge(w_in[i], 16)
                    if n >= 8:
                        pe.wait_ge(added, n - 7)
                    for f in range(KD):
                        last = pe.matmul(k.psum[n % 8][0:r, :], mix[:, f, t * P:t * P + r], w[:, f, i * 512:(i + 1) * 512],
                                         start=(f == 0), stop=(f == KD - 1))
                    last.then_inc(made, 1)

        @block.vector
        def _(dve):
            for t in range(NT + 1):
                r = rows_of(t)
                dve.wait_ge(x_landed[t % 3], 16 * (t // 3 + 1))
                for i in range(2):
                    n = 2 * t + i
                    dve.wait_ge(made, n + 1)
                    dve.tensor_tensor(x2[0:r, t, i * 512:(i + 1) * 512], k.psum[n % 8][0:r, :], x[t % 3][0:r, i * 512:(i + 1) * 512],
                                      ALU.add).then_inc(added, 1)


def stage_mlp(k):
    nc, a = k.nc, k.a
    E, FE = 8, FF // 8
    TF = FE // P
    hT = k.view(k.hT_at, KD, TOK)
    m = Map(k.x2_at)
    x2 = k.view(m.take((NT + 1) * D), NT + 1, D)
    up = [k.view(m.take(KD * FE), KD, FE) for _ in range(2)]
    down = [k.view(m.take(TF * D), TF, D) for _ in range(2)]
    hid = [k.view(m.take(TF * TOK), TF, TOK) for _ in range(2)]
    relu = [k.view(m.take(512), 512) for _ in range(3)]
    hidS = [k.view(m.take(FE), FE) for _ in range(2)]
    assert m.at <= k.words
    up_in, down_in = k.sems("ml_up_landed", 2), k.sems("ml_down_landed", 2)
    names = ("up", "relu", "square", "turned", "laid", "down", "added")
    upped, relued, squared, turned, laid, downed, added = (k.sem("ml_" + n) for n in names)
    wu = a["w_up"][0].rearrange("(k p) n -> p k n", p=P)
    wd = a["w_down"][0].rearrange("(k p) n -> p k n", p=P)
    jobs = [(f, j) for f in range(TF) for j in range(2)] + [(None, None)]
    NJ, ND = len(jobs), 2 * (NT + 1)
    with nc.Block() as block:
        @block.sync
        def _(sp):
            for e in range(E):
                if e >= 2:
                    sp.wait_ge(upped, NJ * (e - 1))
                sp.dma_start(up[e % 2], wu[:, :, e * FE:(e + 1) * FE]).then_inc(up_in[e % 2], 16)
                if e >= 2:
                    sp.wait_ge(downed, ND * (e - 1))
                sp.dma_start(down[e % 2], wd[:, e * TF:(e + 1) * TF, :]).then_inc(down_in[e % 2], 16)

        @block.tensor
        def _(pe):
            def ups(e):
                pe.wait_ge(up_in[e % 2], 16 * (e // 2 + 1))
                for i, (f, j) in enumerate(jobs):
                    n = e * NJ + i
                    if n >= 3:
                        pe.wait_ge(relued, n - 2)
                    bank = k.psum[n % 3]
                    for c in range(KD):
                        if f is None:
                            last = pe.matmul(bank[0:NS, :], hT[:, c, SEQ:TOK], up[e % 2][:, c, :], start=(c == 0), stop=(c == KD - 1))
                        else:
                            last = pe.matmul(bank[:, :], up[e % 2][:, c, f * P:(f + 1) * P], hT[:, c, j * 512:(j + 1) * 512],
                                             start=(c == 0), stop=(c == KD - 1))
                    last.then_inc(upped, 1)

            def downs(e):
                pe.wait_ge(squared, NJ * (e + 1))
                if e:
                    pe.wait_ge(laid, e)
                for f in range(TF):
                    last = pe.transpose(k.psum[3][:, f * NS:(f + 1) * NS], hidS[e % 2][0:NS, f * P:(f + 1) * P], k.c["ident"][0:NS, 0:NS])
                last.then_inc(turned, 1)
                pe.wait_ge(down_in[e % 2], 16 * (e // 2 + 1))
                for t in range(NT + 1):
                    r = rows_of(t)
                    if t == NT:
                        pe.wait_ge(laid, e + 1)
                    for i in range(2):
                        n = e * ND + 2 * t + i
                        if n >= 4:
                            pe.wait_ge(added, n - 3)
                        for f in range(TF):
                            last = pe.matmul(k.psum[4 + n % 4][0:r, :], hid[e % 2][:, f, t * P:t * P + r], down[e % 2][:, f, i * 512:(i + 1) * 512],
                                             start=(f == 0), stop=(f == TF - 1))
                        last.then_inc(downed, 1)

            ups(0)
            for e in range(E):
                if e + 1 < E:
                    ups(e + 1)
                downs(e)

        def lay(act, e):
            act.wait_ge(turned, e + 1)
            act.copy(hid[e % 2][:, :, SEQ:TOK], k.psum[3][:, 0:TF * NS].rearrange("p (f n) -> p f n", f=TF)).then_inc(laid, 1)

        @block.scalar
        def _(act):
            for n in range(E * NJ):
                e, (f, j) = n // NJ, jobs[n % NJ]
                r = NS if f is None else P
                act.wait_ge(upped, n + 1)
                if n >= 3:
                    act.wait_ge(squared, n - 2)
                act.activation(relu[n % 3][0:r, :], k.psum[n % 3][0:r, :], ACT.Relu).then_inc(relued, 1)
                if n % NJ == NJ - 1 and e:
                    lay(act, e - 1)
            lay(act, E - 1)

        @block.vector
        def _(dve):
            def squares(e):
                for i, (f, j) in enumerate(jobs):
                    n = e * NJ + i
                    dve.wait_ge(relued, n + 1)
                    if e >= 2 and i == 0:
                        dve.wait_ge(downed, ND * (e - 1))
                    if f is None:
                        r = relu[n % 3][0:NS, :]
                        if e >= 2:
                            dve.wait_ge(turned, e - 1)
                        dve.tensor_tensor(hidS[e % 2][0:NS, :], r, r, ALU.mult).then_inc(squared, 1)
                    else:
                        r = relu[n % 3]
                        dve.tensor_tensor(hid[e % 2][:, f, j * 512:(j + 1) * 512], r, r, ALU.mult).then_inc(squared, 1)

            squares(0)
            for e in range(E):
                if e + 1 < E:
                    squares(e + 1)
                for t in range(NT + 1):
                    r = rows_of(t)
                    for i in range(2):
                        n = e * ND + 2 * t + i
                        dve.wait_ge(downed, n + 1)
                        if e:
                            dve.wait_ge(added, n - ND + 1)
                        part = x2[0:r, t, i * 512:(i + 1) * 512]
                        dve.tensor_tensor(part, part, k.psum[4 + n % 4][0:r, :], ALU.add).then_inc(added, 1)


def stage_final(k):
    nc, a = k.nc, k.a
    m = Map(k.x2_at)
    x2 = k.view(m.take((NT + 1) * D), NT + 1, D)
    gain = k.view(m.take(D), D)
    junk = k.view(m.take(D), D)
    stat = k.view(m.take(3 * (NT + 1)), 3, NT + 1)
    landed, squared, rooted, inv, done = (k.sem("fn_" + n) for n in ("gain_landed", "squared", "rooted", "inv", "done"))
    out_sem = k.stored["y"]
    yp = a["y_prompt"][0].rearrange("(t p) d -> t p d", p=P)
    ys = a["y_sample"].rearrange("b t d -> (b t) d")
    n = NT + 1
    with nc.Block() as block:
        @block.sync
        def _(sp):
            sp.dma_start(gain, a["norm_final"].rearrange("(a n) -> a n", a=1).partition_broadcast(P).rearrange("p a n -> p (a n)")).then_inc(landed, 16)
            for t in range(n):
                r = rows_of(t)
                sp.wait_ge(done, t + 1)
                sp.dma_start(yp[t] if t < NT else ys, x2[0:r, t, :]).then_inc(out_sem, 16)
            sp.wait_ge(out_sem, 16 * n)

        @block.scalar
        def _(act):
            for t in range(n):
                r = rows_of(t)
                if t:
                    act.wait_ge(squared, t)
                act.activation(junk[0:r, :], x2[0:r, t, :], ACT.Square, accum_out=stat[0:r, 0, t:t + 1]).then_inc(squared, 1)
                act.wait_ge(squared, t + 1)
                act.activation(stat[0:r, 1, t:t + 1], stat[0:r, 0, t:t + 1], ACT.Sqrt, scale=1.0 / D, bias=k.eps[0:r, :]).then_inc(rooted, 1)

        @block.vector
        def _(dve):
            dve.wait_ge(landed, 16)
            for t in range(n):
                r = rows_of(t)
                dve.wait_ge(rooted, t + 1)
                dve.reciprocal(stat[0:r, 2, t:t + 1], stat[0:r, 1, t:t + 1]).then_inc(inv, 1)
                dve.wait_ge(inv, t + 1)
                dve.scalar_tensor_tensor(out=x2[0:r, t, :], in0=x2[0:r, t, :], scalar=stat[0:r, 2, t:t + 1], in1=gain[0:r, :],
                                         op0=ALU.mult, op1=ALU.mult).then_inc(done, 1)


_INS = ["x_prompt", "x_sample", "cache_k", "cache_v", "cache_kidx", "state_ssm", "state_conv", "page_table",
        "norm_mix", "w_in", "conv_w", "a_log", "dt_bias", "norm_gdn_out", "w_out", "norm_mlp", "w_up",
        "w_down", "norm_final"]
_OUTS = [("y_prompt", (1, SEQ, D)), ("y_sample", (DB, DS, D)),
         ("new_k_prompt", (1, 1, SEQ, H, HD)), ("new_v_prompt", (1, 1, SEQ, H, HD)), ("new_kidx_prompt", (1, 1, SEQ, DI)),
         ("new_ssm_prompt", (1, 1, G, DK, DK)), ("new_conv_prompt", (1, 1, CW - 1, CC)),
         ("new_k_sample", (1, DB, DS, H, HD)), ("new_v_sample", (1, DB, DS, H, HD)), ("new_kidx_sample", (1, DB, DS, DI)),
         ("new_ssm_sample", (1, DB, G, DK, DK)), ("new_conv_sample", (1, DB, CW - 1, CC))]


def build_program(nc, a, stop=99):
    with ExitStack() as ctx:
        a["q_T"] = nc.dram_tensor("q_T", (AW, SEQ), F32, kind="Internal").ap()
        a["k_T"] = nc.dram_tensor("k_T", (AW, SEQ), F32, kind="Internal").ap()
        k = Kernel(nc, ctx, a)

        stages(k, stop)


def stages(k, stop):
    a = k.a
    stage_constants(k)
    x_ring = [k.view(k.xc_at + (t % 3) * D, D) for t in range(NT + 1)]
    xp = a["x_prompt"][0].rearrange("(t p) d -> t p d", p=P)
    xs = a["x_sample"].rearrange("b t d -> (b t) d")
    stage_norm(k, "mix", x_ring, k.hT_at, k.g_mix, lambda t: xp[t] if t < NT else xs)
    if stop < 1: return
    stage_indexer_projection(k)
    stage_prompt_scores(k)
    if stop < 2: return
    stage_sample_scores(k)
    if stop < 3: return
    stage_mixer_projection(k)
    if stop < 4: return
    stage_conv(k)
    if stop < 5: return
    stage_l2norm(k)
    stage_gates(k)
    if stop < 6: return
    k.stage_done()
    stage_chunks(k)
    if stop < 7: return
    stage_scan(k)
    if stop < 8: return
    stage_prompt_attention(k)
    if stop < 9: return
    stage_sample_attention(k)
    if stop < 10: return
    stage_output_projection(k)
    x2 = k.view(k.x2_at, NT + 1, D)
    stage_norm(k, "mlp", [x2[:, t, :] for t in range(NT + 1)], k.hT_at, k.g_mlp, None)
    if stop < 11: return
    stage_mlp(k)
    stage_final(k)


def kernel(**inputs):
    import concourse.bacc as bacc
    from concourse.bass_utils import run_bass_kernel_spmd

    nc = bacc.Bacc("TRN2", target_bir_lowering=False, num_devices=1)
    arrays, a = {}, {}
    for name in _INS:
        arrays["in_" + name] = np.ascontiguousarray(inputs[name])
    arrays["in_const"] = CONST
    for name, x in arrays.items():
        a[name[3:]] = nc.dram_tensor(name, x.shape, mybir.dt.from_np(x.dtype), kind="ExternalInput").ap()
    for name, shape in _OUTS:
        a[name] = nc.dram_tensor("out_" + name, shape, F32, kind="ExternalOutput").ap()
    build_program(nc, a)
    r = run_bass_kernel_spmd(nc, [arrays], core_ids=[0])
    return tuple(r.results[0]["out_" + name] for name, _ in _OUTS)
```

```python
from contextlib import ExitStack

import numpy as np

import concourse.bass as bass
from concourse import mybir

F32 = mybir.dt.float32
F32R = mybir.dt.float32r
BF16 = mybir.dt.bfloat16
I32 = mybir.dt.int32
ALU = mybir.AluOpType
ACT = mybir.ActivationFunctionType
AX_X = mybir.AxisListType.X

P = 128
D = 1024
KD = D // P
SEQ = 1024
NT = SEQ // P
DB, DS = 8, 8
NS = DB * DS
TOK = SEQ + NS
PAST, PAGE = 2048, 128
NPG = PAST // PAGE
LS = PAST + NS
H, HD = 8, 64
AW = H * HD
NI, DI = 4, 64
TOPK = 256
G, DK = 4, 128
GW = G * DK
CW = 4
CC = 3 * GW
CF = CC // P
FF = 4 * D
EPS = 1e-6
OFF_Q, OFF_K, OFF_V = 0, AW, 2 * AW
OFF_QI = 3 * AW
OFF_KI = OFF_QI + NI * DI
OFF_WI = OFF_KI + DI
OFF_CONV = OFF_WI + NI
OFF_A = OFF_CONV + CC
OFF_Z = OFF_A + 2 * G
N_IN = OFF_Z + GW
FIRST_SEL = TOPK // P
NEG_SCORE = -3.0e38
TAKEN = -3.3e38
MASKED = -1.0e30
LEVELS = 7
S_LEVELS = 3

IX_QI, IX_KI, IX_KI2, IX_WI, IX_A, IX_B = 0, 256, 320, 384, 388, 392
IX_W = 396


def constants():
    r = np.arange(P)
    row, col = r[:, None], r[None, :]
    s_ok = (row < NS) & (col < NS) & (row // DS == col // DS)
    parts = {}
    parts["ident"] = np.eye(P)
    parts["ones"] = np.ones((P, P))
    parts["tri"] = (row <= col)
    parts["tri_s"] = (row <= col) & s_ok
    parts["block_s"] = s_ok
    lev = []
    for l in range(LEVELS):
        s = 1 << l
        lev.append(-1.0 * ((row // (2 * s) == col // (2 * s)) & (row // s % 2 == 0) & (col // s % 2 == 1)))
    parts["level"] = np.concatenate(lev, 1)
    parts["score_causal"] = NEG_SCORE * (col > row)
    parts["score_new"] = NEG_SCORE * ~(s_ok & (col <= row))[:, :NS]
    parts["attn_causal"] = MASKED * (col > row)
    parts["low_big"] = -MASKED * (col >= row)
    parts["low_big_s"] = -MASKED * ~((col < row) & s_ok)
    parts["up_big"] = MASKED * (col < row)
    parts["up_big_s"] = MASKED * ~((row <= col) & s_ok)
    sel, sum_h = [], []
    for g in range(2):
        m = np.zeros((P, P))
        for bb in range(4):
            for h in range(NI):
                for q in range(DS):
                    m[(4 * g + bb) * DS + q, bb * 32 + h * DS + q] = 1
        sel.append(m)
        sum_h.append(m.T[:, :NS])
    parts["sel_ix"] = np.concatenate(sel, 1)
    parts["sum_ix"] = np.concatenate(sum_h, 1)
    parts["head_ix"] = ((r // DS) % NI)[:, None] == np.arange(NI)[None]
    sel = []
    for i in range(DB // 2):
        m = np.zeros((P, P))
        for b2 in range(2):
            for h in range(H):
                for q in range(DS):
                    m[(2 * i + b2) * DS + q, b2 * 64 + h * DS + q] = 1
        sel.append(m)
    parts["sel_at"] = np.concatenate(sel, 1)
    parts["in_batch"] = (r[:, None] < NS) & (r[:, None] // DS == np.arange(DB)[None])
    parts["columns"] = np.broadcast_to((np.arange(NS) // DS == np.arange(DB)[:, None]).reshape(1, -1), (P, DB * NS))
    at, where = 0, {}
    for n, a in parts.items():
        where[n] = (at, a.shape[1])
        at += a.shape[1]
    return np.ascontiguousarray(np.concatenate([np.asarray(a, np.float32) for a in parts.values()], 1)), where


CONST, CONST_AT = constants()
NC_COLS = CONST.shape[1]
BF_CONST = ("ident", "level", "columns", "attn_causal", "low_big", "low_big_s", "up_big", "up_big_s", "sel_at")
F_CONST = tuple(n for n in CONST_AT if n not in BF_CONST[1:])


class Map:

    def __init__(self, start=0):
        self.at = start

    def take(self, n):
        self.at += n
        return self.at - n


LASTING = 11989
STORES = ("kidx", "mix0", "mix1", "mix2", "mix3", "conv", "ssm", "y")


class Kernel:

    def __init__(self, nc, ctx, a):
        self.nc, self.ctx, self.a = nc, ctx, a
        self.in_use = []
        self.stored = {n: nc.alloc_semaphore(name=n + "_stored") for n in STORES}
        self.words = 53200
        self.arena = ctx.enter_context(nc.sbuf_tensor("arena", [P, LASTING], F32))
        self.work_ctx = ExitStack()
        ctx.callback(self.work_ctx.close)
        self.work = self.work_ctx.enter_context(nc.sbuf_tensor("work", [P, self.words - LASTING], F32))
        self.banks = ctx.enter_context(nc.psum_tensor("banks", [P, 8 * 512], F32))
        self.psum = [self.banks[:, i * 512:(i + 1) * 512] for i in range(8)]
        m = Map()
        self.c = {}
        for n in F_CONST:
            w = CONST_AT[n][1]
            self.c[n] = self.view(m.take(w), w)
        self.b = {}
        for n in BF_CONST:
            w = CONST_AT[n][1]
            self.b[n] = self.view(m.take(w // 2), w // 2).bitcast(BF16)
        self.g_mix = self.view(m.take(KD), KD)
        self.g_mlp = self.view(m.take(KD), KD)
        self.conv_w = self.view(m.take(CF * CW), CF, CW)
        self.gdn_row = self.view(m.take(GW), G, DK)
        self.a_row = self.view(m.take(2 * G), 2 * G)
        self.table = self.view(m.take(DB * NPG), DB * NPG).bitcast(I32)
        self.eps = self.view(m.take(1), 1)
        self.hT_at = m.take(KD * TOK)
        assert m.at == LASTING, m.at
        self.psI = self.view(m.take(IX_W), IX_W)
        self.psA = self.view(m.take(3 * AW), 3 * AW)
        self.psC = self.view(m.take(CC), CC)
        self.psZ = self.view(m.take(GW), GW)
        self.maskP = []
        for t in range(NT):
            n = (t + 1) * P
            self.maskP.append(self.view(m.take(n // 2), n // 2).bitcast(BF16) if t >= FIRST_SEL else None)
        self.maskS = self.view(m.take(LS // 2), LS // 2).bitcast(BF16)
        self.kiwi = self.view(m.take(NT * 76), NT, 76)
        self.xc_at = m.take(CF * (SEQ + CW - 1))
        self.z_at = m.take(NT * GW)
        self.free_at = m.at
        self.sc_at = m.take(sum((t + 1) * P for t in range(FIRST_SEL, NT)) + LS)
        self.ring_at = m.take(2 * KD * 512)
        self.stage_at = m.take(4 * 512)
        self.best_at = m.take(64)
        self.kv_at = self.free_at + 3 * NT * H
        self.pages_at = self.free_at - DB * NPG * DI
        assert m.at <= self.words, m.at

    def view(self, at, *dims):
        n = int(np.prod(dims))
        assert at >= LASTING or at + n <= LASTING
        ap = self.arena[:, at:at + n] if at < LASTING else self.work[:, at - LASTING:at - LASTING + n]
        if len(dims) == 2:
            ap = ap.rearrange("p (a b) -> p a b", a=dims[0])
        if len(dims) == 3:
            ap = ap.rearrange("p (a b c) -> p a b c", a=dims[0], b=dims[1])
        return ap

    def begin_dense_part(self):
        self.work_ctx.close()
        nc, enter = self.nc, self.ctx.enter_context
        self.x2 = enter(nc.sbuf_tensor("x2", [P, NT + 1, D], F32))
        self.h_hi = enter(nc.sbuf_tensor("h_hi", [P, KD, SEQ], F32R))
        self.h_lo = enter(nc.sbuf_tensor("h_lo", [P, KD, SEQ], F32R))

    def sem(self, name):
        self.in_use.append(self.nc.alloc_semaphore(name=name))
        return self.in_use[-1]

    def stage_done(self):
        self.nc.all_engine_barrier()
        self.nc.clear_and_free_semaphores(self.in_use)
        self.nc.all_engine_barrier()
        self.in_use = []

    def sems(self, name, n):
        return [self.sem(f"{name}{i}") for i in range(n)]


def rows_of(t):
    return P if t < NT else NS


def stage_constants(k):
    nc, a = k.nc, k.a
    landed, to_bf = k.sem("const_landed"), k.sem("const_bf16")
    stage = k.view(k.xc_at, NC_COLS)
    small = 6
    with nc.Block() as block:
        @block.sync
        def _(sp):
            sp.dma_start(stage, a["const"]).then_inc(landed, 16)
            with nc.allow_non_contiguous_dma(reason="small parameters laid over partitions"):
                sp.dma_start(k.g_mix, a["norm_mix"].rearrange("a (k p) -> p (a k)", p=P)).then_inc(landed, 16)
                sp.dma_start(k.g_mlp, a["norm_mlp"].rearrange("a (k p) -> p (a k)", p=P)).then_inc(landed, 16)
                for j in range(CW):
                    sp.dma_start(k.conv_w[:, :, j], a["conv_w"][0, j, :].rearrange("(f p) -> p f", p=P)).then_inc(landed, 16)
            for h in range(G):
                sp.dma_start(k.gdn_row[:, h, :], a["norm_gdn_out"].partition_broadcast(P).rearrange("p a n -> p (a n)")).then_inc(landed, 16)
            sp.dma_start(k.a_row[:, 0:G], a["a_log"].partition_broadcast(P).rearrange("p a n -> p (a n)")).then_inc(landed, 16)
            sp.dma_start(k.a_row[:, G:2 * G], a["dt_bias"].partition_broadcast(P).rearrange("p a n -> p (a n)")).then_inc(landed, 16)
            sp.dma_start(k.table[0:1, :], a["page_table"].rearrange("b n -> (b n)").rearrange("(a n) -> a n", a=1)).then_inc(landed, 16)
            sp.wait_ge(landed, 16 * (6 + CW + G))

        @block.vector
        def _(dve):
            dve.memset(k.eps, EPS)
            dve.wait_ge(landed, 16 * (6 + CW + G))
            for n in F_CONST:
                at, w = CONST_AT[n]
                dve.tensor_copy(k.c[n], stage[:, at:at + w])
            for n in BF_CONST:
                at, w = CONST_AT[n]
                dve.tensor_copy(k.b[n], stage[:, at:at + w])


def load_indexer_pages(k, q, batches):
    for b in batches:
        pages = k.view(k.pages_at + b * NPG * DI, NPG, DI)
        for p in range(NPG):
            page = q.value_load(k.table[0:1, b * NPG + p:b * NPG + p + 1], min_val=0, max_val=k.a["cache_kidx"].shape[1] - 1)
            q.dma_start(pages[:, p, :], k.a["cache_kidx"][0, bass.ds(page, 1), :, :].rearrange("a p d -> p (a d)")).then_inc(k.kidx_landed[b], 16)


def stage_norm(k, name, tiles, scratch, gain, load, out=None, split=None):
    nc = k.nc
    free = Map()
    xn = [scratch[:, free.take(D):free.at] for _ in range(2)]
    junk = scratch[:, free.take(D):free.at]
    stat = scratch[:, free.take(3 * (NT + 1)):free.at].rearrange("p (a b) -> p a b", a=3)
    if split:
        hi, lo, sample = split
        tmp = [scratch[:, free.take(512):free.at].rearrange("p (f n) -> p f n", f=4) for _ in range(2)]
        rounded, rest = k.sem(name + "_rounded"), k.sem(name + "_rest")
    loaded = k.sems(name + "_loaded", 3)
    squared, rooted, scaled = k.sem(name + "_squared"), k.sem(name + "_rooted"), k.sem(name + "_rstd")
    normed, turned, kept = k.sem(name + "_normed"), k.sem(name + "_turned"), k.sem(name + "_kept")
    n = NT + 1
    with nc.Block() as block:
        if load is not None:
            @block.gpsimd
            def _(pool):
                load_indexer_pages(k, pool, range(0, 3))

            @block.sync
            def _(sp):
                k.landed_at = {0: 16 * load_indexer_weights(k, sp, k.view(k.ring_at, KD, 512), k.ix_landed[0])}
                for t in range(n):
                    if t >= 3:
                        sp.wait_ge(normed, t - 2)
                    sp.dma_start(tiles[t][0:rows_of(t), :], load(t)).then_inc(loaded[t % 3], 16)

        @block.scalar
        def _(act):
            def round_tile(t):
                for half in range(2):
                    act.wait_ge(kept, 2 * t + half + 1)
                    act.copy(hi[:, 4 * half:4 * half + 4, t * P:(t + 1) * P], tmp[half]).then_inc(rounded, 1)

            for t in range(n):
                r = rows_of(t)
                if load is not None:
                    act.wait_ge(loaded[t % 3], 16 * (t // 3 + 1))
                if t:
                    act.wait_ge(squared, t)
                act.activation(junk[0:r, :], tiles[t][0:r, :], ACT.Square, accum_out=stat[0:r, 0, t:t + 1]).then_inc(squared, 1)
                act.wait_ge(squared, t + 1)
                act.activation(stat[0:r, 1, t:t + 1], stat[0:r, 0, t:t + 1], ACT.Sqrt, scale=1.0 / D, bias=k.eps[0:r, :]).then_inc(rooted, 1)
                if split and t >= 1:
                    round_tile(t - 1)

        @block.vector
        def _(dve):
            def norm(t):
                r = rows_of(t)
                dve.wait_ge(rooted, t + 1)
                dve.reciprocal(stat[0:r, 2, t:t + 1], stat[0:r, 1, t:t + 1]).then_inc(scaled, 1)
                if t >= 2:
                    dve.wait_ge(turned, t - 1)
                dve.wait_ge(scaled, t + 1)
                dve.tensor_scalar(xn[t % 2][0:r, :], tiles[t][0:r, :], stat[0:r, 2, t:t + 1], None, ALU.mult).then_inc(normed, 1)

            def keep(t):
                r = rows_of(t)
                dve.wait_ge(turned, t + 1)
                for half in range(2):
                    part = slice(4 * half, 4 * half + 4)
                    src = k.psum[2 * (t % 2) + half][:, :].rearrange("p (f n) -> p f n", f=4)[:, :, 0:r]
                    g = gain[:, part].unsqueeze(2).to_broadcast([P, 4, r])
                    if not split:
                        dst = out[:, part, t * P:t * P + r]
                    elif t < NT:
                        dst = tmp[half]
                        if t:
                            dve.wait_ge(rest, 2 * (t - 1) + half + 1)
                    else:
                        dst = sample[:, part, 0:r]
                    dve.tensor_tensor(dst, src, g, ALU.mult).then_inc(kept, 1)

            def rest_of(t):
                for half in range(2):
                    part, cols = slice(4 * half, 4 * half + 4), slice(t * P, (t + 1) * P)
                    dve.wait_ge(rounded, 2 * t + half + 1)
                    dve.tensor_tensor(lo[:, part, cols], tmp[half], hi[:, part, cols], ALU.subtract).then_inc(rest, 1)

            if split:
                dve.memset(sample[:, :, NS:P], 0.0)
            norm(0)
            for t in range(n):
                if t + 1 < n:
                    norm(t + 1)
                keep(t)
                if split and t < NT:
                    rest_of(t)

        @block.tensor
        def _(pe):
            for t in range(n):
                r = rows_of(t)
                pe.wait_ge(normed, t + 1)
                if t >= 2:
                    pe.wait_ge(kept, 2 * (t - 1))
                for f in range(KD):
                    last = pe.transpose(k.psum[2 * (t % 2) + f // 4][:, (f % 4) * P:(f % 4) * P + r],
                                        xn[t % 2][0:r, f * P:(f + 1) * P], k.c["ident"][0:r, 0:r])
                last.then_inc(turned, 1)


def projection_of_indexer():
    jobs = [(0, "F", f * P, P, j) for f in range(2) for j in range(2)]
    jobs += [(0, "F", IX_KI, P, j) for j in range(2)]
    jobs += [(0, "T", IX_KI2, IX_W - IX_KI2, t) for t in range(NT)]
    jobs += [(0, "S", 0, IX_W, 0)]
    return jobs


def load_indexer_weights(k, q, dst, sem):
    w = k.a["w_in"][0].rearrange("(k p) n -> p k n", p=P)
    for at, off, n in ((IX_QI, OFF_QI, NI * DI), (IX_KI, OFF_KI, DI), (IX_KI2, OFF_KI, DI + NI), (IX_A, OFF_A, 2 * G)):
        q.dma_start(dst[:, :, at:at + n], w[:, :, off:off + n]).then_inc(sem, 16)
    return 4


def project_products(k, pe, jobs, banks, sems):
    hT = k.view(k.hT_at, KD, TOK)
    landed, made, kept = sems
    seen = -1
    for n, (c, kind, col, w, at) in enumerate(jobs):
        if c != seen:
            pe.wait_ge(landed[c % 2], k.landed_at[c])
            seen = c
        if n >= banks:
            pe.wait_ge(kept, n - banks + 1)
        bank = k.psum[n % banks]
        ring = k.view(k.ring_at + (c % 2) * KD * 512, KD, 512)
        if kind == "K":
            pe.wait_ge(kept, k.turn_of[n] + 1)
            src = k.view(k.stage_at + k.slot_of[k.turn_of[n]] * 512, 512)
            for i in range(4):
                last = pe.transpose(bank[:, i * P:(i + 1) * P], src[:, i * P:(i + 1) * P], k.c["ident"])
        for f in range(KD if kind != "K" else 0):
            if kind == "F":
                last = pe.matmul(bank[0:w, :], ring[:, f, col:col + w], hT[:, f, at * 512:(at + 1) * 512],
                                 start=(f == 0), stop=(f == KD - 1))
            elif kind == "T":
                last = pe.matmul(bank[:, 0:w], hT[:, f, at * P:(at + 1) * P], ring[:, f, col:col + w],
                                 start=(f == 0), stop=(f == KD - 1))
            else:
                last = pe.matmul(bank[0:NS, 0:w], hT[:, f, SEQ:TOK], ring[:, f, col:col + w],
                                 start=(f == 0), stop=(f == KD - 1))
        last.then_inc(made, 1)


def stage_indexer_projection(k):
    nc = k.nc
    jobs = projection_of_indexer()
    landed, made, kept = k.ix_landed, k.sem("ix_made"), k.sem("ix_kept")
    k.qiT = k.view(k.xc_at, 2, SEQ)
    k.kiT = k.view(k.xc_at + 2 * SEQ, SEQ)
    with nc.Block() as block:
        @block.gpsimd
        def _(pool):
            load_indexer_pages(k, pool, range(3, 6))

        @block.tensor
        def _(pe):
            project_products(k, pe, jobs, 8, (landed, made, kept))

        @block.scalar
        def _(act):
            for n, (c, kind, col, w, at) in enumerate(jobs):
                act.wait_ge(made, n + 1)
                bank = k.psum[n % 8]
                if kind == "F" and col == IX_KI:
                    act.copy(k.kiT[:, at * 512:(at + 1) * 512], bank[:, :]).then_inc(kept, 1)
                elif kind == "F":
                    act.copy(k.qiT[:, col // P, at * 512:(at + 1) * 512], bank[:, :]).then_inc(kept, 1)
                elif kind == "T":
                    act.copy(k.kiwi[:, at, :], bank[:, 0:w]).then_inc(kept, 1)
                else:
                    act.copy(k.psI[0:NS, :], bank[0:NS, 0:w]).then_inc(kept, 1)


def stage_prompt_scores(k):
    nc = k.nc
    k.scP, at = [None] * NT, k.sc_at
    for t in range(FIRST_SEL, NT):
        k.scP[t] = k.view(at, (t + 1) * P)
        at += (t + 1) * P
    k.scS = k.view(at, LS)
    relu_buf = [k.view(k.ring_at + i * 512, 512) for i in range(4)]
    w_half = k.view(k.ring_at + 2048, NT, NI)
    made, relued, summed, halved = k.sem("scp_made"), k.sem("scp_relued"), k.sem("scp_summed"), k.sem("scp_halved")
    out_sem = k.stored["kidx"]
    items = [(t, c, min(512, (t + 1) * P - c), h)
             for t in range(FIRST_SEL, NT) for c in range(0, (t + 1) * P, 512) for h in range(NI)]
    with nc.Block() as block:
        @block.gpsimd
        def _(pool):
            load_indexer_pages(k, pool, range(6, DB))

        @block.sync
        def _(sp):
            sp.dma_start(k.a["new_kidx_prompt"][0, 0].rearrange("(t p) d -> p t d", p=P), k.kiwi[:, :, 0:DI]).then_inc(out_sem, 16)
            sp.dma_start(k.a["new_kidx_sample"][0].rearrange("b t d -> (b t) d"), k.psI[0:NS, IX_KI:IX_KI + DI]).then_inc(out_sem, 16)
            sp.wait_ge(out_sem, 32)

        @block.tensor
        def _(pe):
            for n, (t, c, w, h) in enumerate(items):
                if n >= 4:
                    pe.wait_ge(relued, n - 3)
                lo = (h % 2) * DI
                pe.matmul(k.psum[n % 4][:, 0:w], k.qiT[lo:lo + DI, h // 2, t * P:(t + 1) * P],
                          k.kiT[lo:lo + DI, c:c + w], start=True, stop=True).then_inc(made, 1)

        @block.scalar
        def _(act):
            for n, (t, c, w, h) in enumerate(items):
                act.wait_ge(made, n + 1)
                if n >= 4:
                    act.wait_ge(summed, n - 3)
                act.activation(relu_buf[n % 4][:, 0:w], k.psum[n % 4][:, 0:w], ACT.Relu).then_inc(relued, 1)

        @block.vector
        def _(dve):
            dve.tensor_scalar(w_half, k.kiwi[:, :, DI:DI + NI], DI ** -0.5 * NI ** -0.5, None, ALU.mult).then_inc(halved, 1)
            dve.wait_ge(halved, 1)
            done = 0
            for n, (t, c, w, h) in enumerate(items):
                dve.wait_ge(relued, n + 1)
                sc = k.scP[t][:, c:c + w]
                if h == 0:
                    dve.tensor_scalar(sc, relu_buf[n % 4][:, 0:w], w_half[:, t, h:h + 1], None, ALU.mult).then_inc(summed, 1)
                else:
                    dve.wait_ge(summed, n)
                    dve.scalar_tensor_tensor(out=sc, in0=relu_buf[n % 4][:, 0:w], scalar=w_half[:, t, h:h + 1],
                                             in1=sc, op0=ALU.mult, op1=ALU.add).then_inc(summed, 1)
            dve.wait_ge(summed, len(items))
            for t in range(FIRST_SEL, NT):
                own = k.scP[t][:, t * P:(t + 1) * P]
                dve.tensor_tensor(own, own, k.c["score_causal"], ALU.add)


def stage_sample_scores(k):
    nc = k.nc
    m = Map(k.xc_at)
    qi_dup = k.view(m.take(NI * 2 * DI), NI, 2 * DI)
    qiS = k.view(m.take(NI * NS), NI, NS)
    qiB = k.view(m.take(DB * NI * DS), DB, NI * DS)
    kiN = k.view(m.take(NS), NS)
    wi_s = k.view(m.take(NI), NI)
    w_pick = [k.view(m.take(NI), NI) for _ in range(2)]
    w_row = k.view(m.take(2), 2)
    pages = [k.view(k.pages_at + b * NPG * DI, NPG, DI) for b in range(DB)]
    k.kT4 = [k.view(m.take(NPG // 2 * PAGE), NPG // 2, PAGE) for _ in range(4)]
    rel = [k.view(m.take(512), 512) for _ in range(3)]
    assert m.at <= k.pages_at
    k.mx_landed = k.sems("mxw_landed", 2)
    prep, prep_pe, turned, kept = k.sem("scs_prep"), k.sem("scs_prep_pe"), k.sem("scs_turned"), k.sem("scs_kept")
    made, relued, summed, drained = k.sem("scs_made"), k.sem("scs_relued"), k.sem("scs_summed"), k.sem("scs_drained")
    NH = NI * DS
    with nc.Block() as block:
        @block.sync
        def _(sp):
            for c in range(2):
                load_mixer_weights(k, sp, c)

        @block.tensor
        def _(pe):
            pe.wait_ge(prep, 1)
            for h in range(NI):
                last = pe.transpose(k.psum[4][:, h * NS:(h + 1) * NS], qi_dup[0:NS, h, :], k.c["ident"][0:NS, 0:NS])
            last = pe.transpose(k.psum[4][0:DI, NI * NS:NI * NS + NS], k.psI[0:NS, IX_KI:IX_KI + DI], k.c["ident"][0:NS, 0:NS])
            last.then_inc(prep_pe, 1)
            for g in range(2):
                last = pe.matmul(k.psum[5][:, g * NI:(g + 1) * NI], k.c["sel_ix"][0:NS, g * P:(g + 1) * P], wi_s[0:NS, :],
                                 start=True, stop=True)
            last.then_inc(prep_pe, 1)
            pe.wait_ge(prep, 7)

            def turn(b):
                pe.wait_ge(k.kidx_landed[b], 16 * NPG)
                if b >= 1:
                    pe.wait_ge(kept, 2 * b)
                for j in range(NPG // 2):
                    last = pe.transpose(k.psum[4 + j // 4][:, (j % 4) * P:(j % 4 + 1) * P],
                                        pages[b][:, 2 * j:2 * j + 2, :].rearrange("p a d -> p (a d)"), k.c["ident"])
                last.then_inc(turned, 1)

            n = 0
            for g in range(2):
                for bb in range(4):
                    turn(4 * g + bb)
                pe.wait_ge(kept, 8 * (g + 1))
                for par in range(2):
                    for half in range(2):
                        if n >= 2:
                            pe.wait_ge(relued, n - 1)
                        for bb in range(4):
                            last = pe.matmul(k.psum[6 + n % 2][bb * NH:(bb + 1) * NH, :],
                                             qiB[par * DI:(par + 1) * DI, 4 * g + bb, :],
                                             k.kT4[bb][par * DI:(par + 1) * DI, 4 * half:4 * half + 4, :],
                                             start=True, stop=True)
                        last.then_inc(made, 1)
                        pe.wait_ge(relued, n + 1)
                        pe.matmul(k.psum[n % 4][0:NS, :], k.c["sum_ix"][:, g * NS:(g + 1) * NS], rel[n % 3],
                                  start=(g == 0), stop=(g == 1)).then_inc(summed, 1)
                        n += 1
                pe.wait_ge(relued, n)
            pe.wait_ge(drained, 4)
            for g in range(2):
                for bb in range(4):
                    last = pe.matmul(k.psum[6 + g][bb * NH:(bb + 1) * NH, 0:NS], qiB[0:DI, 4 * g + bb, :], kiN[0:DI, :],
                                     start=True, stop=True)
                last.then_inc(made, 1)
            for g in range(2):
                pe.wait_ge(relued, 8 + g + 1)
                pe.matmul(k.psum[0][0:NS, 0:NS], k.c["sum_ix"][:, g * NS:(g + 1) * NS], rel[g][:, 0:NS],
                          start=(g == 0), stop=(g == 1)).then_inc(summed, 1)

        @block.scalar
        def _(act):
            for b in range(DB):
                act.wait_ge(turned, b + 1)
                if b >= 4:
                    act.wait_ge(made, 4)
                if b == 0:
                    act.wait_ge(prep, 7)
                for i in range(2):
                    act.copy(k.kT4[b % 4][:, 4 * i:4 * i + 4, :].rearrange("p a n -> p (a n)"), k.psum[4 + i][:, :]).then_inc(kept, 1)

        @block.vector
        def _(dve):
            for i in range(2):
                last = dve.tensor_copy(qi_dup[0:NS, :, i * DI:(i + 1) * DI], k.psI[0:NS, 0:NI * DI].rearrange("p (h d) -> p h d", h=NI))
            last = dve.tensor_scalar(wi_s[0:NS, :], k.psI[0:NS, IX_WI:IX_WI + NI], DI ** -0.5 * NI ** -0.5, None, ALU.mult)
            last.then_inc(prep, 1)
            dve.wait_ge(prep_pe, 1)
            dve.tensor_copy(qiB.rearrange("p b (h q) -> p b h q", h=NI),
                            k.psum[4][:, 0:NI * NS].rearrange("p (h b q) -> p b h q", h=NI, b=DB)).then_inc(prep, 1)
            dve.tensor_copy(kiN[0:DI, :], k.psum[4][0:DI, NI * NS:NI * NS + NS]).then_inc(prep, 1)
            dve.wait_ge(prep_pe, 2)
            for g in range(2):
                dve.tensor_tensor(w_pick[g], k.psum[5][:, g * NI:(g + 1) * NI], k.c["head_ix"], ALU.mult).then_inc(prep, 1)
            dve.wait_ge(prep, 5)
            for g in range(2):
                dve.reduce_sum(w_row[:, g:g + 1], w_pick[g], AX_X).then_inc(prep, 1)
            dve.wait_ge(prep, 7)
            for n in range(8):
                dve.wait_ge(made, n + 1)
                if n >= 3:
                    dve.wait_ge(summed, n - 2)
                dve.tensor_scalar(rel[n % 3], k.psum[6 + n % 2][:, :], 0.0, w_row[:, n // 4:n // 4 + 1], ALU.max, ALU.mult).then_inc(relued, 1)
            dve.wait_ge(summed, 8)
            for n in range(4):
                par, half = n // 2, n % 2
                dst = k.scS[0:NS, 0:PAST].rearrange("q (j r n) -> q r j n", r=2, n=PAGE)[:, par, 4 * half:4 * half + 4, :]
                dve.tensor_copy(dst, k.psum[n][0:NS, :].rearrange("q (j n) -> q j n", j=4)).then_inc(drained, 1)
            for g in range(2):
                dve.wait_ge(made, 8 + g + 1)
                dve.tensor_scalar(rel[g][:, 0:NS], k.psum[6 + g][:, 0:NS], 0.0, w_row[:, g:g + 1], ALU.max, ALU.mult).then_inc(relued, 1)
            dve.wait_ge(summed, 10)
            dve.tensor_tensor(k.scS[0:NS, PAST:LS], k.psum[0][0:NS, 0:NS], k.c["score_new"][0:NS, :], ALU.add)


CHUNKS = (OFF_CONV, OFF_CONV + 512, OFF_CONV + 1024, OFF_Q, OFF_K, OFF_V, OFF_Z)
Q_CHUNK, K_CHUNK, V_CHUNK, Z_CHUNK = 3, 4, 5, 6


def load_mixer_weights(k, q, c):
    w = k.a["w_in"][0].rearrange("(k p) n -> p k n", p=P)
    dst = k.view(k.ring_at + (c % 2) * KD * 512, KD, 512)
    q.dma_start(dst, w[:, :, CHUNKS[c]:CHUNKS[c] + 512]).then_inc(k.mx_landed[c % 2], 16)


def projection_of_mixers():
    prompt = lambda c: [(c, "F", f * P, P, j) for f in range(4) for j in range(2)]
    by_token = lambda c: [(c, "T", 0, 512, t) for t in range(NT)]
    sample = lambda c: [(c, "S", 0, 512, 0)]
    jobs = []
    for c in range(Q_CHUNK):
        jobs += prompt(c) + sample(c)
    jobs += prompt(Q_CHUNK) + sample(Q_CHUNK)
    jobs += interleave_turns(prompt(K_CHUNK)) + sample(K_CHUNK)
    jobs += by_token(V_CHUNK) + sample(V_CHUNK)
    return jobs + by_token(Z_CHUNK) + sample(Z_CHUNK)


def interleave_turns(keys):
    out = []
    for n in range(len(keys) + 2):
        if n < len(keys):
            out.append(keys[n])
        if n >= 2:
            c, _, col, w, j = keys[n - 2]
            out.append((c, "K", col, w, j))
    return out


def stage_mixer_projection(k):
    nc = k.nc
    jobs = projection_of_mixers()
    landed, made, kept = k.mx_landed, k.sem("mx_made"), k.sem("mx_kept")
    stored = [k.stored[f"mix{i}"] for i in range(4)]
    last_job = {c: max(n for n, j in enumerate(jobs) if j[0] == c) for c in range(len(CHUNKS))}
    k.landed_at = {c: 16 * (c // 2 + 1) for c in range(len(CHUNKS))}
    staged = [n for n, j in enumerate(jobs) if Q_CHUNK <= j[0] <= V_CHUNK and j[1] != "S"]
    k.slot_of = {n: i % 4 for i, n in enumerate(staged)}
    order = {n: i for i, n in enumerate(staged)}
    k.turn_of = {n: jobs.index((K_CHUNK, "F") + j[2:]) for n, j in enumerate(jobs) if j[1] == "K"}
    turned_by = {m: n for n, m in k.turn_of.items()}
    xc = k.view(k.xc_at, CF, SEQ + CW - 1)
    z = k.view(k.z_at, NT, GW)
    stage = [k.view(k.stage_at + i * 512, 512) for i in range(4)]
    topk_at = k.sem("topk_max"), k.sem("topk_taken")
    tap = [k.view(k.stage_at + j * 512, 512) for j in range(CW)]
    tapped, added, silued, padded = k.sem("mx_tapped"), k.sem("mx_added"), k.sem("mx_silu"), k.sem("mx_padded")
    pieces = [(n, c * 4 + col // P, at) for n, (c, kind, col, wd, at) in enumerate(jobs) if c < Q_CHUNK and kind == "F"]
    best = k.view(k.best_at, 8, 8)
    work = [(P, k.scP[t]) for t in range(FIRST_SEL, NT)] + [(NS, k.scS)]
    masks = [k.maskP[t] for t in range(FIRST_SEL, NT)] + [k.maskS]
    with nc.Block() as block:
        @block.sync
        def _(sp):
            for c in range(2, len(CHUNKS)):
                sp.wait_ge(made, last_job[c - 2] + 1)
                load_mixer_weights(k, sp, c)

        @block.tensor
        def _(pe):
            project_products(k, pe, jobs, 8, (landed, made, kept))

        @block.scalar
        def _(act):
            def silu(i):
                _, f, at = pieces[i]
                act.wait_ge(added, (CW - 1) * (i + 1))
                act.activation(xc[:, f, at * 512:(at + 1) * 512], tap[0], ACT.Silu).then_inc(silued, 1)

            for n, (c, kind, col, wd, at) in enumerate(jobs):
                act.wait_ge(made, n + 1)
                bank = k.psum[n % 8]
                if kind == "S":
                    dst = (k.psC[0:NS, c * 512:(c + 1) * 512] if c < Q_CHUNK else
                           k.psA[0:NS, (c - Q_CHUNK) * 512:(c - Q_CHUNK + 1) * 512] if c <= V_CHUNK else k.psZ[0:NS, :])
                    act.copy(dst, bank[0:NS, :]).then_inc(kept, 1)
                elif c < Q_CHUNK:
                    act.copy(xc[:, c * 4 + col // P, CW - 1 + at * 512:CW - 1 + (at + 1) * 512], bank[:, :]).then_inc(kept, 1)
                    i = pieces.index((n, c * 4 + col // P, at))
                    if i:
                        silu(i - 1)
                        act.wait_ge(silued, i)
                    act.wait_ge(padded, 1)
                    act.wait_ge(kept, n + 1)
                    for j in range(CW):
                        act.activation(tap[j], xc[:, c * 4 + col // P, at * 512 + j:at * 512 + j + 512], ACT.Copy,
                                       scale=k.conv_w[:, c * 4 + col // P, j:j + 1]).then_inc(tapped, 1)
                elif c <= V_CHUNK:
                    i = order[n]
                    if i >= 4:
                        act.wait_ge(stored[i % 4], 16 * (i // 4))
                        if staged[i - 4] in turned_by:
                            act.wait_ge(made, turned_by[staged[i - 4]] + 1)
                    elif i == 0:
                        silu(len(pieces) - 1)
                        act.wait_ge(silued, len(pieces))
                    act.copy(stage[i % 4], bank[:, :]).then_inc(kept, 1)
                else:
                    act.copy(z[:, at, :], bank[:, :]).then_inc(kept, 1)

        @block.gpsimd
        def _(pool):
            pool.memset(xc[:, :, 0:CW - 1], 0.0).then_inc(padded, 1)
            for i in range(len(pieces)):
                for j in range(1, CW):
                    pool.wait_ge(tapped, CW * i + j + 1)
                    if j > 1:
                        pool.wait_ge(added, (CW - 1) * i + j - 1)
                    pool.tensor_tensor(tap[0], tap[0], tap[j], ALU.add).then_inc(added, 1)
            for i, n in enumerate(staged):
                c, kind, col, wd, at = jobs[n]
                pool.wait_ge(kept, n + 1)
                if c == Q_CHUNK:
                    dst, src = k.a["q_T"][col:col + P, at * 512:(at + 1) * 512], stage[i % 4]
                elif c == K_CHUNK and kind == "F":
                    dst, src = k.a["k_T"][col:col + P, at * 512:(at + 1) * 512], stage[i % 4]
                elif c == K_CHUNK:
                    rows = k.a["new_k_prompt"][0, 0].rearrange("t h d -> t (h d)").rearrange("(j i p) n -> j p i n", i=4, p=P)
                    dst, src = rows[at, :, :, col:col + P], stage[i % 4].rearrange("p (i n) -> p i n", i=4)
                else:
                    dst, src = k.a["new_v_prompt"][0, 0].rearrange("t h d -> t (h d)")[at * P:(at + 1) * P, :], stage[i % 4]
                pool.dma_start(dst, src).then_inc(stored[i % 4], 16)
            for i in range(4):
                pool.wait_ge(stored[i], 16 * len(staged[i::4]))

        @block.vector
        def _(dve):
            maxed, taken = topk_at
            n = len(work)
            for r in range(TOPK // 8):
                for i, (rows, sc) in enumerate(work):
                    if r:
                        dve.wait_ge(taken, (r - 1) * n + i + 1)
                    dve.max(best[0:rows, i, :], sc[0:rows, :]).then_inc(maxed, 1)
                for i, (rows, sc) in enumerate(work):
                    dve.wait_ge(maxed, r * n + i + 1)
                    dve.match_replace(sc[0:rows, :], best[0:rows, i, :], sc[0:rows, :], TAKEN).then_inc(taken, 1)
            for i, (rows, sc) in enumerate(work):
                dve.wait_ge(taken, (TOPK // 8 - 1) * n + i + 1)
                dve.tensor_scalar(masks[i][0:rows, :], sc[0:rows, :], TAKEN, MASKED, ALU.not_equal, ALU.mult)


def stage_conv(k):
    nc, a = k.nc, k.a
    xc = k.view(k.xc_at, CF, SEQ + CW - 1)
    z = k.view(k.z_at, NT * GW)
    n_all = NT + 1
    m = Map(k.free_at)
    k.qkvS = k.view(m.take(CF * NS), CF, NS)
    k.gates = k.view(m.take(4 * n_all * G), 4, n_all * G)
    k.gdn_at = m.at
    state = k.view(m.take(CC), CC)
    tail = k.view(m.take(CC), CC)
    xs = k.view(m.take(CF * DB * (DS + CW - 1)), CF * DB, DS + CW - 1)
    tap = [k.view(m.take(CF * NS), CF * DB, DS) for _ in range(2)]
    ab = k.view(m.take(n_all * 2 * G), n_all, 2 * G)
    w = [k.view(m.take(n_all * G), n_all, G) for _ in range(7)]
    alog = k.view(m.take(G), G)
    assert m.at <= k.words
    k.alog = alog
    landed, out_sem = k.sem("cv_landed"), k.stored["conv"]
    turned, tails, laid = k.sem("cv_turned"), k.sem("cv_tails"), k.sem("cv_laid")
    tapped_s = k.sem("cv_tapped_sample")
    gate_v, gate_s = k.sem("cv_gate_vector"), k.sem("cv_gate_scalar")
    z_silu, z_done = k.sem("cv_z_silu"), k.sem("cv_z_done")
    with nc.Block() as block:
        @block.sync
        def _(sp):
            sp.dma_start(state[0:DB * (CW - 1), :], a["state_conv"][0].rearrange("b j c -> (b j) c")).then_inc(landed, 16)
            n = 0
            for b in range(DB):
                sp.dma_start(a["new_conv_sample"][0, b], k.psC[b * DS + DS - CW + 1:(b + 1) * DS, :]).then_inc(out_sem, 16)
            sp.dma_start(a["new_k_sample"][0].rearrange("b t h d -> (b t) (h d)"), k.psA[0:NS, AW:2 * AW]).then_inc(out_sem, 16)
            sp.dma_start(a["new_v_sample"][0].rearrange("b t h d -> (b t) (h d)"), k.psA[0:NS, 2 * AW:3 * AW]).then_inc(out_sem, 16)
            sp.wait_ge(tails, 3)
            sp.dma_start(a["new_conv_prompt"][0, 0], tail[0:CW - 1, :]).then_inc(out_sem, 16)
            sp.wait_ge(out_sem, 16 * (DB + 3))

        @block.tensor
        def _(pe):
            for f in range(CF):
                last = pe.transpose(k.psum[f // 4][0:CW - 1, (f % 4) * P:(f % 4 + 1) * P], xc[:, f, SEQ:SEQ + CW - 1], k.c["ident"])
            for f in range(CF):
                last = pe.transpose(k.psum[4 + f // 6][:, (f % 6) * NS:(f % 6 + 1) * NS], k.psC[0:NS, f * P:(f + 1) * P], k.c["ident"][0:NS, 0:NS])
            pe.wait_ge(landed, 16)
            n = DB * (CW - 1)
            for f in range(CF):
                last = pe.transpose(k.psum[3][:, f * n:(f + 1) * n], state[0:n, f * P:(f + 1) * P], k.c["ident"][0:n, 0:n])
            last.then_inc(turned, 1)

        @block.scalar
        def _(act):
            act.wait_ge(turned, 1)
            for i in range(3):
                act.copy(tail[0:CW - 1, i * 512:(i + 1) * 512], k.psum[i][0:CW - 1, :]).then_inc(tails, 1)
            act.wait_ge(gate_v, 4)
            act.activation(alog, k.a_row[:, 0:G], ACT.Exp).then_inc(gate_s, 1)
            act.activation(w[1], w[0], ACT.Abs).then_inc(gate_s, 1)
            act.wait_ge(gate_s, 2)
            act.activation(w[2], w[1], ACT.Exp, scale=-1.0).then_inc(gate_s, 1)
            act.activation(w[3], ab[:, :, G:2 * G], ACT.Exp, scale=-1.0).then_inc(gate_s, 1)
            act.wait_ge(gate_s, 4)
            act.activation(w[4], w[2], ACT.Ln, bias=1.0).then_inc(gate_s, 1)
            act.activation(w[5], w[3], ACT.Ln, bias=1.0).then_inc(gate_s, 1)
            for i in range(4):
                act.activation(z[:, i * 1024:(i + 1) * 1024], z[:, i * 1024:(i + 1) * 1024], ACT.Silu).then_inc(z_silu, 1)
            act.activation(k.psZ[0:NS, :], k.psZ[0:NS, :], ACT.Silu).then_inc(z_silu, 1)
            act.wait_ge(tapped_s, 7)
            act.activation(k.qkvS.rearrange("p f n -> p (f n)"), tap[1].rearrange("p f n -> p (f n)"), ACT.Silu)

        @block.gpsimd
        def _(pool):
            for i in range(NT):
                pool.wait_ge(z_silu, i // 2 + 1)
                zi = z[:, i * GW:(i + 1) * GW]
                pool.tensor_tensor(zi, zi, k.gdn_row.rearrange("p h d -> p (h d)"), ALU.mult)
            pool.wait_ge(z_silu, 5)
            pool.tensor_tensor(k.psZ[0:NS, :], k.psZ[0:NS, :], k.gdn_row[0:NS].rearrange("p h d -> p (h d)"), ALU.mult)

        @block.vector
        def _(dve):
            dve.memset(ab, 0.0).then_inc(gate_v, 1)
            dve.wait_ge(gate_v, 1)
            dve.tensor_copy(ab[:, 0:NT, :], k.kiwi[:, :, DI + NI:DI + NI + 2 * G]).then_inc(gate_v, 1)
            dve.tensor_copy(ab[0:NS, NT, :], k.psI[0:NS, IX_A:IX_A + 2 * G]).then_inc(gate_v, 1)
            dve.wait_ge(gate_v, 3)
            dve.tensor_tensor(w[0], ab[:, :, 0:G], k.a_row[:, G:2 * G].unsqueeze(1).to_broadcast([P, n_all, G]), ALU.add).then_inc(gate_v, 1)
            dve.wait_ge(turned, 1)
            dve.tensor_copy(xs[:, :, 0:CW - 1], k.psum[3][:, 0:CF * DB * (CW - 1)].rearrange("p (f j) -> p f j", j=CW - 1)).then_inc(laid, 1)
            for i in range(2):
                dve.tensor_copy(xs[:, i * 6 * DB:(i + 1) * 6 * DB, CW - 1:], k.psum[4 + i][:, 0:6 * NS].rearrange("p (f j) -> p f j", j=DS)).then_inc(laid, 1)
            g, beta, lnb = (k.gates[:, i, :].rearrange("p (t h) -> p t h", h=G) for i in range(3))
            dve.wait_ge(gate_s, 6)
            dve.scalar_tensor_tensor(out=w[6], in0=w[0], scalar=0.0, in1=w[4], op0=ALU.max, op1=ALU.add).then_inc(gate_v, 1)
            dve.tensor_scalar(lnb, w[5], -1.0, None, ALU.mult)
            dve.tensor_scalar(w[3], w[3], 1.0, None, ALU.add).then_inc(gate_v, 1)
            dve.wait_ge(gate_v, 6)
            dve.scalar_tensor_tensor(out=g, in0=w[6], scalar=-1.0, in1=alog.unsqueeze(1).to_broadcast([P, n_all, G]),
                                     op0=ALU.mult, op1=ALU.mult)
            dve.reciprocal(beta, w[3])
            dve.wait_ge(laid, 3)
            n = 0
            xs4 = xs.rearrange("p (f b) j -> p f b j", b=DB)
            t4 = [t.rearrange("p (f b) j -> p f b j", b=DB) for t in tap]
            for j in range(CW):
                wj = k.conv_w[:, :, j:j + 1].unsqueeze(3).to_broadcast([P, CF, DB, DS])
                if j >= 2:
                    dve.wait_ge(tapped_s, n)
                dve.tensor_tensor(t4[0 if j else 1], xs4[:, :, :, j:j + DS], wj, ALU.mult).then_inc(tapped_s, 1)
                n += 1
                if j:
                    dve.wait_ge(tapped_s, n)
                    dve.tensor_tensor(tap[1], tap[1], tap[0], ALU.add).then_inc(tapped_s, 1)
                    n += 1


def gdn_view(k, t, part):
    if t == NT:
        return k.qkvS[:, part * G:(part + 1) * G, :]
    return k.view(k.xc_at, CF, SEQ + CW - 1)[:, part * G:(part + 1) * G, t * P:(t + 1) * P]


def stage_l2norm(k):
    nc = k.nc
    KEY_ROW = 32
    xc = k.view(k.xc_at, CF, SEQ + CW - 1)
    items = [(xc[:, f, j * 512:(j + 1) * 512], 512, (f % G) * 2 + j + (0 if f < G else KEY_ROW)) for f in range(2 * G) for j in range(2)]
    items += [(k.qkvS[:, part * G:(part + 1) * G, :].rearrange("p f n -> p (f n)"), G * NS, 2 * G + part * KEY_ROW) for part in range(2)]
    n_rows = 2 * G + 1
    rows = KEY_ROW + n_rows
    m = Map(k.gdn_at)
    sq = [k.view(m.take(512), 512) for _ in range(4)]
    root, inv = k.view(m.take(512), 512), k.view(m.take(512), 512)
    pick = [k.view(m.take(2 * rows), 2 * rows) for _ in range(2)]
    spread = k.view(m.take(2 * n_rows * P), 2 * n_rows, P)
    eps = k.view(m.take(1), 1)
    ready, zeroed = k.sem("l2_ready"), k.sem("l2_zeroed")
    squared, summed, rooted, inverted, wide, scaled = (k.sem("l2_" + n) for n in ("squared", "summed", "rooted", "inverted", "wide", "scaled"))
    with nc.Block() as block:
        @block.gpsimd
        def _(pool):
            for part in range(2):
                at = part * KEY_ROW
                pool.tensor_copy(spread[0:rows, part * n_rows:(part + 1) * n_rows, :],
                                 k.c["ident"][0:rows, at:at + n_rows].unsqueeze(2).to_broadcast([rows, n_rows, P])).then_inc(ready, 1)

        @block.scalar
        def _(act):
            for n, (src, w, row) in enumerate(items):
                if n >= 4:
                    act.wait_ge(summed, n - 3)
                act.activation(sq[n % 4][:, 0:w], src, ACT.Square).then_inc(squared, 1)
            act.wait_ge(summed, len(items))
            act.wait_ge(zeroed, 6)
            act.activation(root[0:rows, :], k.psum[0][0:rows, :], ACT.Sqrt, bias=eps[0:rows, :]).then_inc(rooted, 1)

        @block.tensor
        def _(pe):
            pe.wait_ge(zeroed, 6)
            for n, (src, w, row) in enumerate(items):
                pe.wait_ge(squared, n + 1)
                one = pick[row // KEY_ROW][:, rows - 1 - row:2 * rows - 1 - row]
                pe.matmul(k.psum[0][0:rows, 0:w], one, sq[n % 4][:, 0:w], start=(n == 0), stop=(n == len(items) - 1)).then_inc(summed, 1)
            pe.wait_ge(inverted, 1)
            pe.wait_ge(ready, 2)
            for n, (src, w, row) in enumerate(items):
                if n >= 4:
                    pe.wait_ge(scaled, n - 3)
                pe.matmul(k.psum[1 + n % 4][:, 0:w], spread[0:rows, row // KEY_ROW * n_rows + row % KEY_ROW, :], inv[0:rows, 0:w],
                          start=True, stop=True).then_inc(wide, 1)

        @block.vector
        def _(dve):
            for part in range(2):
                dve.memset(pick[part], 0.0).then_inc(zeroed, 1)
            dve.memset(eps[0:KEY_ROW, :], EPS * DK).then_inc(zeroed, 1)
            dve.memset(eps[KEY_ROW:2 * KEY_ROW, :], EPS).then_inc(zeroed, 1)
            dve.wait_ge(zeroed, 2)
            for part in range(2):
                dve.memset(pick[part][:, rows - 1:rows], 1.0 if part else float(DK)).then_inc(zeroed, 1)
            dve.wait_ge(rooted, 1)
            dve.reciprocal(inv[0:rows, :], root[0:rows, :]).then_inc(inverted, 1)
            for n, (src, w, row) in enumerate(items):
                dve.wait_ge(wide, n + 1)
                dve.tensor_tensor(src, src, k.psum[1 + n % 4][:, 0:w], ALU.mult).then_inc(scaled, 1)


def stage_gates(k):
    nc = k.nc
    m = Map(k.gdn_at)
    k.AQ = [k.view(m.take(512), G, P) for _ in range(NT + 1)]
    k.KD = [k.view(m.take(512), G, P) for _ in range(NT + 1)]
    k.uS = k.view(m.take(512), G, P)
    n = (NT + 1) * G
    k.decay_sum, k.gcb, k.ngc, k.egc, k.ebc, k.ekd, k.egl, k.gl, k.t1 = (k.view(m.take(n), NT + 1, G) for _ in range(9))
    k.gb = k.view(m.take(DB * G), DB, G)
    k.eglS = k.view(m.take(DB * G), DB * G)
    k.temp_at = (m.take(8 * 512), k.hT_at)
    k.sc_spare = m.take(3 * 512 + 3 * n)
    assert m.at <= k.words, m.at
    g, beta, lnb = (k.gates[:, i, :].rearrange("p (t h) -> p t h", h=G) for i in range(3))
    summed, base, diff, done = k.sem("gt_summed"), k.sem("gt_base"), k.sem("gt_diff"), k.sem("gt_exp")
    np_ = NT * G
    flat = lambda x: x.rearrange("p t h -> p (t h)")
    with nc.Block() as block:
        @block.tensor
        def _(pe):
            gf = flat(g)
            pe.matmul(k.psum[0][:, 0:np_], k.c["tri"], gf[:, 0:np_], start=True, stop=True)
            pe.matmul(k.psum[0][:, np_:n], k.c["tri_s"], gf[:, np_:n], start=True, stop=True)
            pe.matmul(k.psum[1][:, 0:np_], k.c["ones"], gf[:, 0:np_], start=True, stop=True)
            pe.matmul(k.psum[1][:, np_:n], k.c["block_s"], gf[:, np_:n], start=True, stop=True)
            pe.wait_ge(base, 1)
            pe.matmul(k.psum[2][:, 0:DB * G], k.c["ones"][0:NS, :], k.gb[0:NS].rearrange("p b h -> p (b h)"), start=True, stop=True).then_inc(summed, 1)

        @block.vector
        def _(dve):
            dve.tensor_tensor(k.gb[0:NS], k.c["in_batch"][0:NS].unsqueeze(2).to_broadcast([NS, DB, G]),
                              g[0:NS, NT:NT + 1, :].to_broadcast([NS, DB, G]), ALU.mult).then_inc(base, 1)
            dve.wait_ge(summed, 1)
            dve.tensor_copy(flat(k.decay_sum), k.psum[0][:, 0:n]).then_inc(base, 1)
            dve.tensor_copy(flat(k.gl), k.psum[1][:, 0:n]).then_inc(base, 1)
            dve.wait_ge(base, 3)
            dve.tensor_tensor(flat(k.gcb), flat(k.decay_sum), flat(lnb), ALU.add).then_inc(diff, 1)
            dve.tensor_scalar(flat(k.ngc), flat(k.decay_sum), -1.0, None, ALU.mult).then_inc(diff, 1)
            dve.tensor_tensor(flat(k.t1), flat(k.gl), flat(k.decay_sum), ALU.subtract).then_inc(diff, 1)
            dve.wait_ge(done, 1)
            dve.tensor_tensor(flat(k.ebc), flat(k.egc), flat(beta), ALU.mult)

        @block.scalar
        def _(act):
            act.wait_ge(diff, 3)
            act.activation(flat(k.egc), flat(k.decay_sum), ACT.Exp).then_inc(done, 1)
            act.activation(flat(k.egl), flat(k.gl), ACT.Exp)
            act.activation(flat(k.ekd), flat(k.t1), ACT.Exp)
            act.activation(k.eglS, k.psum[2][:, 0:DB * G], ACT.Exp)


PAIRS = [(0, 1), (2, 3), (4, 5), (6, 7), (8,)]


def stage_chunks(k):
    nc = k.nc
    S = 2
    t_at = [Map(at) for at in k.temp_at]
    kbe, vb, Lm, X, TG = ([k.view(m.take(512), G, P) for m in t_at] for _ in range(5))
    ZM = [k.view(m.take(1024), 2 * G, P) for m in t_at]
    beta = k.gates[:, 1, :].rearrange("p (t h) -> p t h", h=G)
    g = k.gates[:, 0, :].rearrange("p (t h) -> p t h", h=G)
    names = ("spread", "turned", "decay", "kept", "gram", "built", "init", "x_made", "masked", "y_made", "grown", "solved", "left")
    (spread, turned, decay, kept, gram, built, init, x_made, masked, y_made, grown, solved, left) = (k.sems("ch_" + n, S) for n in names)
    decayed = k.sems("ch_decayed", S)
    levels = lambda t: LEVELS if t < NT else S_LEVELS
    steps = LEVELS

    def bank(s, i, r):
        return k.psum[4 * s + i].rearrange("p (h n) -> p h n", h=G)[0:r, :, 0:r]

    with nc.Block() as block:
        @block.tensor
        def _(pe):
            for i, pair in enumerate(PAIRS):
                for s, t in enumerate(pair):
                    r = rows_of(t)
                    if i:
                        pe.wait_ge(left[s], 2 * i)
                    for part, b in ((1, 0), (2, 1)):
                        for h in range(G):
                            last = pe.transpose(k.psum[4 * s + b][0:r, h * P:(h + 1) * P], gdn_view(k, t, part)[:, h, :], k.c["ident"])
                    last.then_inc(turned[s], 1)
                    pe.wait_ge(spread[s], i + 1)
                    for b, mask in ((2, "low_big"), (3, "up_big")):
                        mask = k.b[mask if t < NT else mask + "_s"][0:r, 0:r].unsqueeze(1).to_broadcast([r, G, r])
                        pe.matmul(bank(s, b, r), k.c["ones"][0:r, 0:r], TG[s][0:r, :, 0:r], start=True, stop=False)
                        last = pe.matmul(bank(s, b, r), k.b["ident"][0:r, 0:r], mask, start=False, stop=True)
                    last.then_inc(decay[s], 1)
                for s, t in enumerate(pair):
                    r = rows_of(t)
                    pe.wait_ge(kept[s], i + 1)
                    kT, qT = gdn_view(k, t, 1), gdn_view(k, t, 0)
                    for h in range(G):
                        pe.matmul(bank(s, 0, r)[:, h, :], kT[:, h, :], kT[:, h, :], start=True, stop=True)
                    for h in range(G):
                        last = pe.matmul(bank(s, 1, r)[:, h, :], kT[:, h, :], qT[:, h, :], start=True, stop=True)
                    last.then_inc(gram[s], 1)
                for l in range(steps):
                    for s, t in enumerate(pair):
                        if l >= levels(t):
                            continue
                        r = rows_of(t)
                        if l == 0:
                            pe.wait_ge(built[s], i + 1)
                            pe.wait_ge(init[s], i + 1)
                        else:
                            pe.wait_ge(grown[s], LEVELS * i + l)
                        for h in range(G):
                            last = pe.matmul(bank(s, 2, r)[:, h, :], Lm[s][0:r, h, 0:r], ZM[s][0:r, h, 0:r], start=True, stop=True)
                        last.then_inc(x_made[s], 1)
                    for s, t in enumerate(pair):
                        if l >= levels(t):
                            continue
                        r = rows_of(t)
                        pe.wait_ge(masked[s], LEVELS * i + l + 1)
                        for h in range(G):
                            last = pe.matmul(bank(s, 0, r)[:, h, :], ZM[s][0:r, G + h, 0:r], X[s][0:r, h, 0:r], start=True, stop=True)
                        if l < levels(t) - 1:
                            for h in range(G):
                                last = pe.matmul(bank(s, 1, r)[:, h, :], X[s][0:r, h, 0:r], ZM[s][0:r, G + h, 0:r], start=True, stop=True)
                        last.then_inc(y_made[s], 1)
                for s, t in enumerate(pair):
                    r = rows_of(t)
                    pe.wait_ge(grown[s], LEVELS * i + levels(t))
                    for h in range(G):
                        pe.matmul(k.psum[4 * s + 2][0:r, h * P:(h + 1) * P], ZM[s][0:r, h, 0:r], vb[s][0:r, h, :], start=True, stop=True)
                    for h in range(G):
                        last = pe.matmul(k.psum[4 * s + 3][:, h * P:h * P + r], kbe[s][0:r, h, :], ZM[s][0:r, h, 0:r], start=True, stop=True)
                    last.then_inc(solved[s], 1)

        @block.scalar
        def _(act):
            for i, pair in enumerate(PAIRS):
                for s, t in enumerate(pair):
                    r = rows_of(t)
                    act.wait_ge(decay[s], i + 1)
                    for h in range(G):
                        act.activation(Lm[s][0:r, h, 0:r], bank(s, 2, r)[:, h, :], ACT.Exp, scale=-1.0, bias=k.gcb[0:r, t, h:h + 1])
                        last = act.activation(k.AQ[t][0:r, h, 0:r], bank(s, 3, r)[:, h, :], ACT.Exp, bias=k.ngc[0:r, t, h:h + 1])
                    last.then_inc(decayed[s], 1)
                for s, t in enumerate(pair):
                    r = rows_of(t)
                    act.wait_ge(solved[s], i + 1)
                    u = k.uS[0:NS] if t == NT else gdn_view(k, t, 2)
                    act.copy(u, k.psum[4 * s + 2][0:r, :].rearrange("p (h n) -> p h n", h=G)).then_inc(left[s], 1)
                    act.copy(gdn_view(k, t, 1), k.psum[4 * s + 3][:, :].rearrange("p (h n) -> p h n", h=G)[:, :, 0:r]).then_inc(left[s], 1)

        @block.gpsimd
        def _(pool):
            for i, pair in enumerate(PAIRS):
                for s, t in enumerate(pair):
                    if i:
                        pool.wait_ge(solved[s], i)
                    pool.tensor_copy(ZM[s], k.c["ident"].unsqueeze(1).to_broadcast([P, 2 * G, P])).then_inc(init[s], 1)

        @block.vector
        def _(dve):
            for i, pair in enumerate(PAIRS):
                for s, t in enumerate(pair):
                    r = rows_of(t)
                    tri = k.c["tri" if t < NT else "tri_s"][0:r, 0:r].unsqueeze(1).to_broadcast([r, G, r])
                    if i:
                        dve.wait_ge(decay[s], i)
                    dve.tensor_tensor(TG[s][0:r, :, 0:r], tri, g[0:r, t, :].unsqueeze(2).to_broadcast([r, G, r]), ALU.mult).then_inc(spread[s], 1)
                for s, t in enumerate(pair):
                    r = rows_of(t)
                    wide = lambda x: x[0:r, t, :].unsqueeze(2).to_broadcast([r, G, P])
                    kk, vv = (k.psum[4 * s + b][0:r, :].rearrange("p (h n) -> p h n", h=G) for b in (0, 1))
                    dve.wait_ge(turned[s], i + 1)
                    if i:
                        dve.wait_ge(solved[s], i)
                    dve.tensor_tensor(kbe[s][0:r], kk, wide(k.ebc), ALU.mult)
                    dve.tensor_tensor(k.KD[t][0:r], kk, wide(k.ekd), ALU.mult)
                    dve.tensor_tensor(vb[s][0:r], vv, wide(beta), ALU.mult).then_inc(kept[s], 1)
                for s, t in enumerate(pair):
                    r = rows_of(t)
                    dve.wait_ge(gram[s], i + 1)
                    dve.wait_ge(decayed[s], i + 1)
                    L, A = Lm[s][0:r, :, 0:r], k.AQ[t][0:r, :, 0:r]
                    dve.tensor_tensor(L, bank(s, 0, r), L, ALU.mult)
                    dve.tensor_tensor(A, bank(s, 1, r), A, ALU.mult).then_inc(built[s], 1)
                for l in range(steps):
                    for s, t in enumerate(pair):
                        if l >= levels(t):
                            continue
                        r = rows_of(t)
                        dve.wait_ge(x_made[s], LEVELS * i + l + 1)
                        mask = k.b["level"][0:r, l * P:l * P + r].unsqueeze(1).to_broadcast([r, G, r])
                        dve.tensor_tensor(X[s][0:r, :, 0:r], bank(s, 2, r), mask, ALU.mult).then_inc(masked[s], 1)
                    for s, t in enumerate(pair):
                        if l >= levels(t):
                            continue
                        r = rows_of(t)
                        n = G if l == levels(t) - 1 else 2 * G
                        dve.wait_ge(y_made[s], LEVELS * i + l + 1)
                        if l == 0:
                            dve.wait_ge(init[s], i + 1)
                        zm = ZM[s][0:r, 0:n, 0:r]
                        y = k.banks[0:r, 4 * s * 512:4 * s * 512 + n * P].rearrange("p (h n) -> p h n", h=n)[:, :, 0:r]
                        dve.tensor_tensor(zm, zm, y, ALU.add).then_inc(grown[s], 1)


def stage_scan(k):
    nc, a = k.nc, k.a
    mix = k.view(k.hT_at, KD, TOK)
    z = k.view(k.z_at, NT, G, DK)
    zS = k.psZ[0:NS, :].rearrange("p (h d) -> p h d", h=G)
    m = Map(k.temp_at[0])
    S0 = k.view(m.take(DB * G * DK), DB * G, DK)
    m = Map(k.temp_at[1])
    S = [k.view(m.take(512), G, DK) for _ in range(2)]
    vnew = [k.view(m.take(512), G, DK) for _ in range(2)]
    o = [k.view(m.take(512), G, DK) for _ in range(2)]
    sq = k.view(m.take(512), G, DK)
    m = Map(k.temp_at[1])
    wTm = k.view(m.take(G * DB * NS), G, DB * NS)
    qTm = k.view(m.take(G * DB * NS), G, DB * NS)
    vnm = k.view(k.temp_at[1], G, DB * DK)
    m = Map(k.sc_spare)
    vS, oS, sqS = (k.view(m.take(512), G, DK) for _ in range(3))
    stat = k.view(m.take(3 * G * (NT + 1)), 3, (NT + 1) * G)
    fade, fadeS = k.sem("sc_fade"), k.sem("sc_fadeS")
    names = ("ws", "qs", "vnew", "av", "kv", "state", "scaled", "out", "sq", "sum", "root", "inv", "norm", "gated", "turned", "kept")
    (ws, qs, vn, av, kv, state, faded, outs, sqd, sm, root, inv, normed, gated, turned, kept) = (k.sem("sc_" + n) for n in names)
    landed, out_sem = k.sem("sc_landed"), k.stored["ssm"]
    mask_sem, vm_sem, kvS, addS = k.sem("sc_mask"), k.sem("sc_vmask"), k.sem("sc_kvS"), k.sem("sc_addS")
    heads = lambda b: b.rearrange("p (h n) -> p h n", h=G)
    n_all = NT + 1
    with nc.Block() as block:
        @block.sync
        def _(sp):
            sp.dma_start(S0, a["state_ssm"][0].rearrange("b h k v -> k (b h) v")).then_inc(landed, 16)
            sp.wait_ge(state, NT + 1)
            sp.dma_start(a["new_ssm_prompt"][0, 0].rearrange("h k v -> k h v"), S[NT % 2]).then_inc(out_sem, 16)
            sp.wait_ge(addS, 2 * G)
            sp.dma_start(a["new_ssm_sample"][0].rearrange("b h k v -> k (b h) v"), S0).then_inc(out_sem, 16)
            sp.wait_ge(out_sem, 32)

        @block.tensor
        def _(pe):
            def turn(t):
                r = rows_of(t)
                src = o[t % 2] if t < NT else oS
                pe.wait_ge(gated, t + 1)
                if t:
                    pe.wait_ge(kept, t)
                for h in range(G):
                    last = pe.transpose(k.psum[7][:, h * P:h * P + r], src[0:r, h, :], k.c["ident"][0:r, 0:r])
                last.then_inc(turned, 1)

            for t in range(NT):
                pe.wait_ge(state, t + 1)
                for h in range(G):
                    last = pe.matmul(heads(k.psum[0])[:, h, :], gdn_view(k, t, 1)[:, h, :], S[t % 2][:, h, :], start=True, stop=True)
                last.then_inc(ws, 1)
                if t:
                    pe.wait_ge(outs, t)
                for h in range(G):
                    last = pe.matmul(heads(k.psum[1])[:, h, :], gdn_view(k, t, 0)[:, h, :], S[t % 2][:, h, :], start=True, stop=True)
                last.then_inc(qs, 1)
                pe.wait_ge(vn, t + 1)
                for h in range(G):
                    last = pe.matmul(heads(k.psum[2])[:, h, :], k.KD[t][:, h, :], vnew[t % 2][:, h, :], start=True, stop=True)
                last.then_inc(kv, 1)
                for h in range(G):
                    last = pe.matmul(heads(k.psum[3])[:, h, :], k.AQ[t][:, h, :], vnew[t % 2][:, h, :], start=True, stop=True)
                last.then_inc(av, 1)
                if t:
                    turn(t - 1)
            turn(NT - 1)
            pe.wait_ge(landed, 16)
            pe.wait_ge(mask_sem, 1)
            for src, b0, sem in ((wTm, 4, ws), (qTm, 5, qs)):
                for h in range(G):
                    for b in range(DB):
                        last = pe.matmul(k.psum[b0][0:NS, h * DK:(h + 1) * DK], src[:, h, b * NS:(b + 1) * NS], S0[:, b * G + h, :],
                                         start=(b == 0), stop=(b == DB - 1))
                last.then_inc(sem, 1)
            pe.wait_ge(vn, NT + 1)
            for h in range(G):
                last = pe.matmul(k.psum[6][0:NS, h * DK:(h + 1) * DK], k.AQ[NT][0:NS, h, 0:NS], vS[0:NS, h, :], start=True, stop=True)
            last.then_inc(av, 1)
            pe.wait_ge(vm_sem, 1)
            for n in range(2 * G):
                h, half = n // 2, n % 2
                if n >= 4:
                    pe.wait_ge(addS, n - 3)
                pe.matmul(k.psum[n % 4][:, :], k.KD[NT][0:NS, h, :], vnm[0:NS, h, half * 512:(half + 1) * 512],
                          start=True, stop=True).then_inc(kvS, 1)
            turn(NT)

        @block.scalar
        def _(act):
            for t in range(n_all):
                r = rows_of(t)
                act.wait_ge(sm, t + 1)
                act.activation(stat[0:r, 1, t * G:(t + 1) * G], stat[0:r, 0, t * G:(t + 1) * G], ACT.Sqrt, scale=1.0 / DK, bias=k.eps[0:r, :]).then_inc(root, 1)
                act.wait_ge(turned, t + 1)
                act.copy(mix[:, KD // 2:KD, t * P:t * P + r], heads(k.psum[7])[:, :, 0:r]).then_inc(kept, 1)

        @block.vector
        def _(dve):
            def output(t, q_bank, a_bank, out, sqr, zz):
                r = rows_of(t)
                wide = lambda x: x.unsqueeze(2).to_broadcast([r, G, DK])
                dve.wait_ge(qs, t + 1)
                if 2 <= t < NT:
                    dve.wait_ge(turned, t - 1)
                dve.tensor_tensor(out, heads(k.psum[q_bank])[0:r], wide(k.egc[0:r, t, :]), ALU.mult).then_inc(faded, 1)
                dve.wait_ge(av, t + 1)
                dve.wait_ge(faded, t + 1)
                dve.tensor_tensor(out, out, heads(k.psum[a_bank])[0:r], ALU.add).then_inc(outs, 1)
                dve.wait_ge(outs, t + 1)
                if t:
                    dve.wait_ge(sm, t)
                dve.tensor_tensor(sqr, out, out, ALU.mult).then_inc(sqd, 1)
                dve.wait_ge(sqd, t + 1)
                dve.reduce_sum(stat[0:r, 0, t * G:(t + 1) * G], sqr, AX_X).then_inc(sm, 1)
                dve.tensor_tensor(out, out, zz, ALU.mult).then_inc(normed, 1)
                dve.wait_ge(root, t + 1)
                dve.reciprocal(stat[0:r, 2, t * G:(t + 1) * G], stat[0:r, 1, t * G:(t + 1) * G]).then_inc(inv, 1)
                dve.wait_ge(inv, t + 1)
                dve.wait_ge(normed, t + 1)
                dve.tensor_tensor(out, out, wide(stat[0:r, 2, t * G:(t + 1) * G]), ALU.mult).then_inc(gated, 1)

            dve.memset(S[0], 0.0).then_inc(state, 1)
            for t in range(NT):
                old, new = S[t % 2], S[(t + 1) % 2]
                dve.wait_ge(state, t + 1)
                dve.tensor_tensor(new, old, k.egl[:, t, :].unsqueeze(2).to_broadcast([P, G, DK]), ALU.mult).then_inc(fade, 1)
                dve.wait_ge(ws, t + 1)
                if t >= 2:
                    dve.wait_ge(av, t - 1)
                dve.tensor_tensor(vnew[t % 2], gdn_view(k, t, 2), heads(k.psum[0]), ALU.subtract).then_inc(vn, 1)
                dve.wait_ge(kv, t + 1)
                dve.wait_ge(fade, t + 1)
                dve.tensor_tensor(new, new, heads(k.psum[2]), ALU.add).then_inc(state, 1)
                output(t, 1, 3, o[t % 2], sq, z[:, t])
            dve.wait_ge(turned, NT)
            dve.wait_ge(out_sem, 16)
            cm = k.b["columns"].rearrange("p (b n) -> p b n", b=DB)
            for h in range(G):
                for dst, part in ((wTm, 1), (qTm, 0)):
                    last = dve.tensor_tensor(dst[:, h, :].rearrange("p (b n) -> p b n", b=DB), cm,
                                             gdn_view(k, NT, part)[:, h, :].unsqueeze(1).to_broadcast([P, DB, NS]), ALU.mult)
            last.then_inc(mask_sem, 1)
            dve.wait_ge(ws, NT + 1)
            dve.tensor_tensor(vS[0:NS], k.uS[0:NS], heads(k.psum[4])[0:NS], ALU.subtract).then_inc(vn, 1)
            dve.wait_ge(vn, NT + 1)
            dve.wait_ge(qs, NT + 1)
            for h in range(G):
                last = dve.tensor_tensor(vnm[0:NS, h, :].rearrange("p (b d) -> p b d", b=DB),
                                         vS[0:NS, h, :].unsqueeze(1).to_broadcast([NS, DB, DK]),
                                         k.c["in_batch"][0:NS].unsqueeze(2).to_broadcast([NS, DB, DK]), ALU.mult)
            last.then_inc(vm_sem, 1)
            output(NT, 5, 6, oS[0:NS], sqS[0:NS], zS)
            S0v = S0.rearrange("p (b h) v -> p b h v", h=G)
            eg = k.eglS.rearrange("p (b h) -> p b h", h=G)
            for n in range(2 * G):
                h, half = n // 2, n % 2
                part = S0v[:, 4 * half:4 * half + 4, h, :]
                dve.wait_ge(kvS, n + 1)
                dve.tensor_tensor(part, part, eg[:, 4 * half:4 * half + 4, h].unsqueeze(2).to_broadcast([P, 4, DK]), ALU.mult).then_inc(fadeS, 1)
                dve.wait_ge(fadeS, n + 1)
                dve.tensor_tensor(part, part, k.psum[n % 4].rearrange("p (b v) -> p b v", b=4), ALU.add).then_inc(addS, 1)


KV_RING = 4


class PageStream:

    def __init__(self, k):
        self.k = k
        self.units = [(it, c, b2) for it in range(DB // 2) for c in range(NPG // 4) for b2 in range(2)]
        m = Map(k.kv_at)
        self.keys = [k.view(m.take(4 * AW), 4, AW) for _ in range(KV_RING)]
        self.values = [k.view(m.take(4 * AW), 4, AW) for _ in range(KV_RING)]
        assert m.at <= k.words
        self.keys_landed, self.values_landed = k.sems("sa_k_landed", KV_RING), k.sems("sa_v_landed", KV_RING)

    def load(self, q, n, cache, ring, sems):
        it, c, b2 = self.units[n]
        for p in range(4):
            at = (2 * it + b2) * NPG + 4 * c + p
            page = q.value_load(self.k.table[0:1, at:at + 1], min_val=0, max_val=cache.shape[1] - 1)
            src = cache[0, bass.ds(page, 1), :, :, :].rearrange("a p h d -> p (a h d)")
            q.dma_start(ring[n % KV_RING][:, p, :], src).then_inc(sems[n % KV_RING], 16)

    def load_keys(self, q, n):
        self.load(q, n, self.k.a["cache_k"], self.keys, self.keys_landed)

    def load_values(self, q, n):
        self.load(q, n, self.k.a["cache_v"], self.values, self.values_landed)


def stage_prompt_attention(k):
    nc, a = k.nc, k.a
    m = Map(k.xc_at)
    qT, kT = (k.view(m.take(4 * SEQ), 4, SEQ) for _ in range(2))
    V = k.view(m.take(NT * AW), NT, AW)
    m = Map(k.z_at)
    prob = [k.view(m.take(SEQ), SEQ) for _ in range(2)]
    probT = [k.view(m.take(SEQ), SEQ) for _ in range(2)]
    m = Map(k.free_at)
    stat = k.view(m.take(3 * NT * H), 3, NT * H)
    mix = k.view(k.hT_at, KD, TOK)
    items = [(t, h) for t in range(NT) for h in range(H)]
    q_in, k_in, v_in = k.sem("pa_q_landed"), k.sem("pa_k_landed"), k.sem("pa_v_landed")
    names = ("q_scaled", "scores", "max", "exp", "inv", "scaled", "turned", "kept", "made", "out")
    q_scaled, scores, maxed, exped, inverted, scaled, turned, kept, made, out = (k.sem("pa_" + n) for n in names)
    n_items = len(items)
    k.stream = PageStream(k)
    with nc.Block() as block:
        @block.sync
        def _(sp):
            sp.dma_start(qT, a["q_T"].rearrange("(f p) n -> p f n", p=P)).then_inc(q_in, 16)
            sp.dma_start(kT, a["k_T"].rearrange("(f p) n -> p f n", p=P)).then_inc(k_in, 16)
            sp.dma_start(V, a["new_v_prompt"][0, 0].rearrange("t h d -> t (h d)").rearrange("(t p) n -> p t n", p=P)).then_inc(v_in, 16)
            for n in range(KV_RING):
                k.stream.load_keys(sp, n)

        @block.gpsimd
        def _(pool):
            pool.wait_ge(q_in, 16)
            for f in range(4):
                pool.tensor_scalar(qT[:, f, :], qT[:, f, :], HD ** -0.5, None, ALU.mult).then_inc(q_scaled, 1)
            for n in range(KV_RING):
                k.stream.load_values(pool, n)

        @block.tensor
        def _(pe):
            def score(n):
                t, h = items[n]
                lo = (h % 2) * HD
                if n >= 2:
                    pe.wait_ge(exped, n - 1)
                for c in range(0, (t + 1) * P, 512):
                    w = min(512, (t + 1) * P - c)
                    bank = k.psum[2 * (n % 2) + c // 512]
                    pe.matmul(bank[:, 0:w], qT[lo:lo + HD, h // 2, t * P:(t + 1) * P], kT[lo:lo + HD, h // 2, c:c + w], start=True, stop=False)
                    if t < FIRST_SEL:
                        last = pe.matmul(bank[:, t * P:(t + 1) * P], k.b["ident"], k.b["attn_causal"], start=False, stop=True)
                    else:
                        last = pe.matmul(bank[:, 0:w], k.b["ident"], k.maskP[t][:, c:c + w], start=False, stop=True)
                last.then_inc(scores, 1)

            def turn(n):
                t, h = items[n]
                pe.wait_ge(scaled, n + 1)
                if n:
                    pe.wait_ge(kept, n)
                for j in range(t + 1):
                    last = pe.transpose(k.psum[4 + j // 4][:, (j % 4) * P:(j % 4 + 1) * P], prob[n % 2][:, j * P:(j + 1) * P], k.c["ident"])
                last.then_inc(turned, 1)

            def values(n):
                t, h = items[n]
                lo = (h % 2) * HD
                pe.wait_ge(kept, n + 1)
                if n >= 2:
                    pe.wait_ge(out, n - 1)
                for j in range(t + 1):
                    last = pe.matmul(k.psum[6 + n % 2][lo:lo + HD, 0:P], V[:, j, h * HD:(h + 1) * HD], probT[n % 2][:, j * P:(j + 1) * P],
                                     start=(j == 0), stop=(j == t))
                last.then_inc(made, 1)

            pe.wait_ge(q_scaled, 4)
            pe.wait_ge(k_in, 16)
            score(0)
            score(1)
            pe.wait_ge(v_in, 16)
            for n in range(n_items):
                turn(n)
                if n + 2 < n_items:
                    score(n + 2)
                values(n)

        @block.scalar
        def _(act):
            def exps(n):
                t, h = items[n]
                w = (t + 1) * P
                b0 = 2 * (n % 2) * 512
                act.wait_ge(maxed, n + 1)
                if n >= 2:
                    act.wait_ge(turned, n - 1)
                act.activation(prob[n % 2][:, 0:w], k.banks[:, b0:b0 + w], ACT.Exp, bias=stat[:, 0, n:n + 1],
                               accum_out=stat[:, 1, n:n + 1]).then_inc(exped, 1)

            exps(0)
            exps(1)
            for n in range(n_items):
                w = (items[n][0] + 1) * P
                act.wait_ge(turned, n + 1)
                if n >= 2:
                    act.wait_ge(made, n - 1)
                act.copy(probT[n % 2][:, 0:w], k.banks[:, 4 * 512:4 * 512 + w]).then_inc(kept, 1)
                if n + 2 < n_items:
                    exps(n + 2)

        @block.vector
        def _(dve):
            def maxes(n):
                w = (items[n][0] + 1) * P
                b0 = 2 * (n % 2) * 512
                dve.wait_ge(scores, n + 1)
                dve.tensor_reduce(stat[:, 0, n:n + 1], k.banks[:, b0:b0 + w], AX_X, ALU.max, negate=True).then_inc(maxed, 1)

            def keep(n):
                t, h = items[n]
                lo = (h % 2) * HD
                dve.wait_ge(made, n + 1)
                dve.tensor_copy(mix[lo:lo + HD, h // 2, t * P:(t + 1) * P], k.psum[6 + n % 2][lo:lo + HD, 0:P]).then_inc(out, 1)

            def scale(n):
                w = (items[n][0] + 1) * P
                dve.wait_ge(exped, n + 1)
                dve.reciprocal(stat[:, 2, n:n + 1], stat[:, 1, n:n + 1]).then_inc(inverted, 1)
                dve.wait_ge(inverted, n + 1)
                dve.tensor_scalar(prob[n % 2][:, 0:w], prob[n % 2][:, 0:w], stat[:, 2, n:n + 1], None, ALU.mult).then_inc(scaled, 1)

            maxes(0)
            maxes(1)
            scale(0)
            for n in range(n_items):
                if n + 1 < n_items:
                    scale(n + 1)
                if n + 2 < n_items:
                    maxes(n + 2)
                keep(n)


def stage_sample_attention(k):
    nc, a = k.nc, k.a
    IT = DB // 2
    NCH = NPG // 4
    m = Map(k.xc_at)
    kp, vp = k.stream.keys, k.stream.values
    kts = [k.view(m.take(4 * 512), 4, 512) for _ in range(2)]
    S = [k.view(m.take(LS), LS) for _ in range(2)]
    PT = k.view(m.take((NPG + 1) * P), NPG + 1, P)
    qblk = k.view(m.take(DB * 4 * 64), DB * 4, 64)
    ktn = k.view(m.take(4 * NS), 4, NS)
    osb = k.view(m.take(512), 512)
    stat = k.view(m.take(3 * IT), 3, IT)
    assert m.at <= k.kv_at
    mix = k.view(k.hT_at, KD, TOK)
    kl, vl = k.stream.keys_landed, k.stream.values_landed
    names = ("zero", "prep_pe", "prep", "k_turned", "kept_act", "kept_dve", "qk", "scores", "copied", "max", "exp", "inv",
             "p_turned", "p_kept", "v_used", "out", "out_kept", "o_turned", "laid")
    (zero, prep_pe, prep, k_turned, kept_a, kept_v, qk, scores, copied, maxed, exped, inverted, p_turned,
     p_kept, v_used, out, out_kept, o_turned, laid) = (k.sem("sa_" + n) for n in names)
    loads = k.stream.units
    PG = NCH + 1
    U = 2 * NCH

    with nc.Block() as block:
        @block.sync
        def _(sp):
            for n in range(KV_RING, len(loads)):
                sp.wait_ge(k_turned, 4 * (n - KV_RING + 1))
                k.stream.load_keys(sp, n)

        @block.gpsimd
        def _(pool):
            pool.memset(qblk, 0.0).then_inc(zero, 1)
            for n in range(KV_RING, len(loads)):
                pool.wait_ge(v_used, n - KV_RING + 1)
                k.stream.load_values(pool, n)

        @block.tensor
        def _(pe):
            for p in range(4):
                pe.transpose(k.psum[6][:, p * NS:(p + 1) * NS], k.psA[0:NS, p * P:(p + 1) * P], k.c["ident"][0:NS, 0:NS])
            for p in range(4):
                last = pe.transpose(k.psum[7][:, p * NS:(p + 1) * NS], k.psA[0:NS, AW + p * P:AW + (p + 1) * P], k.c["ident"][0:NS, 0:NS])
            last.then_inc(prep_pe, 1)
            pe.wait_ge(prep, 9)

            def turn(n):
                pe.wait_ge(kl[n % KV_RING], 64 * (n // KV_RING + 1))
                for p in range(4):
                    if n:
                        pe.wait_ge((kept_a, kept_v)[p % 2], 2 * (n - 1) + p // 2 + 1)
                    for j in range(4):
                        last = pe.transpose(k.psum[p][:, j * PAGE:(j + 1) * PAGE], kp[n % KV_RING][:, j, p * P:(p + 1) * P], k.c["ident"])
                    last.then_inc(k_turned, 1)

            def mask_rows(it, b2):
                at = it * P + b2 * 64
                return k.b["sel_at"][0:NS, at:at + 64]

            def product(n):
                it, c, b2 = loads[n]
                i = it * (NCH + 1) + c
                bank = k.psum[4 + i % 2]
                pe.wait_ge(kept_a, 2 * (n + 1))
                pe.wait_ge(kept_v, 2 * (n + 1))
                if b2 == 0 and i >= 2:
                    pe.wait_ge(copied, i - 1)
                rows = bank[b2 * 64:(b2 + 1) * 64, :]
                pe.matmul(rows, mask_rows(it, b2), k.maskS[0:NS, c * 512:(c + 1) * 512], start=True, stop=False)
                for p in range(4):
                    last = pe.matmul(rows, qblk[:, (2 * it + b2) * 4 + p, :], kts[n % 2][:, p, :], start=False, stop=(p == 3))
                last.then_inc(qk, 1)

            def new_keys(it):
                i = it * (NCH + 1) + NCH
                bank = k.psum[4 + i % 2]
                if i >= 2:
                    pe.wait_ge(copied, i - 1)
                for b2 in range(2):
                    rows = bank[b2 * 64:(b2 + 1) * 64, 0:NS]
                    pe.matmul(rows, mask_rows(it, b2), k.maskS[0:NS, PAST:LS], start=True, stop=False)
                    for p in range(4):
                        last = pe.matmul(rows, qblk[:, (2 * it + b2) * 4 + p, :], ktn[:, p, :], start=False, stop=(p == 3))
                last.then_inc(scores, 1)

            def turn_weights(it, g):
                n = it * PG + g
                if g == 0:
                    pe.wait_ge(exped, it + 1)
                    if it:
                        pe.wait_ge(laid, 8 * it)
                if n:
                    pe.wait_ge(p_kept, n)
                for j in range(4 * g, min(4 * g + 4, NPG + 1)):
                    w = PAGE if j < NPG else NS
                    last = pe.transpose(k.psum[7][0:w, (j % 4) * P:(j % 4 + 1) * P], S[it % 2][:, j * P:j * P + w], k.c["ident"])
                last.then_inc(p_turned, 1)

            def values(it, u):
                c, b2 = u // 2, u % 2
                n = it * U + u
                if u == 0 and it:
                    pe.wait_ge(out_kept, it)
                pe.wait_ge(vl[n % KV_RING], 64 * (n // KV_RING + 1))
                pe.wait_ge(p_kept, it * PG + c + 1)
                for j in range(4):
                    last = pe.matmul(k.psum[6][b2 * 64:(b2 + 1) * 64, :], PT[:, 4 * c + j, b2 * 64:(b2 + 1) * 64], vp[n % KV_RING][:, j, :],
                                     start=(c == 0 and j == 0), stop=False)
                last.then_inc(v_used, 1)

            def turn_output(it):
                pe.wait_ge(p_kept, PG * (it + 1))
                pe.wait_ge(out_kept, it + 1)
                for p in range(4):
                    last = pe.transpose(k.psum[7][:, p * P:(p + 1) * P], osb[:, p * P:(p + 1) * P], k.c["ident"])
                last.then_inc(o_turned, 1)

            def values_step(it, u):
                if u == 0 and it:
                    turn_output(it - 1)
                if u >= 2:
                    values(it, u - 2)
                if u % 2:
                    turn_weights(it, u // 2)
                if u == U - 1:
                    values(it, U - 2)
                    values(it, U - 1)
                    turn_weights(it, NCH)
                    pe.wait_ge(p_kept, PG * (it + 1))
                    for b2 in range(2):
                        last = pe.matmul(k.psum[6][b2 * 64:(b2 + 1) * 64, :], PT[0:NS, NPG, b2 * 64:(b2 + 1) * 64], k.psA[0:NS, 2 * AW:3 * AW],
                                         start=False, stop=True)
                    last.then_inc(out, 1)

            turn(0)
            for n in range(len(loads)):
                it, u = n // U, n % U
                if n + 1 < len(loads):
                    turn(n + 1)
                product(n)
                if u == U - 1:
                    new_keys(it)
                if it:
                    values_step(it - 1, u)
            for u in range(U):
                values_step(IT - 1, u)
            turn_output(IT - 1)

        def keep_keys(eng, copy, mine, sem, n):
            for p in mine:
                eng.wait_ge(k_turned, 4 * n + p + 1)
                if n >= 2:
                    eng.wait_ge(qk, n - 1)
                copy(kts[n % 2][:, p, :], k.psum[p][:, :]).then_inc(sem, 1)

        @block.scalar
        def _(act):
            def scores_out(it, c):
                i = it * (NCH + 1) + c
                if c < NCH:
                    act.wait_ge(qk, it * 2 * NCH + 2 * c + 2)
                else:
                    act.wait_ge(scores, it + 1)
                if it >= 2 and c == 0:
                    act.wait_ge(p_turned, PG * (it - 1))
                w = 512 if c < NCH else NS
                act.copy(S[it % 2][:, c * 512:c * 512 + w], k.psum[4 + i % 2][:, 0:w]).then_inc(copied, 1)

            keep_keys(act, act.copy, (0, 2), kept_a, 0)
            for n in range(len(loads)):
                it, u = n // U, n % U
                if n + 1 < len(loads):
                    keep_keys(act, act.copy, (0, 2), kept_a, n + 1)
                if u % 2:
                    scores_out(it, u // 2)
                if u == U - 1:
                    scores_out(it, NCH)
                    act.wait_ge(maxed, it + 1)
                    act.activation(S[it % 2], S[it % 2], ACT.Exp, bias=stat[:, 0, it:it + 1], accum_out=stat[:, 1, it:it + 1]).then_inc(exped, 1)

        @block.vector
        def _(dve):
            dve.wait_ge(prep_pe, 1)
            dve.wait_ge(zero, 1)
            for h in range(H):
                lo, p = (h % 2) * HD, h // 2
                dst = qblk.rearrange("d (b p) n -> d b p n", p=4)[lo:lo + HD, :, p, h * DS:(h + 1) * DS]
                dve.tensor_scalar(dst, k.psum[6][lo:lo + HD, p * NS:(p + 1) * NS].rearrange("d (b q) -> d b q", b=DB),
                                  HD ** -0.5, None, ALU.mult).then_inc(prep, 1)
            dve.tensor_copy(ktn.rearrange("p a n -> p (a n)"), k.psum[7][:, 0:4 * NS]).then_inc(prep, 1)

            def keep_weights(it, g):
                dve.wait_ge(p_turned, it * PG + g + 1)
                if g == 0 and it:
                    dve.wait_ge(out, it)
                if g < NCH:
                    dve.tensor_copy(PT[:, 4 * g:4 * g + 4, :].rearrange("p a n -> p (a n)"), k.psum[7][:, :]).then_inc(p_kept, 1)
                else:
                    dve.tensor_copy(PT[0:NS, NPG, :], k.psum[7][0:NS, 0:P]).then_inc(p_kept, 1)

            def lay_output(it):
                dve.wait_ge(o_turned, it + 1)
                for h in range(H):
                    lo, p = (h % 2) * HD, h // 2
                    src = k.psum[7][lo:lo + HD, p * P:(p + 1) * P].rearrange("d (b n) -> d b n", b=2)[:, :, h * DS:(h + 1) * DS]
                    dst = mix[lo:lo + HD, p, SEQ + it * 2 * DS:SEQ + (it + 1) * 2 * DS].rearrange("d (b q) -> d b q", b=2)
                    dve.tensor_copy(dst, src).then_inc(laid, 1)

            def values_step(it, u):
                if u == 0:
                    dve.wait_ge(exped, it + 1)
                    dve.reciprocal(stat[:, 2, it:it + 1], stat[:, 1, it:it + 1]).then_inc(inverted, 1)
                    if it:
                        lay_output(it - 1)
                if u % 2:
                    keep_weights(it, u // 2)
                if u == U - 1:
                    keep_weights(it, NCH)
                    dve.wait_ge(out, it + 1)
                    dve.wait_ge(inverted, it + 1)
                    if it:
                        dve.wait_ge(o_turned, it)
                    dve.tensor_scalar(osb, k.psum[6][:, :], stat[:, 2, it:it + 1], None, ALU.mult).then_inc(out_kept, 1)

            keep_keys(dve, dve.tensor_copy, (1, 3), kept_v, 0)
            for n in range(len(loads)):
                it, u = n // U, n % U
                if n + 1 < len(loads):
                    keep_keys(dve, dve.tensor_copy, (1, 3), kept_v, n + 1)
                if it:
                    values_step(it - 1, u)
                if u == U - 1:
                    dve.wait_ge(copied, PG * (it + 1))
                    dve.tensor_reduce(stat[:, 0, it:it + 1], S[it % 2], AX_X, ALU.max, negate=True).then_inc(maxed, 1)
            for u in range(U):
                values_step(IT - 1, u)
            lay_output(IT - 1)


def split_product(pe, out, left, right, start, stop):
    (lh, ll), (rh, rl) = left, right
    pe.matmul(out, lh, rh, start=start, stop=False)
    pe.matmul(out, lh, rl, start=False, stop=False)
    return pe.matmul(out, ll, rh, start=False, stop=stop)


def stage_output_projection(k):
    nc, a = k.nc, k.a
    mix = k.view(k.hT_at, KD, TOK)
    w_sem = k.sems("op_w_landed", 4)
    x_landed = k.sem("op_x_landed")
    mix_hi, mix_lo, w_hi, w_lo, made, used, added = (k.sem("op_" + n) for n in
                                                     ("mix_rounded", "mix_rest", "w_rounded", "w_rest", "made", "w_used", "added"))
    xp = a["x_prompt"][0].rearrange("(t p) d -> p t d", p=P)
    xs = a["x_sample"].rearrange("b t d -> (b t) d")
    wv = a["w_out"][0].rearrange("(k p) n -> p k n", p=P)
    parts = [(i, f) for i in range(2) for f in range(KD)]
    with (nc.sbuf_tensor("op_raw", [P, 4, 512], F32) as raw, nc.sbuf_tensor("op_w_hi", [P, KD, 512], F32R) as whi,
          nc.sbuf_tensor("op_w_lo", [P, KD, 512], F32R) as wlo, nc.sbuf_tensor("op_sample_hi", [P, KD, NS], F32R) as shi,
          nc.sbuf_tensor("op_sample_lo", [P, KD, NS], F32R) as slo, nc.Block() as block):
        @block.sync
        def _(sp):
            for n, (i, f) in enumerate(parts):
                if n >= 4:
                    sp.wait_ge(w_lo, n - 3)
                sp.dma_start(raw[:, n % 4, :], wv[:, f, i * 512:(i + 1) * 512]).then_inc(w_sem[n % 4], 16)
                if n == 3:
                    sp.dma_start(k.x2[:, 0:NT, :], xp).then_inc(x_landed, 16)
                    sp.dma_start(k.x2[0:NS, NT, :], xs).then_inc(x_landed, 16)

        @block.tensor
        def _(pe):
            for i in range(2):
                for f in range(KD):
                    pe.wait_ge(w_lo, i * KD + f + 1)
                    if i == 0:
                        pe.wait_ge(mix_lo, f + 1)
                    elif f == 0:
                        pe.wait_ge(added, NT + 1)
                    for t in range(NT):
                        cols = slice(t * P, (t + 1) * P)
                        last = split_product(pe, k.psum[t], (k.h_hi[:, f, cols], k.h_lo[:, f, cols]), (whi[:, f, :], wlo[:, f, :]),
                                             f == 0, f == KD - 1)
                        if f == KD - 1:
                            last.then_inc(made, 1)
                pe.wait_ge(added, i * (NT + 1) + 1)
                for f in range(KD):
                    split_product(pe, k.psum[0][0:NS, :], (shi[:, f, :], slo[:, f, :]), (whi[:, f, :], wlo[:, f, :]),
                                  f == 0, f == KD - 1).then_inc(used, 1)

        @block.scalar
        def _(act):
            for n, (i, f) in enumerate(parts):
                if i == 0:
                    act.copy(shi[:, f, :], mix[:, f, SEQ:TOK])
                    act.copy(k.h_hi[:, f, :], mix[:, f, 0:SEQ]).then_inc(mix_hi, 1)
                else:
                    act.wait_ge(used, f + 1)
                act.wait_ge(w_sem[n % 4], 16 * (n // 4 + 1))
                act.copy(whi[:, f, :], raw[:, n % 4, :]).then_inc(w_hi, 1)

        @block.vector
        def _(dve):
            def add(i, t, r):
                part = k.x2[0:r, t, i * 512:(i + 1) * 512]
                dve.tensor_tensor(part, part, k.psum[t % NT][0:r, :], ALU.add).then_inc(added, 1)

            for i in range(2):
                for f in range(KD):
                    n = i * KD + f
                    if i == 0:
                        dve.wait_ge(mix_hi, f + 1)
                        dve.tensor_tensor(slo[:, f, :], mix[:, f, SEQ:TOK], shi[:, f, :], ALU.subtract)
                        dve.tensor_tensor(k.h_lo[:, f, :], mix[:, f, 0:SEQ], k.h_hi[:, f, :], ALU.subtract).then_inc(mix_lo, 1)
                    dve.wait_ge(w_hi, n + 1)
                    dve.tensor_tensor(wlo[:, f, :], raw[:, n % 4, :], whi[:, f, :], ALU.subtract).then_inc(w_lo, 1)
                if i:
                    dve.wait_ge(used, KD)
                    add(0, NT, NS)
                else:
                    dve.wait_ge(x_landed, 32)
                for t in range(NT):
                    dve.wait_ge(made, i * NT + t + 1)
                    add(i, t, P)
            dve.wait_ge(used, 2 * KD)
            add(1, NT, NS)


def stage_mlp(k):
    nc, a = k.nc, k.a
    F = FF // P
    ND = 2 * (NT + 1)
    x2 = k.x2
    up_sem, down_sem = k.sems("ml_up_landed", 2), k.sems("ml_down_landed", 2)
    names = ("up_rounded", "up_rest", "down_rounded", "down_rest", "up", "relu", "square", "hid_rounded", "hid_rest", "down", "added")
    up_hi, up_lo, down_hi, down_lo, upped, relued, squared, hid_hi, hid_lo, downed, added = (k.sem("ml_" + n) for n in names)
    wu = a["w_up"][0].rearrange("(k p) n -> p k n", p=P)
    wd = a["w_down"][0].rearrange("(k p) n -> p k n", p=P)
    steps = [("up", 0), ("up", 1)]
    for g in range(F // 2):
        steps += [("up", 2 * g + 2)] * (2 * g + 2 < F) + [("down", g)] + [("up", 2 * g + 3)] * (2 * g + 3 < F)
    pieces = [(0, 512), (512, 512), (SEQ, NS)]
    with ExitStack() as ctx:
        sbuf = lambda name, dims: ctx.enter_context(nc.sbuf_tensor("ml_" + name, [P, *dims], F32R))
        m = Map(k.hT_at + KD * P)
        raw_up = k.view(m.take(2 * KD * P), 2, KD, P)
        raw_down, tmp = k.view(m.take(2 * D), 2, D), k.view(m.take(3 * 512), 3, 512)
        uhi, ulo = sbuf("up_hi", [2, KD, P]), sbuf("up_lo", [2, KD, P])
        dhi, dlo = sbuf("down_hi", [2, D]), sbuf("down_lo", [2, D])
        hhi, hlo = sbuf("hid_hi", [3, TOK]), sbuf("hid_lo", [3, TOK])
        block = ctx.enter_context(nc.Block())

        @block.sync
        def _(sp):
            def load_up(f):
                sp.dma_start(raw_up[:, f % 2], wu[:, :, f * P:(f + 1) * P]).then_inc(up_sem[f % 2], 16)

            def load_down(n):
                if n >= 2:
                    sp.wait_ge(down_lo, n - 1)
                sp.dma_start(raw_down[:, n % 2], wd[:, n, :]).then_inc(down_sem[n % 2], 16)

            for f in range(2):
                load_up(f)
            for n in range(2):
                load_down(n)
            for kind, f in steps:
                if kind == "down":
                    continue
                if f + 2 < F:
                    sp.wait_ge(upped, 3 * (f + 1))
                    load_up(f + 2)
                if f % 2 == 0 and f:
                    for n in (f, f + 1):
                        if n < F:
                            load_down(n)

        @block.tensor
        def _(pe):
            for kind, f in steps:
                if kind == "up":
                    pe.wait_ge(up_lo, f + 1)
                    for j, (at, w) in enumerate(pieces):
                        n = 3 * f + j
                        if n >= 4:
                            pe.wait_ge(relued, n - 3)
                        bank = k.psum[n % 4]
                        for c in range(KD):
                            if w == 512:
                                last = split_product(pe, bank, (uhi[:, f % 2, c, :], ulo[:, f % 2, c, :]),
                                                     (k.h_hi[:, c, at:at + w], k.h_lo[:, c, at:at + w]), c == 0, c == KD - 1)
                            else:
                                last = pe.matmul(bank[:, 0:P], raw_up[:, f % 2, c, :], k.h_sample[:, c, :], start=(c == 0), stop=(c == KD - 1))
                        last.then_inc(upped, 1)
                    continue
                pe.wait_ge(hid_lo, 6 * (f + 1))
                pe.wait_ge(down_lo, 2 * (f + 1))
                for t in range(NT + 1):
                    r = rows_of(t)
                    for i in range(2):
                        n = ND * f + 2 * t + i
                        if n >= 4:
                            pe.wait_ge(added, n - 3)
                        for e in (2 * f, 2 * f + 1):
                            cols, half = slice(t * P, t * P + r), slice(i * 512, (i + 1) * 512)
                            last = split_product(pe, k.psum[4 + n % 4][0:r, :], (hhi[:, e % 3, cols], hlo[:, e % 3, cols]),
                                                 (dhi[:, e % 2, half], dlo[:, e % 2, half]), e == 2 * f, e == 2 * f + 1)
                        last.then_inc(downed, 1)

        @block.scalar
        def _(act):
            def round_up(f):
                act.wait_ge(up_sem[f % 2], 16 * (f // 2 + 1))
                if f >= 2:
                    act.wait_ge(upped, 3 * (f - 1))
                act.copy(uhi[:, f % 2], raw_up[:, f % 2]).then_inc(up_hi, 1)

            def round_down(n):
                act.wait_ge(down_sem[n % 2], 16 * (n // 2 + 1))
                if n >= 2:
                    act.wait_ge(downed, ND * (n // 2))
                act.copy(dhi[:, n % 2, :], raw_down[:, n % 2, :]).then_inc(down_hi, 1)

            for f in range(2):
                round_up(f)
            for n in range(2):
                round_down(n)
            for kind, f in steps:
                if kind == "down":
                    for n in (2 * f + 2, 2 * f + 3):
                        if n < F:
                            round_down(n)
                    continue
                for j, (at, w) in enumerate(pieces):
                    n = 3 * f + j
                    act.wait_ge(upped, n + 1)
                    if f:
                        act.wait_ge(hid_lo, n - 2)
                    act.activation(tmp[:, j, 0:w], k.psum[n % 4][:, 0:w], ACT.Relu).then_inc(relued, 1)
                if f >= 3:
                    act.wait_ge(downed, ND * ((f - 3) // 2 + 1))
                for j, (at, w) in enumerate(pieces):
                    act.wait_ge(squared, 3 * f + j + 1)
                    act.copy(hhi[:, f % 3, at:at + w], tmp[:, j, 0:w]).then_inc(hid_hi, 1)
                if f + 2 < F:
                    round_up(f + 2)

        @block.vector
        def _(dve):
            def rest_up(f):
                dve.wait_ge(up_hi, f + 1)
                dve.tensor_tensor(ulo[:, f % 2], raw_up[:, f % 2], uhi[:, f % 2], ALU.subtract).then_inc(up_lo, 1)

            def rest_down(n):
                dve.wait_ge(down_hi, n + 1)
                dve.tensor_tensor(dlo[:, n % 2, :], raw_down[:, n % 2, :], dhi[:, n % 2, :], ALU.subtract).then_inc(down_lo, 1)

            for f in range(2):
                rest_up(f)
            for n in range(2):
                rest_down(n)
            for kind, f in steps:
                if kind == "down":
                    for n in range(ND * f, ND * (f + 1)):
                        t, i = n % ND // 2, n % 2
                        r = rows_of(t)
                        part = x2[0:r, t, i * 512:(i + 1) * 512]
                        dve.wait_ge(downed, n + 1)
                        if f:
                            dve.wait_ge(added, n - ND + 1)
                        dve.tensor_tensor(part, part, k.psum[4 + n % 4][0:r, :], ALU.add).then_inc(added, 1)
                    for n in (2 * f + 2, 2 * f + 3):
                        if n < F:
                            rest_down(n)
                    continue
                for j, (at, w) in enumerate(pieces):
                    n = 3 * f + j
                    dve.wait_ge(relued, n + 1)
                    dve.tensor_tensor(tmp[:, j, 0:w], tmp[:, j, 0:w], tmp[:, j, 0:w], ALU.mult).then_inc(squared, 1)
                for j, (at, w) in enumerate(pieces):
                    dve.wait_ge(hid_hi, 3 * f + j + 1)
                    dve.tensor_tensor(hlo[:, f % 3, at:at + w], tmp[:, j, 0:w], hhi[:, f % 3, at:at + w], ALU.subtract).then_inc(hid_lo, 1)
                if f + 2 < F:
                    rest_up(f + 2)


def stage_final(k):
    nc, a = k.nc, k.a
    x2 = k.x2
    m = Map(k.hT_at)
    gain = k.view(m.take(D), D)
    junk = k.view(m.take(D), D)
    stat = k.view(m.take(3 * (NT + 1)), 3, NT + 1)
    landed, squared, rooted, inv, done = (k.sem("fn_" + n) for n in ("gain_landed", "squared", "rooted", "inv", "done"))
    out_sem = k.stored["y"]
    yp = a["y_prompt"][0].rearrange("(t p) d -> t p d", p=P)
    ys = a["y_sample"].rearrange("b t d -> (b t) d")
    n = NT + 1
    with nc.Block() as block:
        @block.sync
        def _(sp):
            sp.dma_start(gain, a["norm_final"].rearrange("(a n) -> a n", a=1).partition_broadcast(P).rearrange("p a n -> p (a n)")).then_inc(landed, 16)
            for t in range(n):
                r = rows_of(t)
                sp.wait_ge(done, t + 1)
                sp.dma_start(yp[t] if t < NT else ys, x2[0:r, t, :]).then_inc(out_sem, 16)
            sp.wait_ge(out_sem, 16 * n)

        @block.scalar
        def _(act):
            for t in range(n):
                r = rows_of(t)
                if t:
                    act.wait_ge(squared, t)
                act.activation(junk[0:r, :], x2[0:r, t, :], ACT.Square, accum_out=stat[0:r, 0, t:t + 1]).then_inc(squared, 1)
                act.wait_ge(squared, t + 1)
                act.activation(stat[0:r, 1, t:t + 1], stat[0:r, 0, t:t + 1], ACT.Sqrt, scale=1.0 / D, bias=k.eps[0:r, :]).then_inc(rooted, 1)

        @block.vector
        def _(dve):
            dve.wait_ge(landed, 16)
            for t in range(n):
                r = rows_of(t)
                dve.wait_ge(rooted, t + 1)
                dve.reciprocal(stat[0:r, 2, t:t + 1], stat[0:r, 1, t:t + 1]).then_inc(inv, 1)
                dve.wait_ge(inv, t + 1)
                dve.scalar_tensor_tensor(out=x2[0:r, t, :], in0=x2[0:r, t, :], scalar=stat[0:r, 2, t:t + 1], in1=gain[0:r, :],
                                         op0=ALU.mult, op1=ALU.mult).then_inc(done, 1)


_INS = ["x_prompt", "x_sample", "cache_k", "cache_v", "cache_kidx", "state_ssm", "state_conv", "page_table",
        "norm_mix", "w_in", "conv_w", "a_log", "dt_bias", "norm_gdn_out", "w_out", "norm_mlp", "w_up",
        "w_down", "norm_final"]
_OUTS = [("y_prompt", (1, SEQ, D)), ("y_sample", (DB, DS, D)),
         ("new_k_prompt", (1, 1, SEQ, H, HD)), ("new_v_prompt", (1, 1, SEQ, H, HD)), ("new_kidx_prompt", (1, 1, SEQ, DI)),
         ("new_ssm_prompt", (1, 1, G, DK, DK)), ("new_conv_prompt", (1, 1, CW - 1, CC)),
         ("new_k_sample", (1, DB, DS, H, HD)), ("new_v_sample", (1, DB, DS, H, HD)), ("new_kidx_sample", (1, DB, DS, DI)),
         ("new_ssm_sample", (1, DB, G, DK, DK)), ("new_conv_sample", (1, DB, CW - 1, CC))]


def build_program(nc, a, stop=99):
    with ExitStack() as ctx:
        a["q_T"] = nc.dram_tensor("q_T", (AW, SEQ), F32, kind="Internal").ap()
        a["k_T"] = nc.dram_tensor("k_T", (AW, SEQ), F32, kind="Internal").ap()
        k = Kernel(nc, ctx, a)

        stages(k, stop)


def stages(k, stop):
    a = k.a
    stage_constants(k)
    x_ring = [k.view(k.xc_at + (t % 3) * D, D) for t in range(NT + 1)]
    xp = a["x_prompt"][0].rearrange("(t p) d -> t p d", p=P)
    xs = a["x_sample"].rearrange("b t d -> (b t) d")
    k.ix_landed, k.kidx_landed = k.sems("ixw_landed", 2), k.sems("kidx_landed", DB)
    stage_norm(k, "mix", x_ring, k.view(k.ring_at + KD * 512, 4 * D), k.g_mix, lambda t: xp[t] if t < NT else xs, out=k.view(k.hT_at, KD, TOK))
    if stop < 1: return
    stage_indexer_projection(k)
    stage_prompt_scores(k)
    if stop < 2: return
    stage_sample_scores(k)
    if stop < 3: return
    stage_mixer_projection(k)
    if stop < 4: return
    stage_conv(k)
    if stop < 5: return
    stage_l2norm(k)
    stage_gates(k)
    if stop < 6: return
    k.stage_done()
    stage_chunks(k)
    if stop < 7: return
    stage_scan(k)
    if stop < 8: return
    stage_prompt_attention(k)
    if stop < 9: return
    stage_sample_attention(k)
    if stop < 10: return
    k.begin_dense_part()
    stage_output_projection(k)
    k.h_sample = k.view(k.hT_at, KD, P)
    stage_norm(k, "mlp", [k.x2[:, t, :] for t in range(NT + 1)], k.view(k.hT_at + KD * P, 5 * D), k.g_mlp, None,
               split=(k.h_hi, k.h_lo, k.h_sample))
    if stop < 11: return
    stage_mlp(k)
    stage_final(k)


def kernel(**inputs):
    import concourse.bacc as bacc
    from concourse.bass_utils import run_bass_kernel_spmd

    nc = bacc.Bacc("TRN2", target_bir_lowering=False, num_devices=1)
    arrays, a = {}, {}
    for name in _INS:
        arrays["in_" + name] = np.ascontiguousarray(inputs[name])
    arrays["in_const"] = CONST
    for name, x in arrays.items():
        a[name[3:]] = nc.dram_tensor(name, x.shape, mybir.dt.from_np(x.dtype), kind="ExternalInput").ap()
    for name, shape in _OUTS:
        a[name] = nc.dram_tensor("out_" + name, shape, F32, kind="ExternalOutput").ap()
    build_program(nc, a)
    r = run_bass_kernel_spmd(nc, [arrays], core_ids=[0])
    return tuple(r.results[0]["out_" + name] for name, _ in _OUTS)
```

```python
from contextlib import ExitStack

import numpy as np

import concourse.bass as bass
from concourse import mybir

F32 = mybir.dt.float32
F32R = mybir.dt.float32r
BF16 = mybir.dt.bfloat16
I32 = mybir.dt.int32
ALU = mybir.AluOpType
ACT = mybir.ActivationFunctionType
AX_X = mybir.AxisListType.X

P = 128
D = 1024
KD = D // P
SEQ = 1024
NT = SEQ // P
DB, DS = 8, 8
NS = DB * DS
TOK = SEQ + NS
PAST, PAGE = 2048, 128
NPG = PAST // PAGE
LS = PAST + NS
H, HD = 8, 64
AW = H * HD
NI, DI = 4, 64
TOPK = 256
G, DK = 4, 128
GW = G * DK
CW = 4
CC = 3 * GW
CF = CC // P
FF = 4 * D
EPS = 1e-6
OFF_Q, OFF_K, OFF_V = 0, AW, 2 * AW
OFF_QI = 3 * AW
OFF_KI = OFF_QI + NI * DI
OFF_WI = OFF_KI + DI
OFF_CONV = OFF_WI + NI
OFF_A = OFF_CONV + CC
OFF_Z = OFF_A + 2 * G
N_IN = OFF_Z + GW
FIRST_SEL = TOPK // P
NEG_SCORE = -3.0e38
TAKEN = -3.3e38
MASKED = -1.0e30
LEVELS = 7
S_LEVELS = 3

IX_QI, IX_KI, IX_KI2, IX_WI, IX_A, IX_B = 0, 256, 320, 384, 388, 392
IX_W = 396


def constants():
    r = np.arange(P)
    row, col = r[:, None], r[None, :]
    s_ok = (row < NS) & (col < NS) & (row // DS == col // DS)
    parts = {}
    parts["ident"] = np.eye(P)
    parts["ones"] = np.ones((P, P))
    parts["tri"] = (row <= col)
    parts["tri_s"] = (row <= col) & s_ok
    parts["block_s"] = s_ok
    lev = []
    for l in range(LEVELS):
        s = 1 << l
        lev.append(-1.0 * ((row // (2 * s) == col // (2 * s)) & (row // s % 2 == 0) & (col // s % 2 == 1)))
    parts["level"] = np.concatenate(lev, 1)
    parts["first_low"] = -1.0 * ((row // 2 == col // 2) & (row % 2 == 1) & (col % 2 == 0))
    parts["score_causal"] = NEG_SCORE * (col > row)
    parts["score_new"] = NEG_SCORE * ~(s_ok & (col <= row))[:, :NS]
    parts["attn_causal"] = MASKED * (col > row)
    parts["low_big"] = -MASKED * (col >= row)
    parts["low_big_s"] = -MASKED * ~((col < row) & s_ok)
    parts["up_big"] = MASKED * (col < row)
    parts["up_big_s"] = MASKED * ~((row <= col) & s_ok)
    sel, sum_h = [], []
    for g in range(2):
        m = np.zeros((P, P))
        for bb in range(4):
            for h in range(NI):
                for q in range(DS):
                    m[(4 * g + bb) * DS + q, bb * 32 + h * DS + q] = 1
        sel.append(m)
        sum_h.append(m.T[:, :NS])
    parts["sel_ix"] = np.concatenate(sel, 1)
    parts["sum_ix"] = np.concatenate(sum_h, 1)
    parts["head_ix"] = ((r // DS) % NI)[:, None] == np.arange(NI)[None]
    sel = []
    for i in range(DB // 2):
        m = np.zeros((P, P))
        for b2 in range(2):
            for h in range(H):
                for q in range(DS):
                    m[(2 * i + b2) * DS + q, b2 * 64 + h * DS + q] = 1
        sel.append(m)
    parts["sel_at"] = np.concatenate(sel, 1)
    parts["in_batch"] = (r[:, None] < NS) & (r[:, None] // DS == np.arange(DB)[None])
    parts["columns"] = np.broadcast_to((np.arange(NS) // DS == np.arange(DB)[:, None]).reshape(1, -1), (P, DB * NS))
    at, where = 0, {}
    for n, a in parts.items():
        where[n] = (at, a.shape[1])
        at += a.shape[1]
    return np.ascontiguousarray(np.concatenate([np.asarray(a, np.float32) for a in parts.values()], 1)), where


CONST, CONST_AT = constants()
NC_COLS = CONST.shape[1]
BF_CONST = ("ident", "level", "first_low", "columns", "attn_causal", "low_big", "low_big_s", "up_big", "up_big_s", "sel_at")
F_CONST = tuple(n for n in CONST_AT if n not in BF_CONST[1:])


class Map:

    def __init__(self, start=0):
        self.at = start

    def take(self, n):
        self.at += n
        return self.at - n


LASTING = 12053
STORES = ("kidx", "mix0", "mix1", "mix2", "mix3", "conv", "ssm", "y")


class Kernel:

    def __init__(self, nc, ctx, a):
        self.nc, self.ctx, self.a = nc, ctx, a
        self.in_use = []
        self.stored = {n: nc.alloc_semaphore(name=n + "_stored") for n in STORES}
        self.words = 53200
        self.arena = ctx.enter_context(nc.sbuf_tensor("arena", [P, LASTING], F32))
        self.work_ctx = ExitStack()
        ctx.callback(self.work_ctx.close)
        self.work = self.work_ctx.enter_context(nc.sbuf_tensor("work", [P, self.words - LASTING], F32))
        self.banks = ctx.enter_context(nc.psum_tensor("banks", [P, 8 * 512], F32))
        self.psum = [self.banks[:, i * 512:(i + 1) * 512] for i in range(8)]
        m = Map()
        self.c = {}
        for n in F_CONST:
            w = CONST_AT[n][1]
            self.c[n] = self.view(m.take(w), w)
        self.b = {}
        for n in BF_CONST:
            w = CONST_AT[n][1]
            self.b[n] = self.view(m.take(w // 2), w // 2).bitcast(BF16)
        self.g_mix = self.view(m.take(KD), KD)
        self.g_mlp = self.view(m.take(KD), KD)
        self.conv_w = self.view(m.take(CF * CW), CF, CW)
        self.gdn_row = self.view(m.take(GW), G, DK)
        self.a_row = self.view(m.take(2 * G), 2 * G)
        self.table = self.view(m.take(DB * NPG), DB * NPG).bitcast(I32)
        self.eps = self.view(m.take(1), 1)
        self.hT_at = m.take(KD * TOK)
        assert m.at == LASTING, m.at
        self.psI = self.view(m.take(IX_W), IX_W)
        self.psA = self.view(m.take(3 * AW), 3 * AW)
        self.psC = self.view(m.take(CC), CC)
        self.psZ = self.view(m.take(GW), GW)
        self.maskP = []
        for t in range(NT):
            n = (t + 1) * P
            self.maskP.append(self.view(m.take(n // 2), n // 2).bitcast(BF16) if t >= FIRST_SEL else None)
        self.maskS = self.view(m.take(LS // 2), LS // 2).bitcast(BF16)
        self.kiwi = self.view(m.take(NT * 76), NT, 76)
        self.xc_at = m.take(CF * (SEQ + CW - 1))
        self.z_at = m.take(NT * GW)
        self.free_at = m.at
        self.sc_at = m.take(sum((t + 1) * P for t in range(FIRST_SEL, NT)) + LS)
        self.ring_at = m.take(2 * KD * 512)
        self.stage_at = m.take(4 * 512)
        self.best_at = m.take(64)
        self.lengths_at = self.words - 5800
        self.kv_at = self.free_at + 3 * NT * H
        self.pages_at = self.free_at - DB * NPG * DI
        assert m.at <= self.words, m.at

    def view(self, at, *dims):
        n = int(np.prod(dims))
        assert at >= LASTING or at + n <= LASTING
        ap = self.arena[:, at:at + n] if at < LASTING else self.work[:, at - LASTING:at - LASTING + n]
        if len(dims) == 2:
            ap = ap.rearrange("p (a b) -> p a b", a=dims[0])
        if len(dims) == 3:
            ap = ap.rearrange("p (a b c) -> p a b c", a=dims[0], b=dims[1])
        return ap

    def begin_dense_part(self):
        self.work_ctx.close()
        nc, enter = self.nc, self.ctx.enter_context
        x2 = enter(nc.sbuf_tensor("x2", [P, NT, D], F32))
        self.x2 = [x2[:, t, :] for t in range(NT)] + [self.view(self.hT_at, D)]
        self.x2_prompt = x2
        self.h_hi = enter(nc.sbuf_tensor("h_hi", [P, KD, TOK], F32R))
        self.h_lo = enter(nc.sbuf_tensor("h_lo", [P, KD, TOK], F32R))

    def sem(self, name):
        self.in_use.append(self.nc.alloc_semaphore(name=name))
        return self.in_use[-1]

    def stage_done(self):
        self.nc.all_engine_barrier()
        self.nc.clear_and_free_semaphores(self.in_use)
        self.nc.all_engine_barrier()
        self.in_use = []

    def sems(self, name, n):
        return [self.sem(f"{name}{i}") for i in range(n)]


def rows_of(t):
    return P if t < NT else NS


def stage_constants(k):
    nc, a = k.nc, k.a
    landed = k.sem("const_landed")
    stage = k.view(k.xc_at, NC_COLS)
    small = 6 + CW + G
    with nc.Block() as block:
        @block.sync
        def _(sp):
            sp.dma_start(stage, a["const"]).then_inc(landed, 16)
            with nc.allow_non_contiguous_dma(reason="small parameters laid over partitions"):
                sp.dma_start(k.g_mix, a["norm_mix"].rearrange("a (k p) -> p (a k)", p=P)).then_inc(landed, 16)
                sp.dma_start(k.g_mlp, a["norm_mlp"].rearrange("a (k p) -> p (a k)", p=P)).then_inc(landed, 16)
                for j in range(CW):
                    sp.dma_start(k.conv_w[:, :, j], a["conv_w"][0, j, :].rearrange("(f p) -> p f", p=P)).then_inc(landed, 16)
            for h in range(G):
                sp.dma_start(k.gdn_row[:, h, :], a["norm_gdn_out"].partition_broadcast(P).rearrange("p a n -> p (a n)")).then_inc(landed, 16)
            sp.dma_start(k.a_row[:, 0:G], a["a_log"].partition_broadcast(P).rearrange("p a n -> p (a n)")).then_inc(landed, 16)
            sp.dma_start(k.a_row[:, G:2 * G], a["dt_bias"].partition_broadcast(P).rearrange("p a n -> p (a n)")).then_inc(landed, 16)
            sp.dma_start(k.table[0:1, :], a["page_table"].rearrange("b n -> (b n)").rearrange("(a n) -> a n", a=1)).then_inc(landed, 16)
            sp.wait_ge(landed, 16 * small)

        @block.vector
        def _(dve):
            dve.memset(k.eps, EPS)
            dve.wait_ge(landed, 16 * small)
            for n in F_CONST:
                at, w = CONST_AT[n]
                dve.tensor_copy(k.c[n], stage[:, at:at + w])
            for n in BF_CONST:
                at, w = CONST_AT[n]
                dve.tensor_copy(k.b[n], stage[:, at:at + w])


def load_indexer_pages(k, q, batches):
    for b in batches:
        pages = k.view(k.pages_at + b * NPG * DI, NPG, DI)
        for p in range(NPG):
            page = q.value_load(k.table[0:1, b * NPG + p:b * NPG + p + 1], min_val=0, max_val=k.a["cache_kidx"].shape[1] - 1)
            q.dma_start(pages[:, p, :], k.a["cache_kidx"][0, bass.ds(page, 1), :, :].rearrange("a p d -> p (a d)")).then_inc(k.kidx_landed[b], 16)


def stage_norm(k, tiles, load):
    nc = k.nc
    out = k.view(k.hT_at, KD, TOK)
    free = Map(k.ring_at + KD * 512)
    xn = [k.view(free.take(D), D) for _ in range(2)]
    junk = k.view(free.take(D), D)
    stat = k.view(free.take(3 * (NT + 1)), 3, NT + 1)
    loaded = k.sems("norm_loaded", 3)
    squared, rooted, scaled, normed, turned, kept = (k.sem("norm_" + n) for n in ("squared", "rooted", "rstd", "normed", "turned", "kept"))
    n = NT + 1
    with nc.Block() as block:
        @block.gpsimd
        def _(pool):
            load_indexer_pages(k, pool, range(0, 2))

        @block.sync
        def _(sp):
            k.landed_at = {0: 16 * load_indexer_weights(k, sp, k.view(k.ring_at, KD, 512), k.ix_landed[0])}
            for t in range(n):
                if t >= 3:
                    sp.wait_ge(normed, t - 2)
                sp.dma_start(tiles[t][0:rows_of(t), :], load(t)).then_inc(loaded[t % 3], 16)

        @block.scalar
        def _(act):
            for t in range(n):
                r = rows_of(t)
                act.wait_ge(loaded[t % 3], 16 * (t // 3 + 1))
                if t:
                    act.wait_ge(squared, t)
                act.activation(junk[0:r, :], tiles[t][0:r, :], ACT.Square, accum_out=stat[0:r, 0, t:t + 1]).then_inc(squared, 1)
                act.wait_ge(squared, t + 1)
                act.activation(stat[0:r, 1, t:t + 1], stat[0:r, 0, t:t + 1], ACT.Sqrt, scale=1.0 / D, bias=k.eps[0:r, :]).then_inc(rooted, 1)

        @block.vector
        def _(dve):
            def norm(t):
                r = rows_of(t)
                dve.wait_ge(rooted, t + 1)
                dve.reciprocal(stat[0:r, 2, t:t + 1], stat[0:r, 1, t:t + 1]).then_inc(scaled, 1)
                if t >= 2:
                    dve.wait_ge(turned, t - 1)
                dve.wait_ge(scaled, t + 1)
                dve.tensor_scalar(xn[t % 2][0:r, :], tiles[t][0:r, :], stat[0:r, 2, t:t + 1], None, ALU.mult).then_inc(normed, 1)

            def keep(t):
                r = rows_of(t)
                dve.wait_ge(turned, t + 1)
                for half in range(2):
                    src = k.psum[2 * (t % 2) + half][:, :].rearrange("p (f n) -> p f n", f=4)[:, :, 0:r]
                    g = k.g_mix[:, 4 * half:4 * half + 4].unsqueeze(2).to_broadcast([P, 4, r])
                    dve.tensor_tensor(out[:, 4 * half:4 * half + 4, t * P:t * P + r], src, g, ALU.mult).then_inc(kept, 1)

            norm(0)
            for t in range(n):
                if t + 1 < n:
                    norm(t + 1)
                keep(t)

        @block.tensor
        def _(pe):
            for t in range(n):
                r = rows_of(t)
                pe.wait_ge(normed, t + 1)
                if t >= 2:
                    pe.wait_ge(kept, 2 * (t - 1))
                for f in range(KD):
                    last = pe.transpose(k.psum[2 * (t % 2) + f // 4][:, (f % 4) * P:(f % 4) * P + r],
                                        xn[t % 2][0:r, f * P:(f + 1) * P], k.c["ident"][0:r, 0:r])
                last.then_inc(turned, 1)


def projection_of_indexer():
    jobs = [(0, "F", f * P, P, j) for f in range(2) for j in range(2)]
    jobs += [(0, "F", IX_KI, P, j) for j in range(2)]
    jobs += [(0, "T", IX_KI2, IX_W - IX_KI2, t) for t in range(NT)]
    jobs += [(0, "S", 0, IX_W, 0)]
    return jobs


def load_indexer_weights(k, q, dst, sem):
    w = k.a["w_in"][0].rearrange("(k p) n -> p k n", p=P)
    for at, off, n in ((IX_QI, OFF_QI, NI * DI), (IX_KI, OFF_KI, DI), (IX_KI2, OFF_KI, DI + NI), (IX_A, OFF_A, 2 * G)):
        q.dma_start(dst[:, :, at:at + n], w[:, :, off:off + n]).then_inc(sem, 16)
    return 4


def project_products(k, pe, jobs, banks, sems):
    hT = k.view(k.hT_at, KD, TOK)
    landed, made, kept = sems
    seen = -1
    for n, (c, kind, col, w, at) in enumerate(jobs):
        if c != seen:
            pe.wait_ge(landed[c % 2], k.landed_at[c])
            seen = c
        if n >= banks:
            pe.wait_ge(kept, n - banks + 1)
        bank = k.psum[n % banks]
        ring = k.view(k.ring_at + (c % 2) * KD * 512, KD, 512)
        if kind == "K":
            pe.wait_ge(kept, k.turn_of[n] + 1)
            src = k.view(k.stage_at + k.slot_of[k.turn_of[n]] * 512, 512)
            for i in range(4):
                last = pe.transpose(bank[:, i * P:(i + 1) * P], src[:, i * P:(i + 1) * P], k.c["ident"])
        for f in range(KD if kind != "K" else 0):
            if kind == "F":
                last = pe.matmul(bank[0:w, :], ring[:, f, col:col + w], hT[:, f, at * 512:(at + 1) * 512],
                                 start=(f == 0), stop=(f == KD - 1))
            elif kind == "T":
                last = pe.matmul(bank[:, 0:w], hT[:, f, at * P:(at + 1) * P], ring[:, f, col:col + w],
                                 start=(f == 0), stop=(f == KD - 1))
            else:
                last = pe.matmul(bank[0:NS, 0:w], hT[:, f, SEQ:TOK], ring[:, f, col:col + w],
                                 start=(f == 0), stop=(f == KD - 1))
        last.then_inc(made, 1)


def stage_indexer_projection(k):
    nc = k.nc
    jobs = projection_of_indexer()
    landed, made, kept = k.ix_landed, k.sem("ix_made"), k.sem("ix_kept")
    k.qiT = k.view(k.xc_at, 2, SEQ)
    k.kiT = k.view(k.xc_at + 2 * SEQ, SEQ)
    with nc.Block() as block:
        @block.gpsimd
        def _(pool):
            load_indexer_pages(k, pool, range(2, 4))

        @block.sync
        def _(sp):
            load_indexer_pages(k, sp, range(4, 5))

        @block.tensor
        def _(pe):
            project_products(k, pe, jobs, 8, (landed, made, kept))

        @block.scalar
        def _(act):
            for n, (c, kind, col, w, at) in enumerate(jobs):
                act.wait_ge(made, n + 1)
                bank = k.psum[n % 8]
                if kind == "F" and col == IX_KI:
                    act.copy(k.kiT[:, at * 512:(at + 1) * 512], bank[:, :]).then_inc(kept, 1)
                elif kind == "F":
                    act.copy(k.qiT[:, col // P, at * 512:(at + 1) * 512], bank[:, :]).then_inc(kept, 1)
                elif kind == "T":
                    act.copy(k.kiwi[:, at, :], bank[:, 0:w]).then_inc(kept, 1)
                else:
                    act.copy(k.psI[0:NS, :], bank[0:NS, 0:w]).then_inc(kept, 1)


def stage_prompt_scores(k):
    nc = k.nc
    k.scP, at = [None] * NT, k.sc_at
    for t in range(FIRST_SEL, NT):
        k.scP[t] = k.view(at, (t + 1) * P)
        at += (t + 1) * P
    k.scS = k.view(at, LS)
    relu_buf = [k.view(k.ring_at + i * 512, 512) for i in range(4)]
    w_half = k.view(k.ring_at + 2048, NT, NI)
    made, relued, summed, halved = k.sem("scp_made"), k.sem("scp_relued"), k.sem("scp_summed"), k.sem("scp_halved")
    out_sem = k.stored["kidx"]
    items = [(t, c, min(512, (t + 1) * P - c), h)
             for t in range(FIRST_SEL, NT) for c in range(0, (t + 1) * P, 512) for h in range(NI)]
    with nc.Block() as block:
        @block.gpsimd
        def _(pool):
            load_indexer_pages(k, pool, range(5, 7))

        @block.sync
        def _(sp):
            sp.dma_start(k.a["new_kidx_prompt"][0, 0].rearrange("(t p) d -> p t d", p=P), k.kiwi[:, :, 0:DI]).then_inc(out_sem, 16)
            sp.dma_start(k.a["new_kidx_sample"][0].rearrange("b t d -> (b t) d"), k.psI[0:NS, IX_KI:IX_KI + DI]).then_inc(out_sem, 16)
            load_indexer_pages(k, sp, range(7, DB))
            sp.wait_ge(out_sem, 32)

        @block.tensor
        def _(pe):
            for n, (t, c, w, h) in enumerate(items):
                if n >= 4:
                    pe.wait_ge(relued, n - 3)
                lo = (h % 2) * DI
                pe.matmul(k.psum[n % 4][:, 0:w], k.qiT[lo:lo + DI, h // 2, t * P:(t + 1) * P],
                          k.kiT[lo:lo + DI, c:c + w], start=True, stop=True).then_inc(made, 1)

        @block.scalar
        def _(act):
            for n, (t, c, w, h) in enumerate(items):
                act.wait_ge(made, n + 1)
                if n >= 4:
                    act.wait_ge(summed, n - 3)
                act.activation(relu_buf[n % 4][:, 0:w], k.psum[n % 4][:, 0:w], ACT.Relu).then_inc(relued, 1)

        @block.vector
        def _(dve):
            dve.tensor_scalar(w_half, k.kiwi[:, :, DI:DI + NI], DI ** -0.5 * NI ** -0.5, None, ALU.mult).then_inc(halved, 1)
            dve.wait_ge(halved, 1)
            for n, (t, c, w, h) in enumerate(items):
                dve.wait_ge(relued, n + 1)
                sc = k.scP[t][:, c:c + w]
                if h == 0:
                    dve.tensor_scalar(sc, relu_buf[n % 4][:, 0:w], w_half[:, t, h:h + 1], None, ALU.mult).then_inc(summed, 1)
                else:
                    dve.wait_ge(summed, n)
                    dve.scalar_tensor_tensor(out=sc, in0=relu_buf[n % 4][:, 0:w], scalar=w_half[:, t, h:h + 1],
                                             in1=sc, op0=ALU.mult, op1=ALU.add).then_inc(summed, 1)
            dve.wait_ge(summed, len(items))
            for t in range(FIRST_SEL, NT):
                own = k.scP[t][:, t * P:(t + 1) * P]
                dve.tensor_tensor(own, own, k.c["score_causal"], ALU.add)


class TopK:

    def __init__(self, k):
        self.k = k
        self.best = k.view(k.best_at, 8, 8)
        self.work = [(P, k.scP[t]) for t in range(FIRST_SEL, NT)] + [(NS, k.scS)]
        self.prompt, self.sample = list(range(NT - FIRST_SEL)), NT - FIRST_SEL
        self.maxed, self.taken = k.sem("topk_max"), k.sem("topk_taken")
        self.count, self.last = 0, {}

    def round(self, dve, works):
        for i in works:
            rows, sc = self.work[i]
            if i in self.last:
                dve.wait_ge(self.taken, self.last[i])
            dve.max(self.best[0:rows, i, :], sc[0:rows, :]).then_inc(self.maxed, 1)
        for n, i in enumerate(works):
            rows, sc = self.work[i]
            dve.wait_ge(self.maxed, self.count + n + 1)
            dve.match_replace(sc[0:rows, :], self.best[0:rows, i, :], sc[0:rows, :], TAKEN).then_inc(self.taken, 1)
            self.last[i] = self.count + n + 1
        self.count += len(works)


EARLY_ROUNDS = 2


def stage_sample_scores(k):
    nc = k.nc
    m = Map(k.xc_at)
    qi_dup = k.view(m.take(NI * 2 * DI), NI, 2 * DI)
    qiB = k.view(m.take(DB * NI * DS), DB, NI * DS)
    kiN = k.view(m.take(NS), NS)
    wi_s = k.view(m.take(NI), NI)
    w_pick = [k.view(m.take(NI), NI) for _ in range(2)]
    w_row = k.view(m.take(2), 2)
    pages = [k.view(k.pages_at + b * NPG * DI, NPG, DI) for b in range(DB)]
    k.kT4 = [k.view(m.take(NPG // 2 * PAGE), NPG // 2, PAGE) for _ in range(4)]
    rel = [k.view(m.take(512), 512) for _ in range(3)]
    assert m.at <= k.pages_at
    k.mx_landed = k.sems("mxw_landed", 2)
    k.topk = TopK(k)
    prep, prep_pe, turned, kept = k.sem("scs_prep"), k.sem("scs_prep_pe"), k.sem("scs_turned"), k.sem("scs_kept")
    made, relued, summed, drained = k.sem("scs_made"), k.sem("scs_relued"), k.sem("scs_summed"), k.sem("scs_drained")
    NH = NI * DS
    with nc.Block() as block:
        @block.sync
        def _(sp):
            for c in range(2):
                load_mixer_weights(k, sp, c)

        @block.tensor
        def _(pe):
            pe.wait_ge(prep, 1)
            for h in range(NI):
                last = pe.transpose(k.psum[4][:, h * NS:(h + 1) * NS], qi_dup[0:NS, h, :], k.c["ident"][0:NS, 0:NS])
            last = pe.transpose(k.psum[4][0:DI, NI * NS:NI * NS + NS], k.psI[0:NS, IX_KI:IX_KI + DI], k.c["ident"][0:NS, 0:NS])
            last.then_inc(prep_pe, 1)
            for g in range(2):
                last = pe.matmul(k.psum[5][:, g * NI:(g + 1) * NI], k.c["sel_ix"][0:NS, g * P:(g + 1) * P], wi_s[0:NS, :],
                                 start=True, stop=True)
            last.then_inc(prep_pe, 1)
            pe.wait_ge(prep, 7)

            def turn(b):
                pe.wait_ge(k.kidx_landed[b], 16 * NPG)
                if b >= 1:
                    pe.wait_ge(kept, 2 * b)
                for j in range(NPG // 2):
                    last = pe.transpose(k.psum[4 + j // 4][:, (j % 4) * P:(j % 4 + 1) * P],
                                        pages[b][:, 2 * j:2 * j + 2, :].rearrange("p a d -> p (a d)"), k.c["ident"])
                last.then_inc(turned, 1)

            n = 0
            for g in range(2):
                for bb in range(4):
                    turn(4 * g + bb)
                pe.wait_ge(kept, 8 * (g + 1))
                for par in range(2):
                    for half in range(2):
                        if n >= 2:
                            pe.wait_ge(relued, n - 1)
                        for bb in range(4):
                            last = pe.matmul(k.psum[6 + n % 2][bb * NH:(bb + 1) * NH, :],
                                             qiB[par * DI:(par + 1) * DI, 4 * g + bb, :],
                                             k.kT4[bb][par * DI:(par + 1) * DI, 4 * half:4 * half + 4, :],
                                             start=True, stop=True)
                        last.then_inc(made, 1)
                        pe.wait_ge(relued, n + 1)
                        pe.matmul(k.psum[n % 4][0:NS, :], k.c["sum_ix"][:, g * NS:(g + 1) * NS], rel[n % 3],
                                  start=(g == 0), stop=(g == 1)).then_inc(summed, 1)
                        n += 1
                pe.wait_ge(relued, n)
            pe.wait_ge(drained, 4)
            for g in range(2):
                for bb in range(4):
                    last = pe.matmul(k.psum[6 + g][bb * NH:(bb + 1) * NH, 0:NS], qiB[0:DI, 4 * g + bb, :], kiN[0:DI, :],
                                     start=True, stop=True)
                last.then_inc(made, 1)
            for g in range(2):
                pe.wait_ge(relued, 8 + g + 1)
                pe.matmul(k.psum[0][0:NS, 0:NS], k.c["sum_ix"][:, g * NS:(g + 1) * NS], rel[g][:, 0:NS],
                          start=(g == 0), stop=(g == 1)).then_inc(summed, 1)

        @block.scalar
        def _(act):
            for b in range(DB):
                act.wait_ge(turned, b + 1)
                if b >= 4:
                    act.wait_ge(made, 4)
                if b == 0:
                    act.wait_ge(prep, 7)
                for i in range(2):
                    act.copy(k.kT4[b % 4][:, 4 * i:4 * i + 4, :].rearrange("p a n -> p (a n)"), k.psum[4 + i][:, :]).then_inc(kept, 1)

        @block.vector
        def _(dve):
            for i in range(2):
                last = dve.tensor_copy(qi_dup[0:NS, :, i * DI:(i + 1) * DI], k.psI[0:NS, 0:NI * DI].rearrange("p (h d) -> p h d", h=NI))
            last = dve.tensor_scalar(wi_s[0:NS, :], k.psI[0:NS, IX_WI:IX_WI + NI], DI ** -0.5 * NI ** -0.5, None, ALU.mult)
            last.then_inc(prep, 1)
            dve.wait_ge(prep_pe, 1)
            dve.tensor_copy(qiB.rearrange("p b (h q) -> p b h q", h=NI),
                            k.psum[4][:, 0:NI * NS].rearrange("p (h b q) -> p b h q", h=NI, b=DB)).then_inc(prep, 1)
            dve.tensor_copy(kiN[0:DI, :], k.psum[4][0:DI, NI * NS:NI * NS + NS]).then_inc(prep, 1)
            dve.wait_ge(prep_pe, 2)
            for g in range(2):
                dve.tensor_tensor(w_pick[g], k.psum[5][:, g * NI:(g + 1) * NI], k.c["head_ix"], ALU.mult).then_inc(prep, 1)
            dve.wait_ge(prep, 5)
            for g in range(2):
                dve.reduce_sum(w_row[:, g:g + 1], w_pick[g], AX_X).then_inc(prep, 1)
            dve.wait_ge(prep, 7)
            for n in range(8):
                if n % 4 == 0 and n // 4 < EARLY_ROUNDS:
                    k.topk.round(dve, k.topk.prompt)
                dve.wait_ge(made, n + 1)
                if n >= 3:
                    dve.wait_ge(summed, n - 2)
                dve.tensor_scalar(rel[n % 3], k.psum[6 + n % 2][:, :], 0.0, w_row[:, n // 4:n // 4 + 1], ALU.max, ALU.mult).then_inc(relued, 1)
            dve.wait_ge(summed, 8)
            for n in range(4):
                par, half = n // 2, n % 2
                dst = k.scS[0:NS, 0:PAST].rearrange("q (j r n) -> q r j n", r=2, n=PAGE)[:, par, 4 * half:4 * half + 4, :]
                dve.tensor_copy(dst, k.psum[n][0:NS, :].rearrange("q (j n) -> q j n", j=4)).then_inc(drained, 1)
            for g in range(2):
                dve.wait_ge(made, 8 + g + 1)
                dve.tensor_scalar(rel[g][:, 0:NS], k.psum[6 + g][:, 0:NS], 0.0, w_row[:, g:g + 1], ALU.max, ALU.mult).then_inc(relued, 1)
            dve.wait_ge(summed, 10)
            dve.tensor_tensor(k.scS[0:NS, PAST:LS], k.psum[0][0:NS, 0:NS], k.c["score_new"][0:NS, :], ALU.add)


CHUNKS = (OFF_CONV, OFF_CONV + 512, OFF_CONV + 1024, OFF_Q, OFF_K, OFF_V, OFF_Z)
Q_CHUNK, K_CHUNK, V_CHUNK, Z_CHUNK = 3, 4, 5, 6


def load_mixer_weights(k, q, c):
    w = k.a["w_in"][0].rearrange("(k p) n -> p k n", p=P)
    dst = k.view(k.ring_at + (c % 2) * KD * 512, KD, 512)
    q.dma_start(dst, w[:, :, CHUNKS[c]:CHUNKS[c] + 512]).then_inc(k.mx_landed[c % 2], 16)


def projection_of_mixers():
    prompt = lambda c: [(c, "F", f * P, P, j) for f in range(4) for j in range(2)]
    by_token = lambda c: [(c, "T", 0, 512, t) for t in range(NT)]
    sample = lambda c: [(c, "S", 0, 512, 0)]
    jobs = []
    for c in range(Q_CHUNK):
        jobs += prompt(c) + sample(c)
    jobs += prompt(Q_CHUNK) + sample(Q_CHUNK)
    jobs += interleave_turns(prompt(K_CHUNK)) + sample(K_CHUNK)
    jobs += by_token(V_CHUNK) + sample(V_CHUNK)
    return jobs + by_token(Z_CHUNK) + sample(Z_CHUNK)


def interleave_turns(keys):
    out = []
    for n in range(len(keys) + 2):
        if n < len(keys):
            out.append(keys[n])
        if n >= 2:
            c, _, col, w, j = keys[n - 2]
            out.append((c, "K", col, w, j))
    return out


def stage_mixer_projection(k):
    nc = k.nc
    jobs = projection_of_mixers()
    landed, made, kept = k.mx_landed, k.sem("mx_made"), k.sem("mx_kept")
    stored = [k.stored[f"mix{i}"] for i in range(4)]
    last_job = {c: max(n for n, j in enumerate(jobs) if j[0] == c) for c in range(len(CHUNKS))}
    k.landed_at = {c: 16 * (c // 2 + 1) for c in range(len(CHUNKS))}
    staged = [n for n, j in enumerate(jobs) if Q_CHUNK <= j[0] <= V_CHUNK and j[1] != "S"]
    k.slot_of = {n: i % 4 for i, n in enumerate(staged)}
    order = {n: i for i, n in enumerate(staged)}
    k.turn_of = {n: jobs.index((K_CHUNK, "F") + j[2:]) for n, j in enumerate(jobs) if j[1] == "K"}
    turned_by = {m: n for n, m in k.turn_of.items()}
    xc = k.view(k.xc_at, CF, SEQ + CW - 1)
    z = k.view(k.z_at, NT, GW)
    stage = [k.view(k.stage_at + i * 512, 512) for i in range(4)]
    tap = [k.view(k.stage_at + j * 512, 512) for j in range(CW)]
    tapped, added, silued, padded = k.sem("mx_tapped"), k.sem("mx_added"), k.sem("mx_silu"), k.sem("mx_padded")
    pieces = [(n, c * 4 + col // P, at) for n, (c, kind, col, wd, at) in enumerate(jobs) if c < Q_CHUNK and kind == "F"]
    work = k.topk.work
    masks = [k.maskP[t] for t in range(FIRST_SEL, NT)] + [k.maskS]
    with nc.Block() as block:
        @block.sync
        def _(sp):
            for c in range(2, len(CHUNKS)):
                sp.wait_ge(made, last_job[c - 2] + 1)
                load_mixer_weights(k, sp, c)

        @block.tensor
        def _(pe):
            project_products(k, pe, jobs, 8, (landed, made, kept))

        @block.scalar
        def _(act):
            def silu(i):
                _, f, at = pieces[i]
                act.wait_ge(added, (CW - 1) * (i + 1))
                act.activation(xc[:, f, at * 512:(at + 1) * 512], tap[0], ACT.Silu).then_inc(silued, 1)

            for n, (c, kind, col, wd, at) in enumerate(jobs):
                act.wait_ge(made, n + 1)
                bank = k.psum[n % 8]
                if kind == "S":
                    dst = (k.psC[0:NS, c * 512:(c + 1) * 512] if c < Q_CHUNK else
                           k.psA[0:NS, (c - Q_CHUNK) * 512:(c - Q_CHUNK + 1) * 512] if c <= V_CHUNK else k.psZ[0:NS, :])
                    act.copy(dst, bank[0:NS, :]).then_inc(kept, 1)
                elif c < Q_CHUNK:
                    act.copy(xc[:, c * 4 + col // P, CW - 1 + at * 512:CW - 1 + (at + 1) * 512], bank[:, :]).then_inc(kept, 1)
                    i = pieces.index((n, c * 4 + col // P, at))
                    if i:
                        silu(i - 1)
                        act.wait_ge(silued, i)
                    act.wait_ge(padded, 1)
                    act.wait_ge(kept, n + 1)
                    for j in range(CW):
                        act.activation(tap[j], xc[:, c * 4 + col // P, at * 512 + j:at * 512 + j + 512], ACT.Copy,
                                       scale=k.conv_w[:, c * 4 + col // P, j:j + 1]).then_inc(tapped, 1)
                elif c <= V_CHUNK:
                    i = order[n]
                    if i >= 4:
                        act.wait_ge(stored[i % 4], 16 * (i // 4))
                        if staged[i - 4] in turned_by:
                            act.wait_ge(made, turned_by[staged[i - 4]] + 1)
                    elif i == 0:
                        silu(len(pieces) - 1)
                        act.wait_ge(silued, len(pieces))
                    act.activation(stage[i % 4], bank[:, :], ACT.Copy, scale=HD ** -0.5 if c == Q_CHUNK else 1.0).then_inc(kept, 1)
                else:
                    act.copy(z[:, at, :], bank[:, :]).then_inc(kept, 1)

        @block.gpsimd
        def _(pool):
            pool.memset(xc[:, :, 0:CW - 1], 0.0).then_inc(padded, 1)
            for i in range(len(pieces)):
                for j in range(1, CW):
                    pool.wait_ge(tapped, CW * i + j + 1)
                    if j > 1:
                        pool.wait_ge(added, (CW - 1) * i + j - 1)
                    pool.tensor_tensor(tap[0], tap[0], tap[j], ALU.add).then_inc(added, 1)
            for i, n in enumerate(staged):
                c, kind, col, wd, at = jobs[n]
                pool.wait_ge(kept, n + 1)
                if c == Q_CHUNK:
                    dst, src = k.a["q_T"][col:col + P, at * 512:(at + 1) * 512], stage[i % 4]
                elif c == K_CHUNK and kind == "F":
                    dst, src = k.a["k_T"][col:col + P, at * 512:(at + 1) * 512], stage[i % 4]
                elif c == K_CHUNK:
                    rows = k.a["new_k_prompt"][0, 0].rearrange("t h d -> t (h d)").rearrange("(j i p) n -> j p i n", i=4, p=P)
                    dst, src = rows[at, :, :, col:col + P], stage[i % 4].rearrange("p (i n) -> p i n", i=4)
                else:
                    dst, src = k.a["new_v_prompt"][0, 0].rearrange("t h d -> t (h d)")[at * P:(at + 1) * P, :], stage[i % 4]
                pool.dma_start(dst, src).then_inc(stored[i % 4], 16)
            for i in range(4):
                pool.wait_ge(stored[i], 16 * len(staged[i::4]))

        @block.vector
        def _(dve):
            rounds = TOPK // 8
            for r in range(rounds):
                k.topk.round(dve, (k.topk.prompt if r + EARLY_ROUNDS < rounds else []) + [k.topk.sample])
            for i, (rows, sc) in enumerate(work):
                dve.wait_ge(k.topk.taken, k.topk.last[i])
                dve.tensor_scalar(masks[i][0:rows, :], sc[0:rows, :], TAKEN, MASKED, ALU.not_equal, ALU.mult)


def stage_conv(k):
    nc, a = k.nc, k.a
    xc = k.view(k.xc_at, CF, SEQ + CW - 1)
    n_all = NT + 1
    m = Map(k.free_at)
    k.qkvS = k.view(m.take(CF * NS), CF, NS)
    k.gates = k.view(m.take(4 * n_all * G), 4, n_all * G)
    k.gdn_at = m.at
    k.lengths = L = Lengths(k)
    state = k.view(m.take(CC), CC)
    tail = k.view(m.take(CC), CC)
    xs = k.view(m.take(CF * DB * (DS + CW - 1)), CF * DB, DS + CW - 1)
    tap = [k.view(m.take(CF * NS), CF * DB, DS) for _ in range(2)]
    ab = k.view(m.take(n_all * 2 * G), n_all, 2 * G)
    w = [k.view(m.take(n_all * G), n_all, G) for _ in range(7)]
    alog = k.view(m.take(G), G)
    assert m.at <= k.lengths_at
    landed, out_sem = k.sem("cv_landed"), k.stored["conv"]
    turned, tails, laid = k.sem("cv_turned"), k.sem("cv_tails"), k.sem("cv_laid")
    tapped_s = k.sem("cv_tapped_sample")
    gate_v, gate_s = k.sem("cv_gate_vector"), k.sem("cv_gate_scalar")
    with nc.Block() as block:
        @block.sync
        def _(sp):
            sp.dma_start(state[0:DB * (CW - 1), :], a["state_conv"][0].rearrange("b j c -> (b j) c")).then_inc(landed, 16)
            n = 0
            for b in range(DB):
                sp.dma_start(a["new_conv_sample"][0, b], k.psC[b * DS + DS - CW + 1:(b + 1) * DS, :]).then_inc(out_sem, 16)
            sp.dma_start(a["new_k_sample"][0].rearrange("b t h d -> (b t) (h d)"), k.psA[0:NS, AW:2 * AW]).then_inc(out_sem, 16)
            sp.dma_start(a["new_v_sample"][0].rearrange("b t h d -> (b t) (h d)"), k.psA[0:NS, 2 * AW:3 * AW]).then_inc(out_sem, 16)
            sp.wait_ge(tails, 3)
            sp.dma_start(a["new_conv_prompt"][0, 0], tail[0:CW - 1, :]).then_inc(out_sem, 16)
            sp.wait_ge(out_sem, 16 * (DB + 3))

        @block.tensor
        def _(pe):
            for f in range(CF):
                last = pe.transpose(k.psum[f // 4][0:CW - 1, (f % 4) * P:(f % 4 + 1) * P], xc[:, f, SEQ:SEQ + CW - 1], k.c["ident"])
            for f in range(CF):
                last = pe.transpose(k.psum[4 + f // 6][:, (f % 6) * NS:(f % 6 + 1) * NS], k.psC[0:NS, f * P:(f + 1) * P], k.c["ident"][0:NS, 0:NS])
            pe.wait_ge(landed, 16)
            n = DB * (CW - 1)
            for f in range(CF):
                last = pe.transpose(k.psum[3][:, f * n:(f + 1) * n], state[0:n, f * P:(f + 1) * P], k.c["ident"][0:n, 0:n])
            last.then_inc(turned, 1)
            pe.wait_ge(L.zeroed, 6)
            for n, item in enumerate(L.prompt):
                L.sum(pe, k.psum[6], n, item, n == 0, n == len(L.prompt) - 1)

        @block.scalar
        def _(act):
            act.wait_ge(turned, 1)
            for i in range(3):
                act.copy(tail[0:CW - 1, i * 512:(i + 1) * 512], k.psum[i][0:CW - 1, :]).then_inc(tails, 1)
            for n, item in enumerate(L.prompt):
                L.square(act, n, item)
            act.wait_ge(gate_v, 4)
            act.activation(alog, k.a_row[:, 0:G], ACT.Exp).then_inc(gate_s, 1)
            act.activation(w[1], w[0], ACT.Abs).then_inc(gate_s, 1)
            act.wait_ge(gate_s, 2)
            act.activation(w[2], w[1], ACT.Exp, scale=-1.0).then_inc(gate_s, 1)
            act.activation(w[3], ab[:, :, G:2 * G], ACT.Exp, scale=-1.0).then_inc(gate_s, 1)
            act.wait_ge(gate_s, 4)
            act.activation(w[4], w[2], ACT.Ln, bias=1.0).then_inc(gate_s, 1)
            act.activation(w[5], w[3], ACT.Ln, bias=1.0).then_inc(gate_s, 1)
            act.wait_ge(L.summed, len(L.prompt))
            act.wait_ge(L.zeroed, 6)
            L.take_root(act, k.psum[6], 512)
            act.wait_ge(tapped_s, 7)
            act.activation(k.qkvS.rearrange("p f n -> p (f n)"), tap[1].rearrange("p f n -> p (f n)"), ACT.Silu)

        @block.vector
        def _(dve):
            L.prepare(dve)
            dve.memset(ab, 0.0).then_inc(gate_v, 1)
            dve.wait_ge(gate_v, 1)
            dve.tensor_copy(ab[:, 0:NT, :], k.kiwi[:, :, DI + NI:DI + NI + 2 * G]).then_inc(gate_v, 1)
            dve.tensor_copy(ab[0:NS, NT, :], k.psI[0:NS, IX_A:IX_A + 2 * G]).then_inc(gate_v, 1)
            dve.wait_ge(gate_v, 3)
            dve.tensor_tensor(w[0], ab[:, :, 0:G], k.a_row[:, G:2 * G].unsqueeze(1).to_broadcast([P, n_all, G]), ALU.add).then_inc(gate_v, 1)
            dve.wait_ge(turned, 1)
            dve.tensor_copy(xs[:, :, 0:CW - 1], k.psum[3][:, 0:CF * DB * (CW - 1)].rearrange("p (f j) -> p f j", j=CW - 1)).then_inc(laid, 1)
            for i in range(2):
                dve.tensor_copy(xs[:, i * 6 * DB:(i + 1) * 6 * DB, CW - 1:], k.psum[4 + i][:, 0:6 * NS].rearrange("p (f j) -> p f j", j=DS)).then_inc(laid, 1)
            g, beta, lnb = (k.gates[:, i, :].rearrange("p (t h) -> p t h", h=G) for i in range(3))
            dve.wait_ge(gate_s, 6)
            dve.scalar_tensor_tensor(out=w[6], in0=w[0], scalar=0.0, in1=w[4], op0=ALU.max, op1=ALU.add).then_inc(gate_v, 1)
            dve.tensor_scalar(lnb, w[5], -1.0, None, ALU.mult)
            dve.tensor_scalar(w[3], w[3], 1.0, None, ALU.add).then_inc(gate_v, 1)
            dve.wait_ge(gate_v, 6)
            dve.scalar_tensor_tensor(out=g, in0=w[6], scalar=-1.0, in1=alog.unsqueeze(1).to_broadcast([P, n_all, G]),
                                     op0=ALU.mult, op1=ALU.mult)
            dve.reciprocal(beta, w[3])
            dve.wait_ge(laid, 3)
            n = 0
            xs4 = xs.rearrange("p (f b) j -> p f b j", b=DB)
            t4 = [t.rearrange("p (f b) j -> p f b j", b=DB) for t in tap]
            for j in range(CW):
                wj = k.conv_w[:, :, j:j + 1].unsqueeze(3).to_broadcast([P, CF, DB, DS])
                if j >= 2:
                    dve.wait_ge(tapped_s, n)
                dve.tensor_tensor(t4[0 if j else 1], xs4[:, :, :, j:j + DS], wj, ALU.mult).then_inc(tapped_s, 1)
                n += 1
                if j:
                    dve.wait_ge(tapped_s, n)
                    dve.tensor_tensor(tap[1], tap[1], tap[0], ALU.add).then_inc(tapped_s, 1)
                    n += 1
            L.invert(dve, 0, 512)


def gdn_view(k, t, part):
    if t == NT:
        return k.qkvS[:, part * G:(part + 1) * G, :]
    return k.view(k.xc_at, CF, SEQ + CW - 1)[:, part * G:(part + 1) * G, t * P:(t + 1) * P]


class Lengths:

    KEY_ROW = 32

    def __init__(self, k):
        xc = k.view(k.xc_at, CF, SEQ + CW - 1)
        self.prompt = [(xc[:, f, j * 512:(j + 1) * 512], 512, (f % G) * 2 + j + (0 if f < G else self.KEY_ROW))
                       for f in range(2 * G) for j in range(2)]
        self.sample = [(k.qkvS[:, part * G:(part + 1) * G, :].rearrange("p f n -> p (f n)"), G * NS, 2 * G + part * self.KEY_ROW)
                       for part in range(2)]
        self.n_rows = 2 * G + 1
        self.rows = self.KEY_ROW + self.n_rows
        m = Map(k.lengths_at)
        self.sq = [k.view(m.take(512), 512) for _ in range(4)]
        self.root = k.view(m.take(512), 512)
        self.inv = [k.view(m.take(512), 512), k.view(m.take(G * NS), G * NS)]
        self.pick = [k.view(m.take(2 * self.rows), 2 * self.rows) for _ in range(2)]
        self.spread = k.view(m.take(2 * self.n_rows * P), 2 * self.n_rows, P)
        self.eps = k.view(m.take(1), 1)
        assert m.at <= k.words
        self.zeroed, self.squared, self.summed = k.sem("l2_zeroed"), k.sem("l2_squared"), k.sem("l2_summed")
        self.rooted, self.inverted = k.sem("l2_rooted"), k.sem("l2_inverted")

    def prepare(self, dve):
        for part in range(2):
            dve.memset(self.pick[part], 0.0).then_inc(self.zeroed, 1)
        dve.memset(self.eps[0:self.KEY_ROW, :], EPS * DK).then_inc(self.zeroed, 1)
        dve.memset(self.eps[self.KEY_ROW:2 * self.KEY_ROW, :], EPS).then_inc(self.zeroed, 1)
        dve.wait_ge(self.zeroed, 2)
        for part in range(2):
            dve.memset(self.pick[part][:, self.rows - 1:self.rows], 1.0 if part else float(DK)).then_inc(self.zeroed, 1)

    def square(self, act, n, item):
        src, w, row = item
        if n >= 4:
            act.wait_ge(self.summed, n - 3)
        act.activation(self.sq[n % 4][:, 0:w], src, ACT.Square).then_inc(self.squared, 1)

    def sum(self, pe, bank, n, item, start, stop):
        src, w, row = item
        one = self.pick[row // self.KEY_ROW][:, self.rows - 1 - row:2 * self.rows - 1 - row]
        pe.wait_ge(self.squared, n + 1)
        pe.matmul(bank[0:self.rows, 0:w], one, self.sq[n % 4][:, 0:w], start=start, stop=stop).then_inc(self.summed, 1)

    def take_root(self, act, bank, w):
        act.activation(self.root[0:self.rows, 0:w], bank[0:self.rows, 0:w], ACT.Sqrt, bias=self.eps[0:self.rows, :]).then_inc(self.rooted, 1)

    def invert(self, dve, which, w):
        dve.wait_ge(self.rooted, which + 1)
        dve.reciprocal(self.inv[which][0:self.rows, 0:w], self.root[0:self.rows, 0:w]).then_inc(self.inverted, 1)


def stage_l2norm(k, gates):
    nc = k.nc
    L = k.lengths
    ready, wide, scaled = (k.sem("l2_" + n) for n in ("ready", "wide", "scaled"))
    items = [(0, item) for item in L.prompt] + [(1, item) for item in L.sample]
    NPI = len(L.prompt)
    z, z_silu = k.view(k.z_at, NT * GW), k.sem("l2_z_silu")
    with nc.Block() as block:
        @block.gpsimd
        def _(pool):
            for part in range(2):
                at = part * L.KEY_ROW
                pool.tensor_copy(L.spread[0:L.rows, part * L.n_rows:(part + 1) * L.n_rows, :],
                                 k.c["ident"][0:L.rows, at:at + L.n_rows].unsqueeze(2).to_broadcast([L.rows, L.n_rows, P])).then_inc(ready, 1)
            for i in range(NT):
                pool.wait_ge(z_silu, i // 2 + 1)
                zi = z[:, i * GW:(i + 1) * GW]
                pool.tensor_tensor(zi, zi, k.gdn_row.rearrange("p h d -> p (h d)"), ALU.mult)
            pool.wait_ge(z_silu, 5)
            pool.tensor_tensor(k.psZ[0:NS, :], k.psZ[0:NS, :], k.gdn_row[0:NS].rearrange("p h d -> p (h d)"), ALU.mult)

        @block.scalar
        def _(act):
            for i, item in enumerate(L.sample):
                L.square(act, NPI + i, item)
            act.wait_ge(L.summed, NPI + len(L.sample))
            act.wait_ge(L.inverted, 1)
            L.take_root(act, k.psum[3], G * NS)
            gates.scalar(act)
            for i in range(4):
                act.activation(z[:, i * 1024:(i + 1) * 1024], z[:, i * 1024:(i + 1) * 1024], ACT.Silu).then_inc(z_silu, 1)
            act.activation(k.psZ[0:NS, :], k.psZ[0:NS, :], ACT.Silu).then_inc(z_silu, 1)

        @block.tensor
        def _(pe):
            gates.tensor(pe)
            for i, item in enumerate(L.sample):
                L.sum(pe, k.psum[3], NPI + i, item, i == 0, i == len(L.sample) - 1)
            pe.wait_ge(ready, 2)
            for n, (which, (src, w, row)) in enumerate(items):
                if n >= 4:
                    pe.wait_ge(scaled, n - 3)
                pe.wait_ge(L.inverted, which + 1)
                pe.matmul(k.psum[4 + n % 4][:, 0:w], L.spread[0:L.rows, row // L.KEY_ROW * L.n_rows + row % L.KEY_ROW, :],
                          L.inv[which][0:L.rows, 0:w], start=True, stop=True).then_inc(wide, 1)

        @block.vector
        def _(dve):
            gates.vector(dve)
            L.invert(dve, 1, G * NS)
            for n, (which, (src, w, row)) in enumerate(items):
                dve.wait_ge(wide, n + 1)
                dve.tensor_tensor(src, src, k.psum[4 + n % 4][:, 0:w], ALU.mult).then_inc(scaled, 1)
            gates.vector_last(dve)


def stage_gates(k):
    m = Map(k.gdn_at)
    k.AQ = [k.view(m.take(512), G, P) for _ in range(NT + 1)]
    k.KD = [k.view(m.take(512), G, P) for _ in range(NT + 1)]
    k.uS = k.view(m.take(512), G, P)
    n = (NT + 1) * G
    k.decay_sum, k.gcb, k.ngc, k.egc, k.ebc, k.ekd, k.egl, k.gl, k.t1 = (k.view(m.take(n), NT + 1, G) for _ in range(9))
    k.gb = k.view(m.take(DB * G), DB, G)
    k.eglS = k.view(m.take(DB * G), DB * G)
    k.temp_at = (m.take(8 * 512), k.hT_at)
    k.sc_spare = m.take(3 * 512 + 3 * n)
    assert m.at <= k.words, m.at
    g, beta, lnb = (k.gates[:, i, :].rearrange("p (t h) -> p t h", h=G) for i in range(3))
    summed, base, diff, done = k.sem("gt_summed"), k.sem("gt_base"), k.sem("gt_diff"), k.sem("gt_exp")
    np_ = NT * G
    flat = lambda x: x.rearrange("p t h -> p (t h)")

    class Steps:

        @staticmethod
        def tensor(pe):
            gf = flat(g)
            pe.matmul(k.psum[0][:, 0:np_], k.c["tri"], gf[:, 0:np_], start=True, stop=True)
            pe.matmul(k.psum[0][:, np_:n], k.c["tri_s"], gf[:, np_:n], start=True, stop=True)
            pe.matmul(k.psum[1][:, 0:np_], k.c["ones"], gf[:, 0:np_], start=True, stop=True)
            pe.matmul(k.psum[1][:, np_:n], k.c["block_s"], gf[:, np_:n], start=True, stop=True)
            pe.wait_ge(base, 1)
            pe.matmul(k.psum[2][:, 0:DB * G], k.c["ones"][0:NS, :], k.gb[0:NS].rearrange("p b h -> p (b h)"), start=True, stop=True).then_inc(summed, 1)

        @staticmethod
        def vector(dve):
            dve.tensor_tensor(k.gb[0:NS], k.c["in_batch"][0:NS].unsqueeze(2).to_broadcast([NS, DB, G]),
                              g[0:NS, NT:NT + 1, :].to_broadcast([NS, DB, G]), ALU.mult).then_inc(base, 1)
            dve.wait_ge(summed, 1)
            dve.tensor_copy(flat(k.decay_sum), k.psum[0][:, 0:n]).then_inc(base, 1)
            dve.tensor_copy(flat(k.gl), k.psum[1][:, 0:n]).then_inc(base, 1)
            dve.wait_ge(base, 3)
            dve.tensor_tensor(flat(k.gcb), flat(k.decay_sum), flat(lnb), ALU.add).then_inc(diff, 1)
            dve.tensor_scalar(flat(k.ngc), flat(k.decay_sum), -1.0, None, ALU.mult).then_inc(diff, 1)
            dve.tensor_tensor(flat(k.t1), flat(k.gl), flat(k.decay_sum), ALU.subtract).then_inc(diff, 1)

        @staticmethod
        def vector_last(dve):
            dve.wait_ge(done, 1)
            dve.tensor_tensor(flat(k.ebc), flat(k.egc), flat(beta), ALU.mult)

        @staticmethod
        def scalar(act):
            act.wait_ge(diff, 3)
            act.activation(flat(k.egc), flat(k.decay_sum), ACT.Exp).then_inc(done, 1)
            act.activation(flat(k.egl), flat(k.gl), ACT.Exp)
            act.activation(flat(k.ekd), flat(k.t1), ACT.Exp)
            act.activation(k.eglS, k.psum[2][:, 0:DB * G], ACT.Exp)

    return Steps


PAIRS = [(0, 1), (2, 3), (4, 5), (6, 7), (8,)]


def stage_chunks(k):
    nc = k.nc
    S = 2
    t_at = [Map(at) for at in k.temp_at]
    kbe, vb, Lm, X, TG = ([k.view(m.take(512), G, P) for m in t_at] for _ in range(5))
    ZM = [k.view(m.take(1024), 2 * G, P) for m in t_at]
    beta = k.gates[:, 1, :].rearrange("p (t h) -> p t h", h=G)
    g = k.gates[:, 0, :].rearrange("p (t h) -> p t h", h=G)
    names = ("spread", "turned", "decay", "kept", "gram", "built", "first", "x_made", "masked", "y_made", "grown", "solved", "left")
    (spread, turned, decay, kept, gram, built, first, x_made, masked, y_made, grown, solved, left) = (k.sems("ch_" + n, S) for n in names)
    decayed, low_made = k.sems("ch_decayed", S), k.sems("ch_low_made", S)
    levels = lambda t: LEVELS if t < NT else S_LEVELS
    steps = LEVELS

    def bank(s, i, r):
        return k.psum[4 * s + i].rearrange("p (h n) -> p h n", h=G)[0:r, :, 0:r]

    with nc.Block() as block:
        @block.tensor
        def _(pe):
            for i, pair in enumerate(PAIRS):
                for s, t in enumerate(pair):
                    r = rows_of(t)
                    if i:
                        pe.wait_ge(left[s], 2 * i)
                    for part, b in ((1, 0), (2, 1)):
                        for h in range(G):
                            last = pe.transpose(k.psum[4 * s + b][0:r, h * P:(h + 1) * P], gdn_view(k, t, part)[:, h, :], k.c["ident"])
                    last.then_inc(turned[s], 1)
                    pe.wait_ge(spread[s], i + 1)
                    for b, mask in ((2, "low_big"), (3, "up_big")):
                        mask = k.b[mask if t < NT else mask + "_s"][0:r, 0:r].unsqueeze(1).to_broadcast([r, G, r])
                        pe.matmul(bank(s, b, r), k.c["ones"][0:r, 0:r], TG[s][0:r, :, 0:r], start=True, stop=False)
                        last = pe.matmul(bank(s, b, r), k.b["ident"][0:r, 0:r], mask, start=False, stop=True)
                    last.then_inc(decay[s], 1)
                for s, t in enumerate(pair):
                    r = rows_of(t)
                    pe.wait_ge(kept[s], i + 1)
                    kT, qT = gdn_view(k, t, 1), gdn_view(k, t, 0)
                    for h in range(G):
                        pe.matmul(bank(s, 0, r)[:, h, :], kT[:, h, :], kT[:, h, :], start=True, stop=True)
                    for h in range(G):
                        last = pe.matmul(bank(s, 1, r)[:, h, :], kT[:, h, :], qT[:, h, :], start=True, stop=True)
                    last.then_inc(gram[s], 1)
                for l in range(steps):
                    for s, t in enumerate(pair):
                        if l >= levels(t):
                            continue
                        r = rows_of(t)
                        if l == 0:
                            pe.wait_ge(built[s], i + 1)
                        else:
                            if l == 1:
                                pe.wait_ge(low_made[s], 2 * i + 2)
                            pe.wait_ge(grown[s], LEVELS * i + l)
                        for h in range(G):
                            if l == 0:
                                last = pe.transpose(bank(s, 2, r)[:, h, :], Lm[s][0:r, h, 0:r], k.c["ident"][0:r, 0:r])
                            else:
                                last = pe.matmul(bank(s, 2, r)[:, h, :], Lm[s][0:r, h, 0:r], ZM[s][0:r, h, 0:r], start=True, stop=True)
                        last.then_inc(x_made[s], 1)
                    for s, t in enumerate(pair):
                        if l >= levels(t) or l == 0:
                            continue
                        r = rows_of(t)
                        pe.wait_ge(masked[s], (LEVELS - 1) * i + l)
                        for h in range(G):
                            last = pe.matmul(bank(s, 0, r)[:, h, :], ZM[s][0:r, G + h, 0:r], X[s][0:r, h, 0:r], start=True, stop=True)
                        if l < levels(t) - 1:
                            for h in range(G):
                                last = pe.matmul(bank(s, 1, r)[:, h, :], X[s][0:r, h, 0:r], ZM[s][0:r, G + h, 0:r], start=True, stop=True)
                        last.then_inc(y_made[s], 1)
                for s, t in enumerate(pair):
                    r = rows_of(t)
                    pe.wait_ge(grown[s], LEVELS * i + levels(t))
                    for h in range(G):
                        pe.matmul(k.psum[4 * s + 2][0:r, h * P:(h + 1) * P], ZM[s][0:r, h, 0:r], vb[s][0:r, h, :], start=True, stop=True)
                    for h in range(G):
                        last = pe.matmul(k.psum[4 * s + 3][:, h * P:h * P + r], kbe[s][0:r, h, :], ZM[s][0:r, h, 0:r], start=True, stop=True)
                    last.then_inc(solved[s], 1)

        @block.scalar
        def _(act):
            for i, pair in enumerate(PAIRS):
                for s, t in enumerate(pair):
                    r = rows_of(t)
                    act.wait_ge(decay[s], i + 1)
                    for h in range(G):
                        act.activation(Lm[s][0:r, h, 0:r], bank(s, 2, r)[:, h, :], ACT.Exp, scale=-1.0, bias=k.gcb[0:r, t, h:h + 1])
                        last = act.activation(k.AQ[t][0:r, h, 0:r], bank(s, 3, r)[:, h, :], ACT.Exp, bias=k.ngc[0:r, t, h:h + 1])
                    last.then_inc(decayed[s], 1)
                for s, t in enumerate(pair):
                    r = rows_of(t)
                    act.wait_ge(solved[s], i + 1)
                    u = k.uS[0:NS] if t == NT else gdn_view(k, t, 2)
                    act.copy(u, k.psum[4 * s + 2][0:r, :].rearrange("p (h n) -> p h n", h=G)).then_inc(left[s], 1)
                    act.copy(gdn_view(k, t, 1), k.psum[4 * s + 3][:, :].rearrange("p (h n) -> p h n", h=G)[:, :, 0:r]).then_inc(left[s], 1)

        @block.gpsimd
        def _(pool):
            for i, pair in enumerate(PAIRS):
                for s, t in enumerate(pair):
                    r = rows_of(t)
                    ident, low = (c[0:r, 0:r].unsqueeze(1).to_broadcast([r, G, r]) for c in (k.c["ident"], k.b["first_low"]))
                    pool.wait_ge(built[s], i + 1)
                    pool.tensor_tensor(TG[s][0:r, :, 0:r], Lm[s][0:r, :, 0:r], low, ALU.mult).then_inc(low_made[s], 1)
                    pool.wait_ge(low_made[s], 2 * i + 1)
                    if i:
                        pool.wait_ge(solved[s], i)
                    pool.tensor_tensor(ZM[s][0:r, G:2 * G, 0:r], TG[s][0:r, :, 0:r], ident, ALU.add).then_inc(low_made[s], 1)

        @block.vector
        def _(dve):
            for i, pair in enumerate(PAIRS):
                for s, t in enumerate(pair):
                    r = rows_of(t)
                    tri = k.c["tri" if t < NT else "tri_s"][0:r, 0:r].unsqueeze(1).to_broadcast([r, G, r])
                    if i:
                        dve.wait_ge(decay[s], i)
                        dve.wait_ge(low_made[s], 2 * i)
                    dve.tensor_tensor(TG[s][0:r, :, 0:r], tri, g[0:r, t, :].unsqueeze(2).to_broadcast([r, G, r]), ALU.mult).then_inc(spread[s], 1)
                for s, t in enumerate(pair):
                    r = rows_of(t)
                    wide = lambda x: x[0:r, t, :].unsqueeze(2).to_broadcast([r, G, P])
                    kk, vv = (k.psum[4 * s + b][0:r, :].rearrange("p (h n) -> p h n", h=G) for b in (0, 1))
                    dve.wait_ge(turned[s], i + 1)
                    if i:
                        dve.wait_ge(solved[s], i)
                    dve.tensor_tensor(kbe[s][0:r], kk, wide(k.ebc), ALU.mult)
                    dve.tensor_tensor(k.KD[t][0:r], kk, wide(k.ekd), ALU.mult)
                    dve.tensor_tensor(vb[s][0:r], vv, wide(beta), ALU.mult).then_inc(kept[s], 1)
                for s, t in enumerate(pair):
                    r = rows_of(t)
                    dve.wait_ge(gram[s], i + 1)
                    dve.wait_ge(decayed[s], i + 1)
                    L, A = Lm[s][0:r, :, 0:r], k.AQ[t][0:r, :, 0:r]
                    dve.tensor_tensor(L, bank(s, 0, r), L, ALU.mult)
                    dve.tensor_tensor(A, bank(s, 1, r), A, ALU.mult).then_inc(built[s], 1)
                for l in range(steps):
                    for s, t in enumerate(pair):
                        if l >= levels(t):
                            continue
                        r = rows_of(t)
                        dve.wait_ge(x_made[s], LEVELS * i + l + 1)
                        if l == 0:
                            ident = k.c["ident"][0:r, 0:r].unsqueeze(1).to_broadcast([r, G, r])
                            up = k.b["level"][0:r, 0:r].unsqueeze(1).to_broadcast([r, G, r])
                            dve.tensor_tensor(X[s][0:r, :, 0:r], bank(s, 2, r), up, ALU.mult).then_inc(first[s], 1)
                            dve.wait_ge(first[s], i + 1)
                            dve.tensor_tensor(ZM[s][0:r, 0:G, 0:r], X[s][0:r, :, 0:r], ident, ALU.add).then_inc(grown[s], 1)
                            continue
                        mask = k.b["level"][0:r, l * P:l * P + r].unsqueeze(1).to_broadcast([r, G, r])
                        dve.tensor_tensor(X[s][0:r, :, 0:r], bank(s, 2, r), mask, ALU.mult).then_inc(masked[s], 1)
                    for s, t in enumerate(pair):
                        if l >= levels(t) or l == 0:
                            continue
                        r = rows_of(t)
                        n = G if l == levels(t) - 1 else 2 * G
                        dve.wait_ge(y_made[s], (LEVELS - 1) * i + l)
                        zm = ZM[s][0:r, 0:n, 0:r]
                        y = k.banks[0:r, 4 * s * 512:4 * s * 512 + n * P].rearrange("p (h n) -> p h n", h=n)[:, :, 0:r]
                        dve.tensor_tensor(zm, zm, y, ALU.add).then_inc(grown[s], 1)


def stage_scan(k):
    nc, a = k.nc, k.a
    mix = k.view(k.hT_at, KD, TOK)
    z = k.view(k.z_at, NT, G, DK)
    zS = k.psZ[0:NS, :].rearrange("p (h d) -> p h d", h=G)
    m = Map(k.temp_at[0])
    S0 = k.view(m.take(DB * G * DK), DB * G, DK)
    m = Map(k.temp_at[1])
    S = [k.view(m.take(512), G, DK) for _ in range(2)]
    vnew = [k.view(m.take(512), G, DK) for _ in range(2)]
    o = [k.view(m.take(512), G, DK) for _ in range(2)]
    sq = k.view(m.take(512), G, DK)
    masked = [k.psC[:, i * DB * NS:(i + 1) * DB * NS] for i in range(3)]
    units = [(part, h) for part in (1, 0) for h in range(G)]
    assert len(units) == NT
    vnm = k.view(k.temp_at[1], G, DB * DK)
    m = Map(k.sc_spare)
    vS, oS, sqS = (k.view(m.take(512), G, DK) for _ in range(3))
    stat = k.view(m.take(3 * G * (NT + 1)), 3, (NT + 1) * G)
    fade, fadeS = k.sem("sc_fade"), k.sem("sc_fadeS")
    names = ("ws", "qs", "vnew", "av", "kv", "state", "scaled", "out", "sq", "sum", "root", "inv", "norm", "gated", "turned", "kept")
    (ws, qs, vn, av, kv, state, faded, outs, sqd, sm, root, inv, normed, gated, turned, kept) = (k.sem("sc_" + n) for n in names)
    landed, out_sem = k.sem("sc_landed"), k.stored["ssm"]
    mask_sem, with_state, vm_sem, kvS, addS = (k.sem("sc_" + n) for n in ("mask", "with_state", "vmask", "kvS", "addS"))
    heads = lambda b: b.rearrange("p (h n) -> p h n", h=G)
    n_all = NT + 1
    with nc.Block() as block:
        @block.sync
        def _(sp):
            sp.dma_start(S0, a["state_ssm"][0].rearrange("b h k v -> k (b h) v")).then_inc(landed, 16)
            sp.wait_ge(state, NT + 1)
            sp.dma_start(a["new_ssm_prompt"][0, 0].rearrange("h k v -> k h v"), S[NT % 2]).then_inc(out_sem, 16)
            sp.wait_ge(addS, 2 * G)
            sp.dma_start(a["new_ssm_sample"][0].rearrange("b h k v -> k (b h) v"), S0).then_inc(out_sem, 16)
            sp.wait_ge(out_sem, 32)

        @block.tensor
        def _(pe):
            def turn(t):
                r = rows_of(t)
                src = o[t % 2] if t < NT else oS
                pe.wait_ge(gated, t + 1)
                if t:
                    pe.wait_ge(kept, t)
                for h in range(G):
                    last = pe.transpose(k.psum[7][:, h * P:h * P + r], src[0:r, h, :], k.c["ident"][0:r, 0:r])
                last.then_inc(turned, 1)

            for t in range(NT):
                pe.wait_ge(state, t + 1)
                for h in range(G):
                    last = pe.matmul(heads(k.psum[0])[:, h, :], gdn_view(k, t, 1)[:, h, :], S[t % 2][:, h, :], start=True, stop=True)
                last.then_inc(ws, 1)
                if t:
                    pe.wait_ge(outs, t)
                for h in range(G):
                    last = pe.matmul(heads(k.psum[1])[:, h, :], gdn_view(k, t, 0)[:, h, :], S[t % 2][:, h, :], start=True, stop=True)
                last.then_inc(qs, 1)
                if t == 0:
                    pe.wait_ge(landed, 16)
                part, h = units[t]
                pe.wait_ge(mask_sem, t + 1)
                for b in range(DB):
                    last = pe.matmul(k.psum[4 if part else 5][0:NS, h * DK:(h + 1) * DK], masked[t % 3][:, b * NS:(b + 1) * NS],
                                     S0[:, b * G + h, :], start=(b == 0), stop=(b == DB - 1))
                last.then_inc(with_state, 1)
                pe.wait_ge(vn, t + 1)
                for h in range(G):
                    last = pe.matmul(heads(k.psum[2])[:, h, :], k.KD[t][:, h, :], vnew[t % 2][:, h, :], start=True, stop=True)
                last.then_inc(kv, 1)
                for h in range(G):
                    last = pe.matmul(heads(k.psum[3])[:, h, :], k.AQ[t][:, h, :], vnew[t % 2][:, h, :], start=True, stop=True)
                last.then_inc(av, 1)
                if t:
                    turn(t - 1)
            turn(NT - 1)
            pe.wait_ge(vn, NT + 1)
            for h in range(G):
                last = pe.matmul(k.psum[6][0:NS, h * DK:(h + 1) * DK], k.AQ[NT][0:NS, h, 0:NS], vS[0:NS, h, :], start=True, stop=True)
            last.then_inc(av, 1)
            pe.wait_ge(vm_sem, 1)
            for n in range(2 * G):
                h, half = n // 2, n % 2
                if n >= 4:
                    pe.wait_ge(addS, n - 3)
                pe.matmul(k.psum[n % 4][:, :], k.KD[NT][0:NS, h, :], vnm[0:NS, h, half * 512:(half + 1) * 512],
                          start=True, stop=True).then_inc(kvS, 1)
            turn(NT)

        @block.scalar
        def _(act):
            for t in range(n_all):
                r = rows_of(t)
                act.wait_ge(sm, t + 1)
                act.activation(stat[0:r, 1, t * G:(t + 1) * G], stat[0:r, 0, t * G:(t + 1) * G], ACT.Sqrt, scale=1.0 / DK, bias=k.eps[0:r, :]).then_inc(root, 1)
                act.wait_ge(turned, t + 1)
                act.copy(mix[:, KD // 2:KD, t * P:t * P + r], heads(k.psum[7])[:, :, 0:r]).then_inc(kept, 1)

        @block.vector
        def _(dve):
            def output(t, q_bank, a_bank, out, sqr, zz):
                r = rows_of(t)
                wide = lambda x: x.unsqueeze(2).to_broadcast([r, G, DK])
                if t < NT:
                    dve.wait_ge(qs, t + 1)
                else:
                    dve.wait_ge(with_state, len(units))
                if 2 <= t < NT:
                    dve.wait_ge(turned, t - 1)
                dve.tensor_tensor(out, heads(k.psum[q_bank])[0:r], wide(k.egc[0:r, t, :]), ALU.mult).then_inc(faded, 1)
                dve.wait_ge(av, t + 1)
                dve.wait_ge(faded, t + 1)
                dve.tensor_tensor(out, out, heads(k.psum[a_bank])[0:r], ALU.add).then_inc(outs, 1)
                dve.wait_ge(outs, t + 1)
                if t:
                    dve.wait_ge(sm, t)
                dve.tensor_tensor(sqr, out, out, ALU.mult).then_inc(sqd, 1)
                dve.wait_ge(sqd, t + 1)
                dve.reduce_sum(stat[0:r, 0, t * G:(t + 1) * G], sqr, AX_X).then_inc(sm, 1)
                dve.tensor_tensor(out, out, zz, ALU.mult).then_inc(normed, 1)
                dve.wait_ge(root, t + 1)
                dve.reciprocal(stat[0:r, 2, t * G:(t + 1) * G], stat[0:r, 1, t * G:(t + 1) * G]).then_inc(inv, 1)
                dve.wait_ge(inv, t + 1)
                dve.wait_ge(normed, t + 1)
                dve.tensor_tensor(out, out, wide(stat[0:r, 2, t * G:(t + 1) * G]), ALU.mult).then_inc(gated, 1)

            cm = k.b["columns"].rearrange("p (b n) -> p b n", b=DB)

            def mask(u):
                part, h = units[u]
                if u >= 3:
                    dve.wait_ge(with_state, u - 2)
                dve.tensor_tensor(masked[u % 3].rearrange("p (b n) -> p b n", b=DB), cm,
                                  gdn_view(k, NT, part)[:, h, :].unsqueeze(1).to_broadcast([P, DB, NS]), ALU.mult).then_inc(mask_sem, 1)

            dve.memset(S[0], 0.0).then_inc(state, 1)
            mask(0)
            for t in range(NT):
                old, new = S[t % 2], S[(t + 1) % 2]
                dve.wait_ge(state, t + 1)
                dve.tensor_tensor(new, old, k.egl[:, t, :].unsqueeze(2).to_broadcast([P, G, DK]), ALU.mult).then_inc(fade, 1)
                dve.wait_ge(ws, t + 1)
                if t >= 2:
                    dve.wait_ge(av, t - 1)
                dve.tensor_tensor(vnew[t % 2], gdn_view(k, t, 2), heads(k.psum[0]), ALU.subtract).then_inc(vn, 1)
                dve.wait_ge(kv, t + 1)
                dve.wait_ge(fade, t + 1)
                dve.tensor_tensor(new, new, heads(k.psum[2]), ALU.add).then_inc(state, 1)
                if t + 1 < len(units):
                    mask(t + 1)
                output(t, 1, 3, o[t % 2], sq, z[:, t])
            dve.wait_ge(turned, NT)
            dve.wait_ge(out_sem, 16)
            dve.wait_ge(with_state, G)
            dve.tensor_tensor(vS[0:NS], k.uS[0:NS], heads(k.psum[4])[0:NS], ALU.subtract).then_inc(vn, 1)
            dve.wait_ge(vn, NT + 1)
            for h in range(G):
                last = dve.tensor_tensor(vnm[0:NS, h, :].rearrange("p (b d) -> p b d", b=DB),
                                         vS[0:NS, h, :].unsqueeze(1).to_broadcast([NS, DB, DK]),
                                         k.c["in_batch"][0:NS].unsqueeze(2).to_broadcast([NS, DB, DK]), ALU.mult)
            last.then_inc(vm_sem, 1)
            output(NT, 5, 6, oS[0:NS], sqS[0:NS], zS)
            S0v = S0.rearrange("p (b h) v -> p b h v", h=G)
            eg = k.eglS.rearrange("p (b h) -> p b h", h=G)
            for n in range(2 * G):
                h, half = n // 2, n % 2
                part = S0v[:, 4 * half:4 * half + 4, h, :]
                dve.wait_ge(kvS, n + 1)
                dve.tensor_tensor(part, part, eg[:, 4 * half:4 * half + 4, h].unsqueeze(2).to_broadcast([P, 4, DK]), ALU.mult).then_inc(fadeS, 1)
                dve.wait_ge(fadeS, n + 1)
                dve.tensor_tensor(part, part, k.psum[n % 4].rearrange("p (b v) -> p b v", b=4), ALU.add).then_inc(addS, 1)


KV_RING = 4


class PageStream:

    def __init__(self, k):
        self.k = k
        self.units = [(it, c, b2) for it in range(DB // 2) for c in range(NPG // 4) for b2 in range(2)]
        m = Map(k.kv_at)
        self.keys = [k.view(m.take(4 * AW), 4, AW) for _ in range(KV_RING)]
        self.values = [k.view(m.take(4 * AW), 4, AW) for _ in range(KV_RING)]
        assert m.at <= k.words
        self.keys_landed, self.values_landed = k.sems("sa_k_landed", KV_RING), k.sems("sa_v_landed", KV_RING)

    def load(self, q, n, cache, ring, sems):
        it, c, b2 = self.units[n]
        for p in range(4):
            at = (2 * it + b2) * NPG + 4 * c + p
            page = q.value_load(self.k.table[0:1, at:at + 1], min_val=0, max_val=cache.shape[1] - 1)
            src = cache[0, bass.ds(page, 1), :, :, :].rearrange("a p h d -> p (a h d)")
            q.dma_start(ring[n % KV_RING][:, p, :], src).then_inc(sems[n % KV_RING], 16)

    def load_keys(self, q, n):
        self.load(q, n, self.k.a["cache_k"], self.keys, self.keys_landed)

    def load_values(self, q, n):
        self.load(q, n, self.k.a["cache_v"], self.values, self.values_landed)


def stage_prompt_attention(k):
    nc, a = k.nc, k.a
    m = Map(k.xc_at)
    qT, kT = (k.view(m.take(4 * SEQ), 4, SEQ) for _ in range(2))
    V = k.view(m.take(NT * AW), NT, AW)
    m = Map(k.z_at)
    prob = [k.view(m.take(SEQ), SEQ) for _ in range(2)]
    probT = [k.view(m.take(SEQ), SEQ) for _ in range(2)]
    m = Map(k.free_at)
    stat = k.view(m.take(3 * NT * H), 3, NT * H)
    mix = k.view(k.hT_at, KD, TOK)
    items = [(t, h) for t in range(NT) for h in range(H)]
    parts = [(0, 2 * P), (2 * P, 4 * P), (4 * P, SEQ)]
    first = {at // P: i for i, (at, _) in enumerate(parts)}
    qk_in, v_in = k.sems("pa_qk_landed", len(parts)), k.sems("pa_v_landed", len(parts))
    names = ("scores", "max", "exp", "inv", "scaled", "turned", "kept", "made", "out")
    scores, maxed, exped, inverted, scaled, turned, kept, made, out = (k.sem("pa_" + n) for n in names)
    n_items = len(items)
    k.stream = PageStream(k)
    with nc.Block() as block:
        @block.sync
        def _(sp):
            for i, (at, to) in enumerate(parts):
                tiles = slice(at // P, to // P)
                sp.dma_start(qT[:, :, at:to], a["q_T"].rearrange("(f p) n -> p f n", p=P)[:, :, at:to]).then_inc(qk_in[i], 16)
                sp.dma_start(kT[:, :, at:to], a["k_T"].rearrange("(f p) n -> p f n", p=P)[:, :, at:to]).then_inc(qk_in[i], 16)
                rows = a["new_v_prompt"][0, 0].rearrange("t h d -> t (h d)").rearrange("(t p) n -> p t n", p=P)
                sp.dma_start(V[:, tiles, :], rows[:, tiles, :]).then_inc(v_in[i], 16)
            for n in range(KV_RING):
                k.stream.load_keys(sp, n)

        @block.gpsimd
        def _(pool):
            for n in range(KV_RING):
                k.stream.load_values(pool, n)

        @block.tensor
        def _(pe):
            def score(n):
                t, h = items[n]
                lo = (h % 2) * HD
                if h == 0 and t in first:
                    pe.wait_ge(qk_in[first[t]], 32)
                if n >= 2:
                    pe.wait_ge(exped, n - 1)
                for c in range(0, (t + 1) * P, 512):
                    w = min(512, (t + 1) * P - c)
                    bank = k.psum[2 * (n % 2) + c // 512]
                    pe.matmul(bank[:, 0:w], qT[lo:lo + HD, h // 2, t * P:(t + 1) * P], kT[lo:lo + HD, h // 2, c:c + w], start=True, stop=False)
                    if t < FIRST_SEL:
                        last = pe.matmul(bank[:, t * P:(t + 1) * P], k.b["ident"], k.b["attn_causal"], start=False, stop=True)
                    else:
                        last = pe.matmul(bank[:, 0:w], k.b["ident"], k.maskP[t][:, c:c + w], start=False, stop=True)
                last.then_inc(scores, 1)

            def turn(n):
                t, h = items[n]
                pe.wait_ge(scaled, n + 1)
                if n:
                    pe.wait_ge(kept, n)
                for j in range(t + 1):
                    last = pe.transpose(k.psum[4 + j // 4][:, (j % 4) * P:(j % 4 + 1) * P], prob[n % 2][:, j * P:(j + 1) * P], k.c["ident"])
                last.then_inc(turned, 1)

            def values(n):
                t, h = items[n]
                lo = (h % 2) * HD
                if h == 0 and t in first:
                    pe.wait_ge(v_in[first[t]], 16)
                pe.wait_ge(kept, n + 1)
                if n >= 2:
                    pe.wait_ge(out, n - 1)
                for j in range(t + 1):
                    last = pe.matmul(k.psum[6 + n % 2][lo:lo + HD, 0:P], V[:, j, h * HD:(h + 1) * HD], probT[n % 2][:, j * P:(j + 1) * P],
                                     start=(j == 0), stop=(j == t))
                last.then_inc(made, 1)

            score(0)
            score(1)
            for n in range(n_items):
                turn(n)
                if n + 2 < n_items:
                    score(n + 2)
                values(n)

        @block.scalar
        def _(act):
            def exps(n):
                t, h = items[n]
                w = (t + 1) * P
                b0 = 2 * (n % 2) * 512
                act.wait_ge(maxed, n + 1)
                if n >= 2:
                    act.wait_ge(turned, n - 1)
                act.activation(prob[n % 2][:, 0:w], k.banks[:, b0:b0 + w], ACT.Exp, bias=stat[:, 0, n:n + 1],
                               accum_out=stat[:, 1, n:n + 1]).then_inc(exped, 1)

            exps(0)
            exps(1)
            for n in range(n_items):
                w = (items[n][0] + 1) * P
                act.wait_ge(turned, n + 1)
                if n >= 2:
                    act.wait_ge(made, n - 1)
                act.copy(probT[n % 2][:, 0:w], k.banks[:, 4 * 512:4 * 512 + w]).then_inc(kept, 1)
                if n + 2 < n_items:
                    exps(n + 2)

        @block.vector
        def _(dve):
            def maxes(n):
                w = (items[n][0] + 1) * P
                b0 = 2 * (n % 2) * 512
                dve.wait_ge(scores, n + 1)
                dve.tensor_reduce(stat[:, 0, n:n + 1], k.banks[:, b0:b0 + w], AX_X, ALU.max, negate=True).then_inc(maxed, 1)

            def keep(n):
                t, h = items[n]
                lo = (h % 2) * HD
                dve.wait_ge(made, n + 1)
                dve.tensor_copy(mix[lo:lo + HD, h // 2, t * P:(t + 1) * P], k.psum[6 + n % 2][lo:lo + HD, 0:P]).then_inc(out, 1)

            def scale(n):
                w = (items[n][0] + 1) * P
                dve.wait_ge(exped, n + 1)
                dve.reciprocal(stat[:, 2, n:n + 1], stat[:, 1, n:n + 1]).then_inc(inverted, 1)
                dve.wait_ge(inverted, n + 1)
                dve.tensor_scalar(prob[n % 2][:, 0:w], prob[n % 2][:, 0:w], stat[:, 2, n:n + 1], None, ALU.mult).then_inc(scaled, 1)

            maxes(0)
            maxes(1)
            scale(0)
            for n in range(n_items):
                if n + 1 < n_items:
                    scale(n + 1)
                if n + 2 < n_items:
                    maxes(n + 2)
                keep(n)


def stage_sample_attention(k):
    nc = k.nc
    IT = DB // 2
    NCH = NPG // 4
    m = Map(k.xc_at)
    kp, vp = k.stream.keys, k.stream.values
    kts = [k.view(m.take(4 * 512), 4, 512) for _ in range(2)]
    S = [k.view(m.take(LS), LS) for _ in range(2)]
    PT = k.view(m.take((NPG + 1) * P), NPG + 1, P)
    qblk = k.view(m.take(DB * 4 * 64), DB * 4, 64)
    ktn = k.view(m.take(4 * NS), 4, NS)
    osb = k.view(m.take(512), 512)
    stat = k.view(m.take(3 * IT), 3, IT)
    assert m.at <= k.kv_at
    mix = k.view(k.hT_at, KD, TOK)
    kl, vl = k.stream.keys_landed, k.stream.values_landed
    names = ("zero", "prep_pe", "prep", "k_turned", "kept_act", "kept_dve", "qk", "scores", "copied", "max", "exp", "inv",
             "p_turned", "p_kept", "v_used", "out", "out_kept", "o_turned", "laid")
    (zero, prep_pe, prep, k_turned, kept_a, kept_v, qk, scores, copied, maxed, exped, inverted, p_turned,
     p_kept, v_used, out, out_kept, o_turned, laid) = (k.sem("sa_" + n) for n in names)
    loads = k.stream.units
    PG = NCH + 1
    U = 2 * NCH

    with nc.Block() as block:
        @block.sync
        def _(sp):
            for n in range(KV_RING, len(loads)):
                sp.wait_ge(k_turned, 4 * (n - KV_RING + 1))
                k.stream.load_keys(sp, n)

        @block.gpsimd
        def _(pool):
            pool.memset(qblk, 0.0).then_inc(zero, 1)
            for n in range(KV_RING, len(loads)):
                pool.wait_ge(v_used, n - KV_RING + 1)
                k.stream.load_values(pool, n)

        @block.tensor
        def _(pe):
            for p in range(4):
                pe.transpose(k.psum[6][:, p * NS:(p + 1) * NS], k.psA[0:NS, p * P:(p + 1) * P], k.c["ident"][0:NS, 0:NS])
            for p in range(4):
                last = pe.transpose(k.psum[7][:, p * NS:(p + 1) * NS], k.psA[0:NS, AW + p * P:AW + (p + 1) * P], k.c["ident"][0:NS, 0:NS])
            last.then_inc(prep_pe, 1)
            pe.wait_ge(prep, 9)

            def turn(n):
                pe.wait_ge(kl[n % KV_RING], 64 * (n // KV_RING + 1))
                for p in range(4):
                    if n:
                        pe.wait_ge((kept_a, kept_v)[p % 2], 2 * (n - 1) + p // 2 + 1)
                    for j in range(4):
                        last = pe.transpose(k.psum[p][:, j * PAGE:(j + 1) * PAGE], kp[n % KV_RING][:, j, p * P:(p + 1) * P], k.c["ident"])
                    last.then_inc(k_turned, 1)

            def mask_rows(it, b2):
                at = it * P + b2 * 64
                return k.b["sel_at"][0:NS, at:at + 64]

            def product(n):
                it, c, b2 = loads[n]
                i = it * (NCH + 1) + c
                bank = k.psum[4 + i % 2]
                pe.wait_ge(kept_a, 2 * (n + 1))
                pe.wait_ge(kept_v, 2 * (n + 1))
                if b2 == 0 and i >= 2:
                    pe.wait_ge(copied, i - 1)
                rows = bank[b2 * 64:(b2 + 1) * 64, :]
                pe.matmul(rows, mask_rows(it, b2), k.maskS[0:NS, c * 512:(c + 1) * 512], start=True, stop=False)
                for p in range(4):
                    last = pe.matmul(rows, qblk[:, (2 * it + b2) * 4 + p, :], kts[n % 2][:, p, :], start=False, stop=(p == 3))
                last.then_inc(qk, 1)

            def new_keys(it):
                i = it * (NCH + 1) + NCH
                bank = k.psum[4 + i % 2]
                if i >= 2:
                    pe.wait_ge(copied, i - 1)
                for b2 in range(2):
                    rows = bank[b2 * 64:(b2 + 1) * 64, 0:NS]
                    pe.matmul(rows, mask_rows(it, b2), k.maskS[0:NS, PAST:LS], start=True, stop=False)
                    for p in range(4):
                        last = pe.matmul(rows, qblk[:, (2 * it + b2) * 4 + p, :], ktn[:, p, :], start=False, stop=(p == 3))
                last.then_inc(scores, 1)

            def turn_weights(it, g):
                n = it * PG + g
                if g == 0:
                    pe.wait_ge(exped, it + 1)
                    if it:
                        pe.wait_ge(laid, 8 * it)
                if n:
                    pe.wait_ge(p_kept, n)
                for j in range(4 * g, min(4 * g + 4, NPG + 1)):
                    w = PAGE if j < NPG else NS
                    last = pe.transpose(k.psum[7][0:w, (j % 4) * P:(j % 4 + 1) * P], S[it % 2][:, j * P:j * P + w], k.c["ident"])
                last.then_inc(p_turned, 1)

            def values(it, u):
                c, b2 = u // 2, u % 2
                n = it * U + u
                if u == 0 and it:
                    pe.wait_ge(out_kept, it)
                pe.wait_ge(vl[n % KV_RING], 64 * (n // KV_RING + 1))
                pe.wait_ge(p_kept, it * PG + c + 1)
                for j in range(4):
                    last = pe.matmul(k.psum[6][b2 * 64:(b2 + 1) * 64, :], PT[:, 4 * c + j, b2 * 64:(b2 + 1) * 64], vp[n % KV_RING][:, j, :],
                                     start=(c == 0 and j == 0), stop=False)
                last.then_inc(v_used, 1)

            def turn_output(it):
                pe.wait_ge(p_kept, PG * (it + 1))
                pe.wait_ge(out_kept, it + 1)
                for p in range(4):
                    last = pe.transpose(k.psum[7][:, p * P:(p + 1) * P], osb[:, p * P:(p + 1) * P], k.c["ident"])
                last.then_inc(o_turned, 1)

            def values_step(it, u):
                if u == 0 and it:
                    turn_output(it - 1)
                if u >= 2:
                    values(it, u - 2)
                if u % 2:
                    turn_weights(it, u // 2)
                if u == U - 1:
                    values(it, U - 2)
                    values(it, U - 1)
                    turn_weights(it, NCH)
                    pe.wait_ge(p_kept, PG * (it + 1))
                    for b2 in range(2):
                        last = pe.matmul(k.psum[6][b2 * 64:(b2 + 1) * 64, :], PT[0:NS, NPG, b2 * 64:(b2 + 1) * 64], k.psA[0:NS, 2 * AW:3 * AW],
                                         start=False, stop=True)
                    last.then_inc(out, 1)

            turn(0)
            for n in range(len(loads)):
                it, u = n // U, n % U
                if n + 1 < len(loads):
                    turn(n + 1)
                product(n)
                if u == U - 1:
                    new_keys(it)
                if it:
                    values_step(it - 1, u)
            for u in range(U):
                values_step(IT - 1, u)
            turn_output(IT - 1)

        def keep_keys(eng, copy, mine, sem, n):
            for p in mine:
                eng.wait_ge(k_turned, 4 * n + p + 1)
                if n >= 2:
                    eng.wait_ge(qk, n - 1)
                copy(kts[n % 2][:, p, :], k.psum[p][:, :]).then_inc(sem, 1)

        @block.scalar
        def _(act):
            def scores_out(it, c):
                i = it * (NCH + 1) + c
                if c < NCH:
                    act.wait_ge(qk, it * 2 * NCH + 2 * c + 2)
                else:
                    act.wait_ge(scores, it + 1)
                if it >= 2 and c == 0:
                    act.wait_ge(p_turned, PG * (it - 1))
                w = 512 if c < NCH else NS
                act.copy(S[it % 2][:, c * 512:c * 512 + w], k.psum[4 + i % 2][:, 0:w]).then_inc(copied, 1)

            keep_keys(act, act.copy, (0, 2), kept_a, 0)
            for n in range(len(loads)):
                it, u = n // U, n % U
                if n + 1 < len(loads):
                    keep_keys(act, act.copy, (0, 2), kept_a, n + 1)
                if u % 2:
                    scores_out(it, u // 2)
                if u == U - 1:
                    scores_out(it, NCH)
                    act.wait_ge(maxed, it + 1)
                    act.activation(S[it % 2], S[it % 2], ACT.Exp, bias=stat[:, 0, it:it + 1], accum_out=stat[:, 1, it:it + 1]).then_inc(exped, 1)

        @block.vector
        def _(dve):
            dve.wait_ge(prep_pe, 1)
            dve.wait_ge(zero, 1)
            for h in range(H):
                lo, p = (h % 2) * HD, h // 2
                dst = qblk.rearrange("d (b p) n -> d b p n", p=4)[lo:lo + HD, :, p, h * DS:(h + 1) * DS]
                dve.tensor_scalar(dst, k.psum[6][lo:lo + HD, p * NS:(p + 1) * NS].rearrange("d (b q) -> d b q", b=DB),
                                  HD ** -0.5, None, ALU.mult).then_inc(prep, 1)
            dve.tensor_copy(ktn.rearrange("p a n -> p (a n)"), k.psum[7][:, 0:4 * NS]).then_inc(prep, 1)

            def keep_weights(it, g):
                dve.wait_ge(p_turned, it * PG + g + 1)
                if g == 0 and it:
                    dve.wait_ge(out, it)
                if g < NCH:
                    dve.tensor_copy(PT[:, 4 * g:4 * g + 4, :].rearrange("p a n -> p (a n)"), k.psum[7][:, :]).then_inc(p_kept, 1)
                else:
                    dve.tensor_copy(PT[0:NS, NPG, :], k.psum[7][0:NS, 0:P]).then_inc(p_kept, 1)

            def lay_output(it):
                dve.wait_ge(o_turned, it + 1)
                for h in range(H):
                    lo, p = (h % 2) * HD, h // 2
                    src = k.psum[7][lo:lo + HD, p * P:(p + 1) * P].rearrange("d (b n) -> d b n", b=2)[:, :, h * DS:(h + 1) * DS]
                    dst = mix[lo:lo + HD, p, SEQ + it * 2 * DS:SEQ + (it + 1) * 2 * DS].rearrange("d (b q) -> d b q", b=2)
                    dve.tensor_copy(dst, src).then_inc(laid, 1)

            def values_step(it, u):
                if u == 0:
                    dve.wait_ge(exped, it + 1)
                    dve.reciprocal(stat[:, 2, it:it + 1], stat[:, 1, it:it + 1]).then_inc(inverted, 1)
                    if it:
                        lay_output(it - 1)
                if u % 2:
                    keep_weights(it, u // 2)
                if u == U - 1:
                    keep_weights(it, NCH)
                    dve.wait_ge(out, it + 1)
                    dve.wait_ge(inverted, it + 1)
                    if it:
                        dve.wait_ge(o_turned, it)
                    dve.tensor_scalar(osb, k.psum[6][:, :], stat[:, 2, it:it + 1], None, ALU.mult).then_inc(out_kept, 1)

            keep_keys(dve, dve.tensor_copy, (1, 3), kept_v, 0)
            for n in range(len(loads)):
                it, u = n // U, n % U
                if n + 1 < len(loads):
                    keep_keys(dve, dve.tensor_copy, (1, 3), kept_v, n + 1)
                if it:
                    values_step(it - 1, u)
                if u == U - 1:
                    dve.wait_ge(copied, PG * (it + 1))
                    dve.tensor_reduce(stat[:, 0, it:it + 1], S[it % 2], AX_X, ALU.max, negate=True).then_inc(maxed, 1)
            for u in range(U):
                values_step(IT - 1, u)
            lay_output(IT - 1)


def split_product(pe, out, left, right, start, stop):
    (lh, ll), (rh, rl) = left, right
    pe.matmul(out, lh, rh, start=start, stop=False)
    pe.matmul(out, lh, rl, start=False, stop=False)
    return pe.matmul(out, ll, rh, start=False, stop=stop)


def stage_output_projection(k):
    nc, a = k.nc, k.a
    GT = 3
    NG = (NT + 1) // GT
    NP = 2 * GT
    RING = 3
    mix = k.view(k.hT_at, KD, TOK)
    m = Map(k.hT_at + D)
    xn = [k.view(m.take(D), D) for _ in range(2)]
    junk = k.view(m.take(D), D)
    tmp = [k.view(m.take(512), 4, P) for _ in range(2)]
    stat = k.view(m.take(3 * (NT + 1)), 3, NT + 1)
    w_sem = k.sems("op_w_landed", RING)
    x_landed = k.sem("op_x_landed")
    names = ("mix_rounded", "mix_rest", "w_rounded", "w_rest", "made", "w_used", "added",
             "squared", "rooted", "rstd", "normed", "turned", "kept", "rounded", "rest")
    (mix_hi, mix_lo, w_hi, w_lo, made, used, added,
     squared, rooted, scaled, normed, turned, kept, rounded, rest) = (k.sem("op_" + n) for n in names)
    xp = a["x_prompt"][0].rearrange("(t p) d -> p t d", p=P)
    xs = a["x_sample"].rearrange("b t d -> (b t) d")
    wv = a["w_out"][0].rearrange("(k p) n -> p k n", p=P)
    steps = [(g, f) for g in range(NG) for f in range(KD)]
    scale_at, turn_at, keep_at = {0: 0, 1: 1, 3: 2}, {1: 0, 3: 1, 5: 2}, {2: 0, 4: 1, 6: 2}

    def wait_used(eng, n):
        g, f = steps[n]
        if f == KD - 1:
            eng.wait_ge(made, NP * (g + 1))
        else:
            eng.wait_ge(used, (KD - 1) * g + f + 1)

    with (nc.sbuf_tensor("op_raw", [P, RING, D], F32) as raw, nc.sbuf_tensor("op_w_hi", [P, RING, D], F32R) as whi,
          nc.sbuf_tensor("op_w_lo", [P, RING, D], F32R) as wlo, nc.Block() as block):
        @block.sync
        def _(sp):
            for n, (g, f) in enumerate(steps):
                if n >= RING:
                    sp.wait_ge(w_lo, n - RING + 1)
                sp.dma_start(raw[:, n % RING, :], wv[:, f, :]).then_inc(w_sem[n % RING], 16)
                if n == RING - 1:
                    sp.dma_start(k.x2_prompt[:, :, :], xp).then_inc(x_landed, 16)
                if n == KD + RING:
                    sp.wait_ge(mix_lo, KD)
                    sp.dma_start(k.x2[NT][0:NS, :], xs).then_inc(x_landed, 16)

        @block.tensor
        def _(pe):
            def turn(t):
                r = rows_of(t)
                pe.wait_ge(normed, t + 1)
                if t:
                    pe.wait_ge(kept, 2 * t)
                for f in range(KD):
                    last = pe.transpose(k.psum[NP + f // 4][:, (f % 4) * P:(f % 4) * P + r], xn[t % 2][0:r, f * P:(f + 1) * P],
                                        k.c["ident"][0:r, 0:r])
                last.then_inc(turned, 1)

            for g in range(NG + 1):
                for f in range(KD):
                    if g < NG:
                        pe.wait_ge(w_lo, g * KD + f + 1)
                        if g == 0:
                            pe.wait_ge(mix_lo, f + 1)
                        for j in range(NP):
                            t, i = GT * g + j // 2, j % 2
                            if g and f == 0:
                                pe.wait_ge(added, NP * (g - 1) + j + 1)
                            cols = slice(t * P, t * P + rows_of(t))
                            left = k.h_hi[:, f, cols], k.h_lo[:, f, cols]
                            right = whi[:, (g * KD + f) % RING, i * 512:(i + 1) * 512], wlo[:, (g * KD + f) % RING, i * 512:(i + 1) * 512]
                            last = split_product(pe, k.psum[j][0:rows_of(t), :], left, right, f == 0, f == KD - 1)
                            if f == KD - 1:
                                last.then_inc(made, 1)
                        if f < KD - 1:
                            last.then_inc(used, 1)
                    if g and f in turn_at:
                        turn(GT * (g - 1) + turn_at[f])

        @block.scalar
        def _(act):
            def round_rows(n):
                if n >= RING:
                    wait_used(act, n - RING)
                act.wait_ge(w_sem[n % RING], 16 * (n // RING + 1))
                act.copy(whi[:, n % RING, :], raw[:, n % RING, :]).then_inc(w_hi, 1)

            def round_mix(f):
                act.copy(k.h_hi[:, f, :], mix[:, f, :]).then_inc(mix_hi, 1)

            def length(t):
                r = rows_of(t)
                act.wait_ge(added, 2 * (t + 1))
                if t:
                    act.wait_ge(squared, t)
                act.activation(junk[0:r, :], k.x2[t][0:r, :], ACT.Square, accum_out=stat[0:r, 0, t:t + 1]).then_inc(squared, 1)
                act.wait_ge(squared, t + 1)
                act.activation(stat[0:r, 1, t:t + 1], stat[0:r, 0, t:t + 1], ACT.Sqrt, scale=1.0 / D, bias=k.eps[0:r, :]).then_inc(rooted, 1)

            for n in range(RING - 1):
                round_mix(n)
                round_rows(n)
            for g in range(NG + 1):
                for f in range(KD):
                    n = g * KD + f + RING - 1
                    if n < KD:
                        round_mix(n)
                    if n < len(steps):
                        round_rows(n)
                    if g and f in scale_at:
                        length(GT * (g - 1) + scale_at[f])
                    if g and f in keep_at:
                        t = GT * (g - 1) + keep_at[f]
                        r = rows_of(t)
                        for half in range(2):
                            act.wait_ge(kept, 2 * t + half + 1)
                            act.copy(k.h_hi[:, 4 * half:4 * half + 4, t * P:t * P + r], tmp[half][:, :, 0:r]).then_inc(rounded, 1)

        @block.vector
        def _(dve):
            def rest_of_rows(n):
                dve.wait_ge(w_hi, n + 1)
                dve.tensor_tensor(wlo[:, n % RING, :], raw[:, n % RING, :], whi[:, n % RING, :], ALU.subtract).then_inc(w_lo, 1)

            def rest_of_mix(f):
                dve.wait_ge(mix_hi, f + 1)
                dve.tensor_tensor(k.h_lo[:, f, :], mix[:, f, :], k.h_hi[:, f, :], ALU.subtract).then_inc(mix_lo, 1)

            def scale(t):
                r = rows_of(t)
                dve.wait_ge(rooted, t + 1)
                dve.reciprocal(stat[0:r, 2, t:t + 1], stat[0:r, 1, t:t + 1]).then_inc(scaled, 1)
                if t >= 2:
                    dve.wait_ge(turned, t - 1)
                dve.wait_ge(scaled, t + 1)
                dve.tensor_scalar(xn[t % 2][0:r, :], k.x2[t][0:r, :], stat[0:r, 2, t:t + 1], None, ALU.mult).then_inc(normed, 1)

            def keep(t):
                r = rows_of(t)
                dve.wait_ge(turned, t + 1)
                if t:
                    dve.wait_ge(rest, 2 * t)
                for half in range(2):
                    part = slice(4 * half, 4 * half + 4)
                    src = k.psum[NP + half][:, :].rearrange("p (f n) -> p f n", f=4)[:, :, 0:r]
                    g = k.g_mlp[:, part].unsqueeze(2).to_broadcast([P, 4, r])
                    dve.tensor_tensor(tmp[half][:, :, 0:r], src, g, ALU.mult).then_inc(kept, 1)
                for half in range(2):
                    part, cols = slice(4 * half, 4 * half + 4), slice(t * P, t * P + r)
                    dve.wait_ge(rounded, 2 * t + half + 1)
                    dve.tensor_tensor(k.h_lo[:, part, cols], tmp[half][:, :, 0:r], k.h_hi[:, part, cols], ALU.subtract).then_inc(rest, 1)

            for n in range(RING - 1):
                rest_of_mix(n)
                rest_of_rows(n)
            for g in range(NG + 1):
                for f in range(KD):
                    if g in (1, NG) and f == 0:
                        dve.wait_ge(x_landed, 16 if g == 1 else 32)
                    for j in range(NP if g and f == 0 else 0):
                        t, i = GT * (g - 1) + j // 2, j % 2
                        r = rows_of(t)
                        part = k.x2[t][0:r, i * 512:(i + 1) * 512]
                        dve.wait_ge(made, NP * (g - 1) + j + 1)
                        dve.tensor_tensor(part, part, k.psum[j][0:r, :], ALU.add).then_inc(added, 1)
                    n = g * KD + f + RING - 1
                    if n < KD:
                        rest_of_mix(n)
                    if n < len(steps):
                        rest_of_rows(n)
                    if g and f in scale_at:
                        scale(GT * (g - 1) + scale_at[f])
                    if g and f in keep_at:
                        keep(GT * (g - 1) + keep_at[f])


def stage_mlp(k):
    nc, a = k.nc, k.a
    F = FF // P
    ND = 2 * (NT + 1)
    x2 = k.x2
    up_sem, down_sem = k.sems("ml_up_landed", 2), k.sems("ml_down_landed", 2)
    names = ("up_rounded", "up_rest", "down_rounded", "down_rest", "up", "relu", "square", "hid_rounded", "hid_rest", "down", "added")
    up_hi, up_lo, down_hi, down_lo, upped, relued, squared, hid_hi, hid_lo, downed, added = (k.sem("ml_" + n) for n in names)
    wu = a["w_up"][0].rearrange("(k p) n -> p k n", p=P)
    wd = a["w_down"][0].rearrange("(k p) n -> p k n", p=P)
    steps = [("up", 0), ("up", 1)]
    for g in range(F // 2):
        steps += [("up", 2 * g + 2)] * (2 * g + 2 < F) + [("down", g)] + [("up", 2 * g + 3)] * (2 * g + 3 < F)
    gain_landed, summed, rooted, inv, done = (k.sem("fn_" + n) for n in ("gain_landed", "summed", "rooted", "inv", "done"))
    yp = a["y_prompt"][0].rearrange("(t p) d -> t p d", p=P)
    ys = a["y_sample"].rearrange("b t d -> (b t) d")
    W = -(-TOK // 3 // 4) * 4
    pieces = [(at, min(W, TOK - at)) for at in range(0, TOK, W)]
    with ExitStack() as ctx:
        sbuf = lambda name, dims: ctx.enter_context(nc.sbuf_tensor("ml_" + name, [P, *dims], F32R))
        m = Map(k.hT_at + D)
        raw_up = k.view(m.take(2 * KD * P), 2, KD, P)
        raw_down, tmp = k.view(m.take(2 * D), 2, D), k.view(m.take(3 * 512), 3, 512)
        stat = k.view(m.take(3 * (NT + 1)), 3, NT + 1)
        gain = k.view(m.take(D), D)
        assert m.at <= LASTING
        uhi, ulo = sbuf("up_hi", [2, KD, P]), sbuf("up_lo", [2, KD, P])
        dhi, dlo = sbuf("down_hi", [2, D]), sbuf("down_lo", [2, D])
        hhi, hlo = sbuf("hid_hi", [3, TOK]), sbuf("hid_lo", [3, TOK])
        block = ctx.enter_context(nc.Block())

        @block.sync
        def _(sp):
            def load_up(f):
                sp.dma_start(raw_up[:, f % 2], wu[:, :, f * P:(f + 1) * P]).then_inc(up_sem[f % 2], 16)

            def load_down(n):
                if n >= 2:
                    sp.wait_ge(down_lo, n - 1)
                sp.dma_start(raw_down[:, n % 2], wd[:, n, :]).then_inc(down_sem[n % 2], 16)

            for f in range(2):
                load_up(f)
            for n in range(2):
                load_down(n)
            sp.dma_start(gain, a["norm_final"].rearrange("(a n) -> a n", a=1).partition_broadcast(P).rearrange("p a n -> p (a n)")).then_inc(gain_landed, 16)
            for kind, f in steps:
                if kind == "down":
                    continue
                if f + 2 < F:
                    sp.wait_ge(upped, 3 * (f + 1))
                    load_up(f + 2)
                if f % 2 == 0 and f:
                    for n in (f, f + 1):
                        if n < F:
                            load_down(n)
            for t in range(NT + 1):
                sp.wait_ge(done, t + 1)
                sp.dma_start(yp[t] if t < NT else ys, x2[t][0:rows_of(t), :]).then_inc(k.stored["y"], 16)
            sp.wait_ge(k.stored["y"], 16 * (NT + 1))

        @block.tensor
        def _(pe):
            for kind, f in steps:
                if kind == "up":
                    pe.wait_ge(up_lo, f + 1)
                    for j, (at, w) in enumerate(pieces):
                        n = 3 * f + j
                        if n >= 4:
                            pe.wait_ge(relued, n - 3)
                        bank = k.psum[n % 4]
                        for c in range(KD):
                            last = split_product(pe, bank[:, 0:w], (uhi[:, f % 2, c, :], ulo[:, f % 2, c, :]),
                                                 (k.h_hi[:, c, at:at + w], k.h_lo[:, c, at:at + w]), c == 0, c == KD - 1)
                        last.then_inc(upped, 1)
                    continue
                pe.wait_ge(hid_lo, 6 * (f + 1))
                pe.wait_ge(down_lo, 2 * (f + 1))
                for t in range(NT + 1):
                    r = rows_of(t)
                    for i in range(2):
                        n = ND * f + 2 * t + i
                        if n >= 4:
                            pe.wait_ge(added, n - 3)
                        for e in (2 * f, 2 * f + 1):
                            cols, half = slice(t * P, t * P + r), slice(i * 512, (i + 1) * 512)
                            last = split_product(pe, k.psum[4 + n % 4][0:r, :], (hhi[:, e % 3, cols], hlo[:, e % 3, cols]),
                                                 (dhi[:, e % 2, half], dlo[:, e % 2, half]), e == 2 * f, e == 2 * f + 1)
                        last.then_inc(downed, 1)

        @block.scalar
        def _(act):
            def round_up(f):
                act.wait_ge(up_sem[f % 2], 16 * (f // 2 + 1))
                if f >= 2:
                    act.wait_ge(upped, 3 * (f - 1))
                act.copy(uhi[:, f % 2], raw_up[:, f % 2]).then_inc(up_hi, 1)

            def round_down(n):
                act.wait_ge(down_sem[n % 2], 16 * (n // 2 + 1))
                if n >= 2:
                    act.wait_ge(downed, ND * (n // 2))
                act.copy(dhi[:, n % 2, :], raw_down[:, n % 2, :]).then_inc(down_hi, 1)

            for f in range(2):
                round_up(f)
            for n in range(2):
                round_down(n)
            for kind, f in steps:
                if kind == "down":
                    for n in (2 * f + 2, 2 * f + 3):
                        if n < F:
                            round_down(n)
                    continue
                for j, (at, w) in enumerate(pieces):
                    n = 3 * f + j
                    act.wait_ge(upped, n + 1)
                    if f:
                        act.wait_ge(hid_lo, n - 2)
                    act.activation(tmp[:, j, 0:w], k.psum[n % 4][:, 0:w], ACT.Relu).then_inc(relued, 1)
                if f >= 3:
                    act.wait_ge(downed, ND * ((f - 3) // 2 + 1))
                for j, (at, w) in enumerate(pieces):
                    act.wait_ge(squared, 3 * f + j + 1)
                    act.copy(hhi[:, f % 3, at:at + w], tmp[:, j, 0:w]).then_inc(hid_hi, 1)
                if f + 2 < F:
                    round_up(f + 2)
            for t in range(NT + 1):
                r = rows_of(t)
                act.wait_ge(added, ND * (F // 2 - 1) + 2 * t + 2)
                if t:
                    act.wait_ge(summed, t)
                act.activation(k.banks[0:r, 0:D], x2[t][0:r, :], ACT.Square,
                               accum_out=stat[0:r, 0, t:t + 1]).then_inc(summed, 1)
                act.wait_ge(summed, t + 1)
                act.activation(stat[0:r, 1, t:t + 1], stat[0:r, 0, t:t + 1], ACT.Sqrt, scale=1.0 / D, bias=k.eps[0:r, :]).then_inc(rooted, 1)

        @block.vector
        def _(dve):
            def rest_up(f):
                dve.wait_ge(up_hi, f + 1)
                dve.tensor_tensor(ulo[:, f % 2], raw_up[:, f % 2], uhi[:, f % 2], ALU.subtract).then_inc(up_lo, 1)

            def rest_down(n):
                dve.wait_ge(down_hi, n + 1)
                dve.tensor_tensor(dlo[:, n % 2, :], raw_down[:, n % 2, :], dhi[:, n % 2, :], ALU.subtract).then_inc(down_lo, 1)

            def final(t):
                r = rows_of(t)
                if t == 0:
                    dve.wait_ge(gain_landed, 16)
                dve.wait_ge(rooted, t + 1)
                dve.reciprocal(stat[0:r, 2, t:t + 1], stat[0:r, 1, t:t + 1]).then_inc(inv, 1)
                dve.wait_ge(inv, t + 1)
                dve.scalar_tensor_tensor(out=x2[t][0:r, :], in0=x2[t][0:r, :], scalar=stat[0:r, 2, t:t + 1], in1=gain[0:r, :],
                                         op0=ALU.mult, op1=ALU.mult).then_inc(done, 1)

            for f in range(2):
                rest_up(f)
            for n in range(2):
                rest_down(n)
            for kind, f in steps:
                if kind == "down":
                    for n in range(ND * f, ND * (f + 1)):
                        t, i = n % ND // 2, n % 2
                        r = rows_of(t)
                        part = x2[t][0:r, i * 512:(i + 1) * 512]
                        dve.wait_ge(downed, n + 1)
                        if f:
                            dve.wait_ge(added, n - ND + 1)
                        dve.tensor_tensor(part, part, k.psum[4 + n % 4][0:r, :], ALU.add).then_inc(added, 1)
                        if f == F // 2 - 1 and i and t:
                            final(t - 1)
                    for n in (2 * f + 2, 2 * f + 3):
                        if n < F:
                            rest_down(n)
                    continue
                for j, (at, w) in enumerate(pieces):
                    n = 3 * f + j
                    dve.wait_ge(relued, n + 1)
                    dve.tensor_tensor(tmp[:, j, 0:w], tmp[:, j, 0:w], tmp[:, j, 0:w], ALU.mult).then_inc(squared, 1)
                for j, (at, w) in enumerate(pieces):
                    dve.wait_ge(hid_hi, 3 * f + j + 1)
                    dve.tensor_tensor(hlo[:, f % 3, at:at + w], tmp[:, j, 0:w], hhi[:, f % 3, at:at + w], ALU.subtract).then_inc(hid_lo, 1)
                if f + 2 < F:
                    rest_up(f + 2)
            final(NT)


_INS = ["x_prompt", "x_sample", "cache_k", "cache_v", "cache_kidx", "state_ssm", "state_conv", "page_table",
        "norm_mix", "w_in", "conv_w", "a_log", "dt_bias", "norm_gdn_out", "w_out", "norm_mlp", "w_up",
        "w_down", "norm_final"]
_OUTS = [("y_prompt", (1, SEQ, D)), ("y_sample", (DB, DS, D)),
         ("new_k_prompt", (1, 1, SEQ, H, HD)), ("new_v_prompt", (1, 1, SEQ, H, HD)), ("new_kidx_prompt", (1, 1, SEQ, DI)),
         ("new_ssm_prompt", (1, 1, G, DK, DK)), ("new_conv_prompt", (1, 1, CW - 1, CC)),
         ("new_k_sample", (1, DB, DS, H, HD)), ("new_v_sample", (1, DB, DS, H, HD)), ("new_kidx_sample", (1, DB, DS, DI)),
         ("new_ssm_sample", (1, DB, G, DK, DK)), ("new_conv_sample", (1, DB, CW - 1, CC))]


def build_program(nc, a):
    with ExitStack() as ctx:
        a["q_T"] = nc.dram_tensor("q_T", (AW, SEQ), F32, kind="Internal").ap()
        a["k_T"] = nc.dram_tensor("k_T", (AW, SEQ), F32, kind="Internal").ap()
        k = Kernel(nc, ctx, a)

        stages(k)


def stages(k):
    a = k.a
    stage_constants(k)
    x_ring = [k.view(k.xc_at + (t % 3) * D, D) for t in range(NT + 1)]
    xp = a["x_prompt"][0].rearrange("(t p) d -> t p d", p=P)
    xs = a["x_sample"].rearrange("b t d -> (b t) d")
    k.ix_landed, k.kidx_landed = k.sems("ixw_landed", 2), k.sems("kidx_landed", DB)
    stage_norm(k, x_ring, lambda t: xp[t] if t < NT else xs)
    stage_indexer_projection(k)
    stage_prompt_scores(k)
    stage_sample_scores(k)
    stage_mixer_projection(k)
    stage_conv(k)
    stage_l2norm(k, stage_gates(k))
    k.stage_done()
    stage_chunks(k)
    stage_scan(k)
    stage_prompt_attention(k)
    stage_sample_attention(k)
    k.begin_dense_part()
    stage_output_projection(k)
    stage_mlp(k)


def kernel(**inputs):
    import concourse.bacc as bacc
    from concourse.bass_utils import run_bass_kernel_spmd

    nc = bacc.Bacc("TRN2", target_bir_lowering=False, num_devices=1)
    arrays, a = {}, {}
    for name in _INS:
        arrays["in_" + name] = np.ascontiguousarray(inputs[name])
    arrays["in_const"] = CONST
    for name, x in arrays.items():
        a[name[3:]] = nc.dram_tensor(name, x.shape, mybir.dt.from_np(x.dtype), kind="ExternalInput").ap()
    for name, shape in _OUTS:
        a[name] = nc.dram_tensor("out_" + name, shape, F32, kind="ExternalOutput").ap()
    build_program(nc, a)
    r = run_bass_kernel_spmd(nc, [arrays], core_ids=[0])
    return tuple(r.results[0]["out_" + name] for name, _ in _OUTS)
```
